# Optimizing a Trainium2 kernel written in Bass

```python
import math
import jax, jax.numpy as jnp
from jax import lax
import numpy as np

D_MODEL = 2048
BATCH = 1
SEQ = 256
DEPTH = 2

S5_WIDTH = D_MODEL // 2
S5_GROUP = 16
S5_GROUPS = S5_WIDTH // S5_GROUP
S5_STATE = 64
DA_HEADS = 8
DA_HEAD_DIM = 64
DA_V_DIM = 2 * DA_HEAD_DIM
DA_WIDTH = DA_HEADS * DA_V_DIM
E_IN = 2 * S5_WIDTH + 4 * DA_WIDTH
E_OUT = S5_WIDTH + DA_WIDTH
FOX_HEADS = 16
FOX_HEAD_DIM = D_MODEL // FOX_HEADS
FOX_WIDTH = FOX_HEADS * FOX_HEAD_DIM
O_IN = 4 * FOX_WIDTH + FOX_HEADS
Q_BLOCK = 128
N_EVEN = (DEPTH + 1) // 2
N_ODD = DEPTH // 2
EPS = 1e-6

kernel_name = "hybrid_s5_diffattn_fox_block"

def _rms(x, g):
    xf = x.astype(jnp.float32)
    r = lax.rsqrt(jnp.mean(xf * xf, axis=-1, keepdims=True) + EPS)
    return (xf * r * g.astype(jnp.float32)).astype(x.dtype)

def _alibi_slopes(n):
    return np.array([2.0 ** (-8.0 * (h + 1) / n) for h in range(n)], dtype=np.float32)

def _block_sweep(block_fn, seq):
    nb = seq // Q_BLOCK
    out = lax.map(block_fn, jnp.arange(nb))
    nbk, bsz, h, qb, dv = out.shape
    return out.transpose(1, 0, 3, 2, 4).reshape(bsz, seq, h * dv)

def _complex_linear_combine(e1, e2):
    a1r, a1i, b1r, b1i = e1
    a2r, a2i, b2r, b2i = e2
    ar = a1r * a2r - a1i * a2i
    ai = a1r * a2i + a1i * a2r
    br = a2r * b1r - a2i * b1i + b2r
    bi = a2r * b1i + a2i * b1r + b2i
    return (ar, ai, br, bi)

def _s5_mixer(u, lam_re, lam_im, log_dt, b_re, b_im, c_re, c_im, d, w_glu, b_glu):
    bsz, seq, _ = u.shape
    f32 = jnp.float32
    uf = u.astype(f32).reshape(bsz, seq, S5_GROUPS, S5_GROUP)
    dt = jnp.exp(log_dt.astype(f32))[:, None]
    lr = lam_re.astype(f32)
    li = lam_im.astype(f32)
    mag = jnp.exp(lr * dt)
    ar = mag * jnp.cos(li * dt)
    ai = mag * jnp.sin(li * dt)
    den = lr * lr + li * li
    nr = ar - 1.0
    ni = ai
    kr = (nr * lr + ni * li) / den
    ki = (ni * lr - nr * li) / den
    br = b_re.astype(f32)
    bi = b_im.astype(f32)
    bbr = kr[..., None] * br - ki[..., None] * bi
    bbi = kr[..., None] * bi + ki[..., None] * br
    xr = jnp.einsum('blgh,gph->blgp', uf, bbr)
    xi = jnp.einsum('blgh,gph->blgp', uf, bbi)
    a_r = jnp.broadcast_to(ar, (1, seq, S5_GROUPS, S5_STATE))
    a_i = jnp.broadcast_to(ai, (1, seq, S5_GROUPS, S5_STATE))
    _, _, hr, hi = lax.associative_scan(_complex_linear_combine, (a_r, a_i, xr, xi), axis=1)
    y = (jnp.einsum('blgp,ghp->blgh', hr, c_re.astype(f32))
         - jnp.einsum('blgp,ghp->blgh', hi, c_im.astype(f32)))
    y = y.reshape(bsz, seq, S5_WIDTH) + d.astype(f32) * u.astype(f32)
    y = jax.nn.gelu(y)
    y = y * jax.nn.sigmoid(y @ w_glu.astype(f32) + b_glu.astype(f32))
    return y.astype(u.dtype)

def _diff_attention(q, k, v, q_gain, k_gain, lq1, lk1, lq2, lk2, out_gain, lambda_init):
    bsz, seq = q.shape[:2]
    q = _rms(q.reshape(bsz, seq, DA_HEADS, 2, DA_HEAD_DIM), q_gain.reshape(2, DA_HEAD_DIM))
    k = _rms(k.reshape(bsz, seq, DA_HEADS, 2, DA_HEAD_DIM), k_gain.reshape(2, DA_HEAD_DIM))
    q = q.transpose(0, 2, 3, 1, 4)
    k = k.transpose(0, 2, 3, 1, 4)
    v = v.reshape(bsz, seq, DA_HEADS, DA_V_DIM).transpose(0, 2, 1, 3)
    f32 = jnp.float32
    lam = (jnp.exp(jnp.sum(lq1.astype(f32) * lk1.astype(f32)))
           - jnp.exp(jnp.sum(lq2.astype(f32) * lk2.astype(f32))) + lambda_init)
    slopes = jnp.asarray(_alibi_slopes(DA_HEADS))[:, None, None, None]
    scale = DA_HEAD_DIM ** -0.5
    kpos = jnp.arange(seq)

    def blk(i):
        start = i * Q_BLOCK
        qb = lax.dynamic_slice_in_dim(q, start, Q_BLOCK, axis=3)
        s = jnp.einsum('bhcqd,bhckd->bhcqk', qb, k).astype(f32) * scale
        dist = (start + jnp.arange(Q_BLOCK))[:, None] - kpos[None, :]
        s = s - slopes * dist.astype(f32)
        s = jnp.where(dist >= 0, s, -jnp.inf)
        p = jax.nn.softmax(s, axis=-1)
        p = p[:, :, 0] - lam * p[:, :, 1]
        return jnp.einsum('bhqk,bhkd->bhqd', p.astype(v.dtype), v)

    o = _block_sweep(blk, seq).reshape(bsz, seq, DA_HEADS, DA_V_DIM)
    o = _rms(o, out_gain) * (1.0 - lambda_init)
    return o.reshape(bsz, seq, DA_WIDTH)

def _forgetting_attention(q, k, v, f_logit, b_f, q_gain, k_gain):
    bsz, seq = q.shape[:2]
    f32 = jnp.float32
    q = _rms(q.reshape(bsz, seq, FOX_HEADS, FOX_HEAD_DIM), q_gain).transpose(0, 2, 1, 3)
    k = _rms(k.reshape(bsz, seq, FOX_HEADS, FOX_HEAD_DIM), k_gain).transpose(0, 2, 1, 3)
    v = v.reshape(bsz, seq, FOX_HEADS, FOX_HEAD_DIM).transpose(0, 2, 1, 3)
    logf = jax.nn.log_sigmoid(f_logit.astype(f32) + b_f.astype(f32))
    c = jnp.cumsum(logf, axis=1).transpose(0, 2, 1)
    scale = FOX_HEAD_DIM ** -0.5
    kpos = jnp.arange(seq)

    def blk(i):
        start = i * Q_BLOCK
        qb = lax.dynamic_slice_in_dim(q, start, Q_BLOCK, axis=2)
        cq = lax.dynamic_slice_in_dim(c, start, Q_BLOCK, axis=2)
        s = jnp.einsum('bhqd,bhkd->bhqk', qb, k).astype(f32) * scale
        s = s + cq[..., :, None] - c[..., None, :]
        causal = (start + jnp.arange(Q_BLOCK))[:, None] >= kpos[None, :]
        s = jnp.where(causal, s, -jnp.inf)
        p = jax.nn.softmax(s, axis=-1)
        return jnp.einsum('bhqk,bhkd->bhqd', p.astype(v.dtype), v)

    return _block_sweep(blk, seq)

def setup_inputs(seed: int = 0) -> dict:
    key = jax.random.key(seed)
    ks = iter(jax.random.split(key, 40))
    f32 = jnp.float32

    def nrm(shape, scale):
        return jax.random.normal(next(ks), shape, f32) * scale

    ne, no, g, p, gs = N_EVEN, N_ODD, S5_GROUPS, S5_STATE, S5_GROUP
    x = nrm((BATCH, SEQ, D_MODEL), 1.0)
    e_norm = 1.0 + nrm((ne, D_MODEL), 0.02)
    e_w_in = nrm((ne, D_MODEL, E_IN), D_MODEL ** -0.5)
    e_w_out = nrm((ne, E_OUT, D_MODEL), E_OUT ** -0.5)
    n_idx = jnp.arange(p, dtype=f32)
    s5_lambda_re = -0.5 + nrm((ne, g, p), 0.01)
    s5_lambda_im = math.pi * n_idx + nrm((ne, g, p), 0.01)
    s5_log_dt = jax.random.uniform(next(ks), (ne, g), f32, math.log(1e-3), math.log(1e-1))
    s5_b_re = nrm((ne, g, p, gs), (2.0 * gs) ** -0.5)
    s5_b_im = nrm((ne, g, p, gs), (2.0 * gs) ** -0.5)
    s5_c_re = nrm((ne, g, gs, p), (2.0 * p) ** -0.5)
    s5_c_im = nrm((ne, g, gs, p), (2.0 * p) ** -0.5)
    s5_d = nrm((ne, S5_WIDTH), 1.0)
    s5_w_glu = nrm((ne, S5_WIDTH, S5_WIDTH), S5_WIDTH ** -0.5)
    s5_b_glu = nrm((ne, S5_WIDTH), 0.01)
    da_q_norm = 1.0 + nrm((ne, DA_V_DIM), 0.02)
    da_k_norm = 1.0 + nrm((ne, DA_V_DIM), 0.02)
    da_lambda_q1 = nrm((ne, DA_HEAD_DIM), 0.1)
    da_lambda_k1 = nrm((ne, DA_HEAD_DIM), 0.1)
    da_lambda_q2 = nrm((ne, DA_HEAD_DIM), 0.1)
    da_lambda_k2 = nrm((ne, DA_HEAD_DIM), 0.1)
    da_out_norm = 1.0 + nrm((ne, DA_V_DIM), 0.02)
    o_norm = 1.0 + nrm((no, D_MODEL), 0.02)
    o_w_in = nrm((no, D_MODEL, O_IN), D_MODEL ** -0.5)
    o_b_f = jax.random.uniform(next(ks), (no, FOX_HEADS), f32, 1.0, 6.0)
    o_w_out = nrm((no, FOX_WIDTH, D_MODEL), FOX_WIDTH ** -0.5)
    fox_q_norm = 1.0 + nrm((no, FOX_HEAD_DIM), 0.02)
    fox_k_norm = 1.0 + nrm((no, FOX_HEAD_DIM), 0.02)
    return {
        "x": x, "e_norm": e_norm, "e_w_in": e_w_in, "e_w_out": e_w_out,
        "s5_lambda_re": s5_lambda_re, "s5_lambda_im": s5_lambda_im, "s5_log_dt": s5_log_dt,
        "s5_b_re": s5_b_re, "s5_b_im": s5_b_im, "s5_c_re": s5_c_re, "s5_c_im": s5_c_im,
        "s5_d": s5_d, "s5_w_glu": s5_w_glu, "s5_b_glu": s5_b_glu,
        "da_q_norm": da_q_norm, "da_k_norm": da_k_norm,
        "da_lambda_q1": da_lambda_q1, "da_lambda_k1": da_lambda_k1,
        "da_lambda_q2": da_lambda_q2, "da_lambda_k2": da_lambda_k2, "da_out_norm": da_out_norm,
        "o_norm": o_norm, "o_w_in": o_w_in, "o_b_f": o_b_f, "o_w_out": o_w_out,
        "fox_q_norm": fox_q_norm, "fox_k_norm": fox_k_norm,
    }

def reference(x, e_norm, e_w_in, e_w_out, s5_lambda_re, s5_lambda_im, s5_log_dt,
              s5_b_re, s5_b_im, s5_c_re, s5_c_im, s5_d, s5_w_glu, s5_b_glu,
              da_q_norm, da_k_norm, da_lambda_q1, da_lambda_k1, da_lambda_q2, da_lambda_k2,
              da_out_norm, o_norm, o_w_in, o_b_f, o_w_out, fox_q_norm, fox_k_norm):
    e_splits = [S5_WIDTH, 2 * S5_WIDTH, 2 * S5_WIDTH + DA_WIDTH,
                2 * S5_WIDTH + 2 * DA_WIDTH, 2 * S5_WIDTH + 3 * DA_WIDTH]
    o_splits = [FOX_WIDTH, 2 * FOX_WIDTH, 3 * FOX_WIDTH, 4 * FOX_WIDTH]
    for layer in range(DEPTH):
        j = layer // 2
        if layer % 2 == 0:
            h = _rms(x, e_norm[j])
            proj = h @ e_w_in[j]
            u, z_s5, q, k, v, z_da = jnp.split(proj, e_splits, axis=-1)
            y_s5 = _s5_mixer(u, s5_lambda_re[j], s5_lambda_im[j], s5_log_dt[j],
                             s5_b_re[j], s5_b_im[j], s5_c_re[j], s5_c_im[j],
                             s5_d[j], s5_w_glu[j], s5_b_glu[j]) * jax.nn.silu(z_s5)
            lambda_init = 0.8 - 0.6 * math.exp(-0.3 * layer)
            y_da = _diff_attention(q, k, v, da_q_norm[j], da_k_norm[j],
                                   da_lambda_q1[j], da_lambda_k1[j],
                                   da_lambda_q2[j], da_lambda_k2[j],
                                   da_out_norm[j], lambda_init) * jax.nn.silu(z_da)
            x = x + jnp.concatenate([y_s5, y_da], axis=-1) @ e_w_out[j]
        else:
            h = _rms(x, o_norm[j])
            proj = h @ o_w_in[j]
            q, k, v, z, f_logit = jnp.split(proj, o_splits, axis=-1)
            y = _forgetting_attention(q, k, v, f_logit, o_b_f[j],
                                      fox_q_norm[j], fox_k_norm[j]) * jax.nn.silu(z)
            x = x + y @ o_w_out[j]
    return x


_drawn_inputs = setup_inputs


def setup_inputs(seed=0):
    import zlib

    import numpy as np

    out = dict(_drawn_inputs(seed))
    spreads = {}
    factors = {'e_norm': 4.084,
     's5_lambda_re': 64.0,
     's5_lambda_im': 55.184,
     's5_log_dt': 55.688,
     's5_b_re': 64.0,
     's5_b_im': 64.0,
     's5_c_re': 64.0,
     's5_c_im': 64.0,
     's5_b_glu': 8.0,
     'da_q_norm': 8.0,
     'da_k_norm': 8.0,
     'da_out_norm': 8.0,
     'o_norm': 8.0,
     'fox_q_norm': 8.0,
     'fox_k_norm': 8.0}
    for name, (base, spread) in spreads.items():
        noise = np.random.default_rng([zlib.crc32(name.encode()), seed]).standard_normal(out[name].shape)
        drawn = base * np.exp(spread * noise) if base else spread * noise
        out[name] = __import__('jax').numpy.asarray(drawn.astype(out[name].dtype))
    for name, factor in factors.items():
        out[name] = (out[name] * factor).astype(out[name].dtype)
    return out
```

```python
from contextlib import ExitStack
import math

import numpy as np

import concourse.bass as bass
from concourse import mybir

F32 = mybir.dt.float32
F32R = mybir.dt.float32r
I32 = mybir.dt.int32
ALU = mybir.AluOpType
ACT = mybir.ActivationFunctionType
AX = mybir.AxisListType

P = 128
T = 256
NT = T // P
D = 2048
KT = D // P
CW = 512
UK = 2
UNITS = KT // UK
RING = 4
LEAD = 3
S5W = 1024
CT = S5W // P
GP = 32
GPI = 8
DA_PAIRS = 4
FOX_PAIRS = 8
HD = 128
EPS = 1e-6
FAR = 1e30
MAGIC = 1.5 * 2.0 ** 23

TWO_PI = 2.0 * math.pi
PI_A = 6.28125
PI_B = float(np.float32(round((TWO_PI - PI_A) * 2.0 ** 17) / 2.0 ** 17))
PI_C = float(np.float32(TWO_PI - PI_A - PI_B))
SIN_SCALE = 6.283185

CH_S5 = 0
CH_DA = CH_S5 + 4
CH_GLU = CH_DA + 2 * DA_PAIRS
CH_OUT0 = CH_GLU + 1
CH_FOX = CH_OUT0 + D // CW
CH_OUT1 = CH_FOX + 2 * FOX_PAIRS
CH_END = CH_OUT1 + D // CW
FREE_DA = 2
FREE_FOX = FREE_DA + DA_PAIRS
FREE_OUT1 = FREE_FOX + FOX_PAIRS
LAMBDA_INIT = 0.8 - 0.6 * math.exp(-0.3 * 0)
DA_LINKS, FOX_LINKS, DA_POOL_LINKS, FOX_POOL_LINKS = 15, 8, 52, 2

X_SLOT = [1, 3, 5, 6, 8, 9, 11, 12]
Y_SLOT = [5, 6, 8, 9, 11, 12, 14, 15]
QKT_SLOT = [0, 1]
SC_SLOT = {0: [2, 3, 4, 5], 1: [2, 4]}
PT_SLOT = [8, 9]
PV_SLOT = [10, 11]
YT_SLOT = [13, 14]


class Count:

    def __init__(self, sem):
        self.sem, self.base, self.local, self.it, self.per = sem, 0, 0, None, 0

    def enter(self, it, per):
        self.it, self.per, self.local = it, per, 0

    def leave(self, trips):
        assert self.local == self.per, (self.local, self.per)
        self.base += self.per * trips
        self.it, self.local = None, 0

    def inc(self, ins):
        ins.then_inc(self.sem, 1)
        if self.it is None:
            self.base += 1
        else:
            self.local += 1
        return ins

    def value(self):
        return self.base if self.it is None else self.it * self.per + (self.base + self.local)


def build(nc, d, out_dram):
    ctx = ExitStack()
    with ctx:
        def sb(name, shape, dt=F32):
            return ctx.enter_context(nc.sbuf_tensor(name, shape, dt))

        def sem(name):
            return ctx.enter_context(nc.semaphore(name))

        raw = sb("raw", [P, RING, UK * CW])
        wh = sb("wh", [P, RING, UK * CW], F32R)
        wl = sb("wl", [P, RING, UK * CW], F32R)
        xh = sb("xh", [P, KT, T], F32R)
        xl = sb("xl", [P, KT, T], F32R)
        yh = sb("yh", [P, KT, T], F32R)
        yl = sb("yl", [P, KT, T], F32R)
        res = sb("res", [P, NT, D])
        uz = sb("uz", [P, KT, T])
        scr = sb("scr", [P, 12864])
        con = sb("con", [P, 2880])

        used = {"scr": 0, "con": 0}

        def carve(name, *shape, parts=P):
            buf = scr if name == "scr" else con
            n = int(np.prod(shape))
            at = used[name]
            used[name] += n
            assert used[name] <= (12864 if name == "scr" else 2880), (name, used[name])
            v = buf[0:parts, at:at + n]
            if len(shape) == 2:
                v = v.rearrange("p (a b) -> p a b", a=shape[0])
            if len(shape) == 3:
                v = v.rearrange("p (a b c) -> p a b c", a=shape[0], b=shape[1])
            return v

        ident = carve("con", P)
        ones = carve("con", P)
        upto = carve("con", P)
        dist = carve("con", 3 * P)
        mask = carve("con", 3 * P)
        steps = carve("con", T)
        rbc = carve("con", T)
        colp = carve("con", 48)
        g_da = carve("con", 2, P)
        g_dao = carve("con", P)
        g_fox = carve("con", 2, P)
        lamv = carve("con", 4, 64)
        small = carve("con", 256)
        e_col, o_col, d_col, bg_col = colp[:, 0:16], colp[:, 16:32], colp[:, 32:40], colp[:, 40:48]

        def small_at(a, n):
            return small[:, a:a + n]

        ssq = small_at(0, 2)
        r_tok = small_at(2, 2)
        expo = small_at(4, 16)
        par = small_at(20, 2)
        nlam = small_at(22, 1)
        lt = small_at(23, 4)
        slope = small_at(27, 2)
        bf = small_at(29, 16)
        ss1 = small_at(45, 8).rearrange("p (t n) -> p t n", t=2)
        nmax = small_at(53, 8)
        lsum = small_at(61, 8)
        rec = small_at(69, 8)
        sso = small_at(77, 4)
        rno = small_at(81, 4)
        ssn = small_at(85, 16)
        rnn = small_at(101, 16)
        cq = small_at(117, 4)
        cols = small_at(121, 24)
        r2_tok = small_at(145, 2)
        junk1 = small_at(160, 5)
        pint = small_at(150, 1)
        ssr = small_at(152, 2)
        half_pi = small_at(154, 1)
        magic, eps = small_at(155, 1), small_at(156, 2)

        qk = carve("scr", NT, CW)
        vz = carve("scr", NT, CW)
        sq = carve("scr", CW)
        qkt = carve("scr", 2, 2, T)
        s_sb = carve("scr", 4, 3 * P)
        p_t = carve("scr", 2, 3 * P)
        y_o = qkt.rearrange("p h b (t e) -> p h (b t) e", t=NT)[:, :, 0:NT, :]
        main0 = used["scr"]
        rot = [[carve("scr", 2, T) for _ in range(3)] for _ in range(2)]
        tab = [carve("scr", 2, T) for _ in range(2)]
        ang = [carve("scr", T) for _ in range(2)]
        ph = [carve("scr", T) for _ in range(2)]
        lb_st = carve("scr", 2, 2, P)
        cd_st = carve("scr", 2, 2, P)
        u_st = carve("scr", 2, T)
        main1 = used["scr"]
        used["scr"] = main0
        x1_st = [carve("scr", NT, CW) for _ in range(2)]
        wf = carve("scr", KT, 16)
        wfx = carve("scr", NT, 16)
        nct = carve("scr", T, parts=16)
        nck = carve("scr", 2, T, parts=16)
        c_sb = carve("scr", NT, 16)
        ls = carve("scr", NT, 16)
        lsa = carve("scr", NT, 16)
        glu_s = carve("scr", 2, T)
        used["scr"] = 0
        rows = carve("scr", P, parts=48)
        lamr_r = carve("scr", P, parts=GP)
        lami_r = carve("scr", P, parts=GP)
        ldt_r = carve("scr", 2, 64, parts=GP)
        ldt_in = carve("scr", 2, parts=GP)
        b_n = carve("scr", 2, GP, 16)
        c_n = carve("scr", 2, CT, 64)
        bt = [carve("scr", GP, 16) for _ in range(4)]
        bd = carve("scr", 2, GP, 32)
        cb = carve("scr", CT, P)
        cb2 = carve("scr", CT, P)
        prm = [carve("scr", GP) for _ in range(20)]
        iot = carve("scr", 5 * P)
        junk = uz[:, 0:CT, :].rearrange("p a t -> p (a t)")
        used["scr"] = main1
        phc = carve("scr", 3, GP)
        whf = sb("whf", [P, KT * 16], F32R)
        wlf = sb("wlf", [P, KT * 16], F32R)
        phr = sb("phr", [P, GP], F32R)

        lb = res[:, 0, :].rearrange("p (c r s) -> p c r s", c=CT, r=2)
        cd = res[:, 1, :].rearrange("p (r c s) -> p r c s", r=2, c=CT)

        bank = [ctx.enter_context(nc.psum_tensor(f"bank{i}", [P, CW], F32)) for i in range(8)]
        acc = [bank[0:2], bank[2:4]]
        trb, scb, xb, yb = bank[4], bank[5], bank[6], bank[7]

        raw_in = [sem(f"raw_in{i}") for i in range(RING)]
        hi_done = sem("hi_done")
        lo_done = sem("lo_done")
        unit_used = sem("unit_used")
        acc_free = [sem("acc_free0"), sem("acc_free1")]
        x_in, par_in, bc_in, s5_in, wf_in, res_in = (sem(n) for n in
            ("x_in", "par_in", "bc_in", "s5_in", "wf_in", "res_in"))
        out_done = sem("out_done")
        pool_const, tile_ps, tile_hi, tile_lo = (sem(n) for n in
            ("pool_const", "tile_ps", "tile_hi", "tile_lo"))
        ssq_done, r_done, diag_done, rbc_ps, rbc_done = (sem(n) for n in
            ("ssq_done", "r_done", "diag_done", "rbc_ps", "rbc_done"))
        prm_rows, prm_ps, prm_ld, prm_exp, prm_ang, prm_trig, bd_done, cb_done = (sem(n) for n in
            ("prm_rows", "prm_ps", "prm_ld", "prm_exp", "prm_ang", "prm_trig", "bd_done", "cb_done"))
        mat_ps, mat_sb, prm_done = (sem(n) for n in ("mat_ps", "mat_sb", "prm_done"))
        staged, slopes = sem("staged"), sem("slopes")
        ang_done, tab_done, x_ps, x_read, g_done, scan_done, n1_done, h_done, y_ps, y_read = (
            sem(n) for n in ("ang_done", "tab_done", "x_ps", "x_read", "g_done", "scan_done",
                             "n1_done", "h_done", "y_ps", "y_read"))
        gelu_done, s5_hi, s5_lo = sem("gelu_done"), sem("s5_hi"), sem("s5_lo")
        qk_ss, qk_ready, vz_ready = (sem(n) for n in
            ("qk_ss", "qk_ready", "vz_ready"))
        qkt_ps, qkt_sb, sc_ps, sc_max, p_exp, p_ready, pt_ps, pt_sb = (sem(n) for n in
            ("qkt_ps", "qkt_sb", "sc_ps", "sc_max", "p_exp", "p_ready", "pt_ps", "pt_sb"))
        pv_ps, pv_ssq, pv_rn, y_ready, yt_ps, yt_hi, yt_lo = (sem(n) for n in
            ("pv_ps", "pv_ssq", "pv_rn", "y_ready", "yt_ps", "yt_hi", "yt_lo"))
        fox_b, fox_cq = sem("fox_b"), sem("fox_cq")
        glu_sig, glu_y0, glu_y, glu_hi, glu_lo, silu_done = (sem(n) for n in
            ("glu_sig", "glu_y0", "glu_y", "glu_hi", "glu_lo", "silu_done"))
        x1_done, x1_kept, x1_ps, x1_hi, x1_lo, x1_ssq, r2_done, r2_sum = (sem(n) for n in
            ("x1_done", "x1_kept", "x1_ps", "x1_hi", "x1_lo", "x1_ssq", "r2_done", "r2_sum"))
        wf_hi, wf_lo, f_ps, f_z, f_abs, f_exp1, f_ln, f_ls, c_ps, c_done = (sem(n) for n in
            ("wf_hi", "wf_lo", "f_ps", "f_z", "f_abs", "f_exp1", "f_ln", "f_ls", "c_ps", "c_done"))
        dve_link, act_link, pool_link = (Count(sem(n)) for n in ("dve_link", "act_link", "pool_link"))
        lambda_done = sem("lambda_done")

        def head_no(layer, a, h):
            return 2 * a + h + (2 * DA_PAIRS if layer else 0)

        def score_no(layer, a, k):
            return (4 * DA_PAIRS + 2 * a if layer else 4 * a) + k

        def place(eng, at):
            return at if isinstance(at, int) else eng.snap(at)

        def unit_rows(w, kt0, n=UK):
            return w.rearrange("(k p) n -> p k n", p=P)[:, kt0:kt0 + n, :]

        block = ctx.enter_context(nc.Block())

        @block.sync
        def _(sp):
            def load(c, j, src):
                dst = raw[:, j % RING, :]
                if len(src.shape) == 3:
                    sp.dma_start(dst.rearrange("p (k n) -> p k n", k=src.shape[1]), src).then_inc(raw_in[j % RING], 32)
                else:
                    dst = dst.rearrange("p (k b n) -> p k b n", k=UK, b=2)
                    for k in range(UK):
                        sp.dma_start(dst[:, k, :, :], src[:, k, :, :]).then_inc(raw_in[j % RING], 16)

            def chunk(c, cols, rot_kt=0):
                for j in range(UNITS):
                    src = cols(j)
                    if isinstance(c, int):
                        if UNITS * c + j >= RING:
                            sp.wait_ge(lo_done, UNITS * c + j - RING + 1)
                    load(c, j, src)

            w_e, w_eo, w_o, w_oo, w_g = d["e_w_in"][0], d["e_w_out"][0], d["o_w_in"][0], d["o_w_out"][0], d["s5_w_glu"][0]
            for c in range(4):
                chunk(CH_S5 + c, lambda j: unit_rows(w_e, UK * j)[:, :, CW * c:CW * (c + 1)])

            def pair_cols(w, base, width, j, at):
                v = unit_rows(w, UK * j)[:, :, base:base + 2 * width]
                return v.rearrange("p k (b s) -> p k b s", b=2)[:, :, :, bass.ds(at, 2 * HD)]

            def steps_of(w, base, width, ch, trips):
                for c in (0, 1):
                    chunk(ch + c, lambda j: pair_cols(w, base + 2 * width * c, width, j, 0))
                with sp.Fori(1, trips) as i:
                    at = sp.snap(i * (2 * HD))
                    for c in (0, 1):
                        for j in range(UNITS):
                            need = sp.snap(i * (2 * UNITS) + (UNITS * (ch + c) + j - RING + 1))
                            sp.wait_ge(lo_done, need)
                            load(None, j, pair_cols(w, base + 2 * width * c, width, j, at))

            steps_of(w_e, 2 * S5W, S5W, CH_DA, DA_PAIRS)
            chunk(CH_GLU, lambda j: w_g.rearrange("(k p) n -> p k n", p=P)[:, j:j + 1, :])
            sp.wait_ge(staged, DA_PAIRS)
            sp.dma_start(res[:, :, :], d["x"][0].rearrange("(t p) n -> p t n", p=P)).then_inc(res_in, 16)
            for c in range(4):
                chunk(CH_OUT0 + c, lambda j: unit_rows(w_eo, (8 + UK * j) % KT)[:, :, CW * c:CW * (c + 1)])
            steps_of(w_o, 0, D, CH_FOX, FOX_PAIRS)
            for c in range(4):
                chunk(CH_OUT1 + c, lambda j: unit_rows(w_oo, UK * j)[:, :, CW * c:CW * (c + 1)])
            sp.wait_ge(out_done, 16 * 4)

        @block.tensor
        def _(pe):
            def unit_ready(c, j):
                pe.wait_ge(lo_done, (c * UNITS) + (j + 1))

            def rows_unit(c, j, left, kts, pair):
                lh, ll = left
                unit_ready(c, j)
                for a, kt in enumerate(kts):
                    w_hi, w_lo = wh[:, j % RING, a * CW:(a + 1) * CW], wl[:, j % RING, a * CW:(a + 1) * CW]
                    first, last = j == 0 and a == 0, j == UNITS - 1 and a == UK - 1
                    for t in range(NT):
                        o = acc[pair][t][:, :]
                        l_hi, l_lo = lh[:, kt, t * P:(t + 1) * P], ll[:, kt, t * P:(t + 1) * P]
                        nc.tensor.matmul(o, l_hi, w_hi, start=first, stop=False)
                        nc.tensor.matmul(o, l_hi, w_lo, start=False, stop=False)
                        mm = nc.tensor.matmul(o, l_lo, w_hi, start=False, stop=last)
                mm.then_inc(unit_used, 1)

            def cols_unit(c, j, right, kt_of, banks, nk, width):
                rh, rl = right
                unit_ready(c, j)
                for a in range(nk):
                    kt = kt_of(a)
                    first, last = j == 0 and a == 0, j == UNITS - 1 and a == nk - 1
                    for n in range(width // P):
                        o = banks[n // 2][:, (n % 2) * T:(n % 2 + 1) * T]
                        at = a * width + n * P
                        w_hi, w_lo = wh[:, j % RING, at:at + P], wl[:, j % RING, at:at + P]
                        nc.tensor.matmul(o, w_hi, rh[:, kt, :], start=first and n % 2 == 0, stop=False, skip_group_check=True)
                        nc.tensor.matmul(o, w_hi, rl[:, kt, :], start=False, stop=False, skip_group_check=True)
                        mm = nc.tensor.matmul(o, w_lo, rh[:, kt, :], start=False, stop=last, skip_group_check=True)
                mm.then_inc(unit_used, 1)

            def chunk_start(pair, free):
                pe.wait_ge(acc_free[pair], free + 1)

            def qk_turn(layer, a, h):
                if h == 0:
                    pe.wait_ge(qk_ready, a + 1 + (DA_PAIRS if layer else 0))
                n = head_no(layer, a, h)
                if h:
                    pe.wait_ge(qkt_sb, n)
                else:
                    pe.wait_ge(yt_lo, n + 1)
                for b in range(2):
                    for t in range(NT):
                        at = b * T + h * HD
                        mm = nc.tensor.transpose(trb[:, b * T + t * P:b * T + (t + 1) * P],
                                                 qk[:, t, at:at + HD], ident)
                mm.then_inc(qkt_ps, 1)

            def scores(layer, a, h, comp):
                k = (2 * h + comp) if layer == 0 else h
                n = score_no(layer, a, k)
                if comp == 0:
                    pe.wait_ge(qkt_sb, head_no(layer, a, h) + 1)
                if k:
                    pe.wait_ge(sc_max, n)
                else:
                    pe.wait_ge(y_ready, head_no(layer, a, 0) + 1)
                lo, hi = (64 * comp, 64 * comp + 64) if layer == 0 else (0, P)
                if layer:
                    pe.wait_ge(fox_b, n - 4 * DA_PAIRS + 1)
                for o, t, w in ((0, 1, T), (T, 0, P)):
                    mm = nc.tensor.matmul(scb[:, o:o + w], qkt[lo:hi, h, 0, t * P:(t + 1) * P],
                                          qkt[lo:hi, h, 1, 0:w], start=True, stop=layer == 0)
                    if layer:
                        mm = nc.tensor.matmul(scb[:, o:o + w], ones[0:16, :], nck[:, h, 0:w],
                                              start=False, stop=True)
                mm.then_inc(sc_ps, 1)

            def p_turn(layer, a, h):
                n = head_no(layer, a, h)
                pe.wait_ge(p_ready, n + 1)
                if h == 0:
                    pe.wait_ge(qkt_sb, head_no(layer, a, 1) + 1)
                else:
                    pe.wait_ge(pt_sb, n)
                for b in range(3):
                    mm = nc.tensor.transpose(trb[:, b * P:(b + 1) * P],
                                             s_sb[:, 2 * h, b * P:(b + 1) * P], ident)
                mm.then_inc(pt_ps, 1)

            def values(layer, a, h):
                n = head_no(layer, a, h)
                pe.wait_ge(pt_sb, n + 1)
                if h == 0:
                    if layer:
                        pe.wait_ge(acc_free[1], a + (FREE_FOX + 2))
                    else:
                        pe.wait_ge(vz_ready, a + 1)
                    pe.wait_ge(sc_max, score_no(layer, a, 3 if layer == 0 else 1) + 1)
                else:
                    pe.wait_ge(y_ready, n + 1)
                v = [vz[:, t, h * HD:(h + 1) * HD] for t in range(NT)]
                nc.tensor.matmul(scb[:, 0:P], p_t[:, h, 2 * P:3 * P], v[0], start=True, stop=True)
                nc.tensor.matmul(scb[:, P:2 * P], p_t[:, h, 0:P], v[0], start=True, stop=False)
                nc.tensor.matmul(scb[:, P:2 * P], p_t[:, h, P:2 * P], v[1], start=False, stop=True)\
                    .then_inc(pv_ps, 1)

            def y_turn(layer, a, h):
                n = head_no(layer, a, h)
                pe.wait_ge(y_ready, n + 2)
                if h == 0:
                    pe.wait_ge(pt_sb, head_no(layer, a, 1) + 1)
                else:
                    pe.wait_ge(yt_lo, n + 1)
                for t in range(NT):
                    mm = nc.tensor.transpose(trb[:, t * P:(t + 1) * P], y_o[:, h, t, :], ident)
                mm.then_inc(yt_ps, 1)

            def attention(layer, a, s):
                for h in range(2):
                    if QKT_SLOT[h] == s:
                        qk_turn(layer, a, h)
                for k, at in enumerate(SC_SLOT[layer]):
                    if at == s:
                        scores(layer, a, *((k // 2, k % 2) if layer == 0 else (k, 0)))
                for h in range(2):
                    if PT_SLOT[h] == s:
                        p_turn(layer, a, h)
                    if PV_SLOT[h] == s:
                        values(layer, a, h)
                    if YT_SLOT[h] == s:
                        y_turn(layer, a, h)

            def s5_in_x(i, j):
                c, q = j // 4, j % 4
                if j == 0:
                    pe.wait_ge(staged, i + 1)
                if not (isinstance(i, int) and i == 0 and j == 0):
                    pe.wait_ge(x_read, i * GPI + j)
                for r in range(2):
                    mm = nc.tensor.matmul(xb[:, r * T:(r + 1) * T], lb_st[32 * q:32 * q + 32, c, r, :],
                                          u_st[32 * q:32 * q + 32, c, :], start=True, stop=True)
                mm.then_inc(x_ps, 1)

            def s5_out_y(i, j):
                c, q = j // 4, j % 4
                pe.wait_ge(h_done, i * GPI + (j + 1))
                if j == 0 and not (isinstance(i, int) and i == 0):
                    pe.wait_ge(y_read, i)
                for r in range(2):
                    mm = nc.tensor.matmul(yb[32 * q:32 * q + 32, c * T:(c + 1) * T],
                                          cd_st[:, r, c, 32 * q:32 * q + 32], rot[j % 2][0][:, r, :],
                                          start=r == 0, stop=r == 1)
                mm.then_inc(y_ps, 1)

            pe.wait_ge(pool_const, 1)
            pe.wait_ge(par_in, 16 * 8)
            nc.tensor.transpose(xb[:, 0:48], rows, ident[0:48, 0:48])
            nc.tensor.transpose(xb[:, 64:96], lamr_r, ident[0:GP, 0:GP])
            nc.tensor.transpose(xb[:, 96:128], lami_r, ident[0:GP, 0:GP])
            pe.wait_ge(prm_rows, 1)
            nc.tensor.transpose(xb[:, 128:160], ldt_r.rearrange("p a b -> p (a b)"), ident[0:GP, 0:GP])\
                .then_inc(prm_ps, 1)
            pe.wait_ge(x_in, 16)
            for b in range(KT // 2):
                if b >= 2:
                    pe.wait_ge(tile_lo, 2 * (b - 1))
                for e in range(2):
                    for t in range(NT):
                        kt = 2 * b + e
                        mm = nc.tensor.transpose(bank[4 + b % 2][:, e * T + t * P:e * T + (t + 1) * P],
                                                 res[:, t, kt * P:(kt + 1) * P], ident)
                mm.then_inc(tile_ps, 1)

            def s5_matrix(m):
                if m >= 2:
                    pe.wait_ge(mat_sb, m - 1)
                if m == 0:
                    pe.wait_ge(bd_done, 1)
                if m == 8:
                    pe.wait_ge(cb_done, 2)
                for r in range(2):
                    src = bd[:, r, 4 * m:4 * m + 4, :].rearrange("p a b -> p (a b)") if m < 8 else (cb, cb2)[r][:, m - 8, :]
                    mm = nc.tensor.transpose(bank[4 + m % 2][:, r * P:(r + 1) * P], src, ident)
                mm.then_inc(mat_ps, 1)

            pe.wait_ge(tile_lo, KT)
            for c in range(4):
                chunk_start(c % 2, c // 2)
                for j in range(UNITS):
                    cols_unit(CH_S5 + c, j, (xh, xl), lambda a: UK * j + a, acc[c % 2], UK, CW)
                    if c == 0 and j == 5:
                        pe.wait_ge(diag_done, 1)
                        nc.tensor.matmul(yb[:, 0:T], ones, rbc, start=True, stop=True).then_inc(rbc_ps, 1)
                    if c == 2:
                        s5_matrix(2 * j)
                        s5_matrix(2 * j + 1)

            def step(layer, i, ch, use, first, side=None):
                for c in range(2):
                    chunk_start(c, i + use)
                    for j in range(UNITS):
                        s = c * UNITS + j
                        rows_unit(2 * i + (ch + c), j, (xh, xl), (UK * j, UK * j + 1), c)
                        if layer == 0:
                            for g in range(GPI):
                                if X_SLOT[g] == s:
                                    s5_in_x(i, g)
                                if Y_SLOT[g] == s:
                                    s5_out_y(i, g)
                        if not first:
                            attention(layer, i - 1, s)
                        if side:
                            side(s)

            step(0, 0, CH_DA, FREE_DA, True)
            with pe.Fori(1, DA_PAIRS) as i:
                step(0, i, CH_DA, FREE_DA, False)

            glu_banks = [acc[0][0], acc[0][1], acc[1][0], acc[1][1]]
            for s in (0, 1, 2, 3):
                attention(0, DA_PAIRS - 1, s)
            pe.wait_ge(s5_lo, 2 * DA_PAIRS)
            chunk_start(0, FREE_FOX)
            chunk_start(1, FREE_FOX)
            for j in range(UNITS):
                cols_unit(CH_GLU, j, (yh, yl), lambda a: j, glu_banks, 1, S5W)
                for s in ({0: [4], 1: [5], 3: [8], 4: [9], 5: [10], 6: [11], 7: [13]}).get(j, []):
                    attention(0, DA_PAIRS - 1, s)
            attention(0, DA_PAIRS - 1, 14)

            def x1_turn(n):
                pe.wait_ge(x1_done, 2 * (n + 1))
                if n == 0:
                    pe.wait_ge(yt_lo, 2 * DA_PAIRS + 1)
                for b in range(2):
                    o = bank[4 + 2 * (n % 2) + b]
                    if n >= 2:
                        pe.wait_ge(x1_lo, 4 * (n - 2) + 2 * b + 2)
                    for e in range(2):
                        for t in range(NT):
                            at = (2 * b + e) * P
                            mm = nc.tensor.transpose(o[:, e * T + t * P:e * T + (t + 1) * P],
                                                     x1_st[n % 2][:, t, at:at + P], ident)
                    mm.then_inc(x1_ps, 1)

            for n in range(4):
                if n < 2:
                    pe.wait_ge(glu_sig, CT)
                else:
                    pe.wait_ge(x1_done, 2 * (n - 1))
                for j in range(UNITS):
                    if n == 0 and j == 0:
                        pe.wait_ge(yt_lo, 2 * DA_PAIRS + 1)
                    if n == 0 and j == 4:
                        pe.wait_ge(glu_lo, CT)
                    kt = (8 + UK * j) % KT
                    rows_unit(CH_OUT0 + n, j, (yh, yl), (kt, kt + 1), n % 2)
                    if n and j == 2:
                        x1_turn(n - 1)

            def fox_gates():
                pe.wait_ge(wf_lo, 1)
                for t in range(NT):
                    for kt in range(KT):
                        w_hi, w_lo = whf[:, kt * 16:kt * 16 + 16], wlf[:, kt * 16:kt * 16 + 16]
                        o = yb[:, t * 16:t * 16 + 16]
                        l_hi, l_lo = xh[:, kt, t * P:(t + 1) * P], xl[:, kt, t * P:(t + 1) * P]
                        nc.tensor.matmul(o, l_hi, w_hi, start=kt == 0, stop=False)
                        nc.tensor.matmul(o, l_hi, w_lo, start=False, stop=False)
                        mm = nc.tensor.matmul(o, l_lo, w_hi, start=False, stop=kt == KT - 1)
                mm.then_inc(f_ps, 1)

            def fox_sums():
                pe.wait_ge(f_ls, 1)
                nc.tensor.matmul(yb[:, 64:80], upto, ls[:, 0, :], start=True, stop=True)
                nc.tensor.matmul(yb[:, 80:96], ones, ls[:, 0, :], start=True, stop=False)
                nc.tensor.matmul(yb[:, 80:96], upto, ls[:, 1, :], start=False, stop=True)
                nc.tensor.matmul(yb[0:16, 128:256], ls[:, 0, :], upto, start=True, stop=True)
                nc.tensor.matmul(yb[0:16, 256:384], ls[:, 0, :], ones, start=True, stop=False)
                nc.tensor.matmul(yb[0:16, 256:384], ls[:, 1, :], upto, start=False, stop=True)\
                    .then_inc(c_ps, 1)

            def side(s):
                if s == 0:
                    x1_turn(3)
                if s == 5:
                    pe.wait_ge(x1_lo, KT)
                if s == 8:
                    fox_gates()
                if s == 13:
                    fox_sums()

            pe.wait_ge(x1_lo, 12)
            def fox_first():
                for c in range(2):
                    pe.wait_ge(x1_done, 6 + 2 * c)
                    for j in range(UNITS):
                        s = c * UNITS + j
                        if s == 6:
                            pe.wait_ge(x1_lo, KT)
                        rows_unit(CH_FOX + c, j, (xh, xl), (UK * j, UK * j + 1), c)
                        side(s)

            fox_first()
            with pe.Fori(1, FOX_PAIRS) as i:
                step(1, i, CH_FOX, FREE_FOX, False)

            for n in range(4):
                if n < 2:
                    chunk_start(n, FREE_OUT1)
                else:
                    pe.wait_ge(x1_done, 8 + 2 * (n - 1))
                for j in range(UNITS):
                    if n == 0 and j == 0:
                        pe.wait_ge(yt_lo, 2 * (DA_PAIRS + FOX_PAIRS) - 1)
                    if n == 0 and j == UNITS - 1:
                        pe.wait_ge(yt_lo, 2 * (DA_PAIRS + FOX_PAIRS) + 1)
                    rows_unit(CH_OUT1 + n, j, (yh, yl), (UK * j, UK * j + 1), n % 2)
                    if n == 0:
                        for s in ({0: [0, 1, 2], 1: [4], 2: [8], 3: [9, 10], 4: [11], 5: [13], 6: [14]}).get(j, []):
                            attention(1, FOX_PAIRS - 1, s)

        def split_hi(act, c, j):
            if j >= UNITS:
                c, j = c + 1, j - UNITS
            act.wait_ge(raw_in[j % RING], c * 64 + (32 * (j // RING) + 32))
            act.wait_ge(unit_used, c * UNITS + (j - RING + 2)) if not (isinstance(c, int) and c * UNITS + j < RING) else None
            nc.scalar.activation(wh[:, j % RING, :], raw[:, j % RING, :], ACT.Copy).then_inc(hi_done, 1)

        def split_lo(dve, c, j):
            if j >= UNITS:
                c, j = c + 1, j - UNITS
            dve.wait_ge(hi_done, c * UNITS + (j + 1))
            nc.vector.tensor_tensor(wl[:, j % RING, :], raw[:, j % RING, :],
                                    wh[:, j % RING, :].bitcast(F32), ALU.subtract).then_inc(lo_done, 1)

        @block.scalar
        def _(act):
            link = act_link.inc

            def bc(src, n):
                return src.rearrange("(a n) -> a n", a=1).to_broadcast([P, n])

            act.dma_start(res[:, :, :], d["x"][0].rearrange("(t p) n -> p t n", p=P)).then_inc(x_in, 16)
            for at, name, n in ((0, "e_norm", 16), (16, "o_norm", 16), (32, "s5_d", 8), (40, "s5_b_glu", 8)):
                act.dma_start(rows[at:at + n, :], d[name][0].rearrange("(a n) -> a n", n=P)).then_inc(par_in, 16)
            act.dma_start(lamr_r, d["s5_lambda_re"][0].rearrange("(a b) p -> a (b p)", b=2)).then_inc(par_in, 16)
            act.dma_start(lami_r, d["s5_lambda_im"][0].rearrange("(a b) p -> a (b p)", b=2)).then_inc(par_in, 16)
            act.dma_start(ldt_in, d["s5_log_dt"][0].rearrange("(a b) -> a b", b=2)).then_inc(par_in, 16)
            act.dma_start(bf, bc(d["o_b_f"][0], 16)).then_inc(par_in, 16)
            for at, name in ((0, "s5_b_re"), (1, "s5_b_im")):
                act.dma_start(b_n[:, at, :, :], d[name][0].rearrange("(a b) p h -> (b p) a h", b=2)).then_inc(s5_in, 16)
            for at, name in ((0, "s5_c_re"), (1, "s5_c_im")):
                act.dma_start(c_n[:, at, :, :], d[name][0].rearrange("(a b) h p -> (b h) a p", b=8)).then_inc(s5_in, 16)
            for dst, name in ((g_da[:, 0, :], "da_q_norm"), (g_da[:, 1, :], "da_k_norm"), (g_dao, "da_out_norm"),
                              (g_fox[:, 0, :], "fox_q_norm"), (g_fox[:, 1, :], "fox_k_norm")):
                act.dma_start(dst, bc(d[name][0], P)).then_inc(bc_in, 16)
            for k, name in enumerate(("da_lambda_q1", "da_lambda_k1", "da_lambda_q2", "da_lambda_k2")):
                act.dma_start(lamv[:, k, :], bc(d[name][0], 64)).then_inc(bc_in, 16)

            for j in range(LEAD):
                split_hi(act, 0, j)
            act.wait_ge(prm_ps, 1)
            nc.scalar.activation(colp, xb[:, 0:48], ACT.Copy).then_inc(prm_ld, 1)
            act.wait_ge(prm_ld, 1)
            for kt in range(KT):
                if kt % 2 == 0:
                    act.wait_ge(tile_ps, kt // 2 + 1)
                nc.scalar.activation(xh[:, kt, :], bank[4 + kt // 2 % 2][:, kt % 2 * T:(kt % 2 + 1) * T],
                                     ACT.Copy, scale=e_col[:, kt:kt + 1]).then_inc(tile_hi, 1)
            for t in range(NT):
                ins = nc.scalar.activation(junk, res[:, t, :], ACT.Square, accum_out=ssq[:, t:t + 1])
                ins.then_inc(ssq_done, 1)
                act.wait_ge(ssq_done, t + 1)

            def params(c, j):
                if (c, j) == (0, 7):
                    act.wait_ge(prm_ang, 1)
                    nc.scalar.activation(prm[3], prm[2], ACT.Exp).then_inc(prm_exp, 1)
                if (c, j) == (1, 1):
                    act.wait_ge(prm_ang, 2)
                    nc.scalar.activation(phc[:, 2, :], prm[4], ACT.Exp).then_inc(prm_exp, 1)
                    act.wait_ge(lambda_done, 1)
                    nc.scalar.activation(lt[:, 2:4], lt[:, 0:2], ACT.Exp).then_inc(prm_exp, 1)
                    act.wait_ge(prm_ang, 3)
                    nc.scalar.activation(prm[11], prm[10], ACT.Sin, scale=SIN_SCALE).then_inc(prm_trig, 1)
                    nc.scalar.activation(prm[13], prm[10], ACT.Abs).then_inc(prm_trig, 1)
                    act.wait_ge(prm_trig, 2)
                    nc.scalar.activation(prm[12], prm[13], ACT.Sin, scale=-SIN_SCALE, bias=half_pi).then_inc(prm_trig, 1)
                if c == 2:
                    for m in (2 * j, 2 * j + 1):
                        act.wait_ge(mat_ps, m + 1)
                        o = bank[4 + m % 2][:, 0:2 * P].rearrange("p (r s) -> p r s", r=2)
                        dst = lb[:, m, :, :] if m < 8 else cd[:, :, m - 8, :]
                        nc.scalar.activation(dst, o, ACT.Copy).then_inc(mat_sb, 1)

            for c in range(4):
                for j in range(UNITS):
                    split_hi(act, c, j + LEAD)
                    params(c, j)
            act.wait_ge(acc_free[1], FREE_DA + 1)
            nc.scalar.activation(uz[:, CT:2 * CT, :], uz[:, CT:2 * CT, :], ACT.Silu).then_inc(silu_done, 1)

            def stage(i):
                if not (isinstance(i, int) and i == 0):
                    act.wait_ge(y_read, i)
                    act.wait_ge(ang_done, i * GPI)
                else:
                    act.wait_ge(mat_sb, 16)
                    act.wait_ge(prm_done, 1)
                    act.wait_ge(prm_exp, 2)
                    act.wait_ge(acc_free[1], FREE_DA)
                g, c = place(act, i * GPI), place(act, i * 2)
                nc.scalar.activation(cols.rearrange("p (a b) -> p a b", a=3), phc[:, :, bass.ds(g, GPI)], ACT.Copy)
                nc.scalar.activation(lb_st, lb[:, bass.ds(c, 2), :, :], ACT.Copy)
                nc.scalar.activation(cd_st, cd[:, :, bass.ds(c, 2), :], ACT.Copy)
                nc.scalar.activation(u_st, uz[:, bass.ds(c, 2), :], ACT.Copy).then_inc(staged, 1)

            def table(i, j):
                act.wait_ge(ang_done, i * GPI + (j + 1))
                if j >= 2 or not (isinstance(i, int) and i == 0):
                    act.wait_ge(h_done, i * GPI + (j - 1))
                a = ang[j % 2]
                nc.scalar.activation(tab[j % 2][:, 1, :], a, ACT.Sin, scale=SIN_SCALE).then_inc(tab_done, 1)
                link(nc.scalar.activation(a, a, ACT.Abs))
                act.wait_ge(act_link.sem, act_link.value())
                nc.scalar.activation(tab[j % 2][:, 0, :], a, ACT.Sin, scale=-SIN_SCALE, bias=half_pi).then_inc(tab_done, 1)

            def gelus(i):
                act.wait_ge(y_read, i + 1)
                for c in (1, 0):
                    at = uz[:, bass.ds(place(act, i * 2 + c), 1), :].rearrange("p a t -> p (a t)")
                    nc.scalar.activation(at, u_st[:, c, :], ACT.Gelu_apprx_tanh).then_inc(gelu_done, 1)
                for k, c in enumerate((1, 0)):
                    act.wait_ge(gelu_done, i * 2 + (k + 1))
                    at = bass.ds(place(act, i * 2 + c), 1)
                    nc.scalar.activation(yh[:, at, :], uz[:, at, :], ACT.Copy).then_inc(s5_hi, 1)

            def qk_out(layer, i):
                r = r2_tok if layer else r_tok
                na = DA_PAIRS if layer else 0
                act.wait_ge(unit_used, i * (2 * UNITS) + (UNITS * ((CH_FOX if layer else CH_DA) + 1) + 1))
                if layer and isinstance(i, int):
                    act.wait_ge(r2_done, 1)
                if not (isinstance(i, int) and i == 0 and layer == 0):
                    act.wait_ge(qkt_ps, i * 2 + 2 * na)
                nc.scalar.activation(qk[:, 0, :], acc[0][0][:, :], ACT.Copy, scale=r[:, 0:1])
                nc.scalar.activation(qk[:, 1, :], acc[0][1][:, :], ACT.Copy, scale=r[:, 1:2]).then_inc(acc_free[0], 1)

            def vz_out(layer, i):
                r = r2_tok if layer else r_tok
                na = DA_PAIRS if layer else 0
                act.wait_ge(unit_used, i * (2 * UNITS) + (UNITS * ((CH_FOX if layer else CH_DA) + 2) + 1))
                if not (isinstance(i, int) and i == 0 and layer == 0):
                    act.wait_ge(y_ready, i * 2 + (2 * na + 1))
                for t in range(NT):
                    nc.scalar.activation(vz[:, t, 0:T], acc[1][t][:, 0:T], ACT.Copy, scale=r[:, t:t + 1])
                for t in range(NT):
                    ins = nc.scalar.activation(vz[:, t, T:2 * T], acc[1][t][:, T:2 * T], ACT.Silu, scale=r[:, t:t + 1])
                ins.then_inc(acc_free[1], 1)

            def qkt_out(layer, a, h):
                act.wait_ge(qkt_ps, head_no(layer, a, h) + 1)
                nc.scalar.activation(qkt[:, h, :, :], trb[:, :].rearrange("p (a b) -> p a b", a=2), ACT.Copy)\
                    .then_inc(qkt_sb, 1)

            def exps(layer, a, k):
                s = k if layer == 0 else 2 * k
                act.wait_ge(sc_max, score_no(layer, a, k) + 1)
                for t, o, w in ((0, T, P), (1, 0, T)):
                    ins = nc.scalar.activation(s_sb[:, s, o:o + w], s_sb[:, s, o:o + w], ACT.Exp,
                                               bias=nmax[:, 2 * s + t:2 * s + t + 1],
                                               accum_out=lsum[:, 2 * s + t:2 * s + t + 1])
                ins.then_inc(p_exp if layer == 0 else p_ready, 1)

            def pt_out(layer, a, h):
                n = head_no(layer, a, h)
                act.wait_ge(pt_ps, n + 1)
                nc.scalar.activation(p_t[:, h, :], trb[:, 0:3 * P], ACT.Copy).then_inc(pt_sb, 1)

            def out_squares(a, h):
                act.wait_ge(pv_ps, head_no(0, a, h) + 1)
                for t in range(NT):
                    ins = nc.scalar.activation(y_o[:, h, t, :], scb[:, t * P:(t + 1) * P], ACT.Square, scale=HD ** -0.5,
                                               accum_out=sso[:, 2 * h + t:2 * h + t + 1])
                ins.then_inc(pv_ssq, 1)

            def yt_out(layer, a, h):
                n = head_no(layer, a, h)
                act.wait_ge(yt_ps, n + 1)
                kt = place(act, 2 * a + h + (8 if layer == 0 else 0))
                nc.scalar.activation(yh[:, bass.ds(kt, 1), :], trb[:, 0:T].rearrange("p (a t) -> p a t", a=1), ACT.Copy)\
                    .then_inc(yt_hi, 1)

            def fox_cols(a, h):
                n = 2 * a + h
                if h == 0:
                    act.wait_ge(sc_max, score_no(1, a, 0))
                    act.wait_ge(c_done, 2)
                nc.scalar.activation(cq[:, 2 * h:2 * h + 2].rearrange("p (a b) -> p a b", b=1),
                                     c_sb[:, :, bass.ds(place(act, n), 1)], ACT.Copy).then_inc(fox_cq, 1)

            def attention(layer, a, s):
                for h in range(2):
                    if QKT_SLOT[h] == s:
                        qkt_out(layer, a, h)
                        if layer:
                            fox_cols(a, h)
                for k, at in enumerate(SC_SLOT[layer]):
                    if at + 1 == s:
                        exps(layer, a, k)
                for h in range(2):
                    if PT_SLOT[h] == s:
                        pt_out(layer, a, h)
                    if PV_SLOT[h] == s and layer == 0:
                        out_squares(a, h)
                    if YT_SLOT[h] == s:
                        yt_out(layer, a, h)

            def step(layer, i, ch, first, side=None):
                for c in range(2):
                    for j in range(UNITS):
                        s = c * UNITS + j
                        split_hi(act, 2 * i + (ch + c), j + LEAD)
                        if layer == 0:
                            if s == 0:
                                stage(i)
                            for g in range(GPI):
                                if X_SLOT[g] - 1 == s:
                                    table(i, g)
                        if not first:
                            attention(layer, i - 1, s)
                        if side:
                            side(s)
                    if c == 0:
                        qk_out(layer, i)
                    else:
                        vz_out(layer, i)
                if layer == 0:
                    gelus(i)

            step(0, 0, CH_DA, True)
            with act.Fori(1, DA_PAIRS) as i:
                act_link.enter(i - 1, GPI)
                step(0, i, CH_DA, False)
            act_link.leave(DA_PAIRS - 1)

            for s in (0, 1, 2, 3):
                attention(0, DA_PAIRS - 1, s)
            for j in range(UNITS):
                split_hi(act, CH_GLU, j + LEAD)
                for s in ({0: [4], 1: [5], 2: [6], 3: [8], 4: [9], 5: [10], 6: [11], 7: [13]}).get(j, []):
                    attention(0, DA_PAIRS - 1, s)
            attention(0, DA_PAIRS - 1, 14)

            def glu_out(n):
                if n == 0:
                    act.wait_ge(unit_used, UNITS * (CH_GLU + 1) + 1)
                if n >= 2:
                    act.wait_ge(glu_y, n - 1)
                nc.scalar.activation(glu_s[:, n % 2, :], acc[n // 4][n // 2 % 2][:, n % 2 * T:(n % 2 + 1) * T],
                                     ACT.Sigmoid, bias=bg_col[:, n:n + 1]).then_inc(glu_sig, 1)

            def glu_up(n):
                act.wait_ge(glu_y, n + 1)
                nc.scalar.activation(yh[:, n, :], uz[:, n, :], ACT.Copy).then_inc(glu_hi, 1)

            for n in range(CT):
                glu_out(n)
                if n >= 1:
                    glu_up(n - 1)
            glu_up(CT - 1)

            def x1_up(n):
                for e in range(4):
                    kt = 4 * n + e
                    if e % 2 == 0:
                        act.wait_ge(x1_ps, 2 * n + e // 2 + 1)
                    nc.scalar.activation(xh[:, kt, :], bank[4 + 2 * (n % 2) + e // 2][:, e % 2 * T:(e % 2 + 1) * T],
                                         ACT.Copy, scale=o_col[:, kt:kt + 1]).then_inc(x1_hi, 1)

            def x1_keep(n):
                for t in range(NT):
                    act.wait_ge(x1_done, 2 * n + t + 1)
                    if n or t:
                        act.wait_ge(x1_ssq, 2 * n + t)
                    nc.scalar.activation(sq, x1_st[n % 2][:, t, :], ACT.Square,
                                         accum_out=ss1[:, t, n:n + 1]).then_inc(x1_ssq, 1)

            for n in range(4):
                for j in range(UNITS):
                    split_hi(act, CH_OUT0 + n, j + LEAD)
                    if n and j == 2:
                        x1_up(n - 1)
                x1_keep(n)

            act.dma_start(wf, d["o_w_in"][0].rearrange("(k p) n -> p k n", p=P)[:, :, 4 * D:4 * D + 16]).then_inc(wf_in, 16)

            def side(s):
                if s == 0:
                    x1_up(3)
                if s == 2:
                    act.wait_ge(wf_in, 16)
                    nc.scalar.activation(whf[:, :], wf.rearrange("p a b -> p (a b)"), ACT.Copy).then_inc(wf_hi, 1)
                if s == 9:
                    act.wait_ge(f_z, 1)
                    nc.scalar.activation(lsa, ls, ACT.Abs).then_inc(f_abs, 1)
                    act.wait_ge(f_abs, 1)
                    nc.scalar.activation(lsa, lsa, ACT.Exp, scale=-1.0).then_inc(f_abs, 1)
                if s == 10:
                    act.wait_ge(f_exp1, 1)
                    nc.scalar.activation(lsa, lsa, ACT.Ln).then_inc(f_ln, 1)
                if s == 13:
                    act.wait_ge(c_ps, 1)
                    nc.scalar.activation(c_sb, yb[:, 64:96].rearrange("p (a b) -> p a b", a=2), ACT.Copy).then_inc(c_done, 1)
                    nc.scalar.mul(nct, yb[0:16, 128:384], -1.0).then_inc(c_done, 1)

            step(1, 0, CH_FOX, True, side)
            with act.Fori(1, FOX_PAIRS) as i:
                step(1, i, CH_FOX, False)

            for n in range(4):
                for j in range(UNITS):
                    if UNITS * (CH_OUT1 + n) + j + LEAD < UNITS * CH_END:
                        split_hi(act, CH_OUT1 + n, j + LEAD)
                    if n == 0:
                        for s in ({0: [0, 1, 2, 3], 1: [4, 5], 2: [8], 3: [9, 10], 4: [11], 5: [13], 6: [14]}).get(j, []):
                            attention(1, FOX_PAIRS - 1, s)
                act.wait_ge(x1_done, 8 + 2 * (n + 1))
                act.dma_start(out_dram[0, :, n * CW:(n + 1) * CW].rearrange("(t p) n -> p t n", p=P),
                              res[:, :, n * CW:(n + 1) * CW]).then_inc(out_done, 16)

        @block.vector
        def _(dve):
            def link(ins):
                dve_link.inc(ins)
                dve.wait_ge(dve_link.sem, dve_link.value())

            v = nc.vector

            v.memset(half_pi, 0.5 * math.pi)
            v.memset(magic, MAGIC)
            link(v.memset(eps, EPS))
            for k, first in enumerate((yt_lo, y_ready, acc_free[0], acc_free[1], unit_used)):
                v.memset(junk1[:, k:k + 1], 0.0).then_inc(first, 1)
            v.memset(expo, -0.5).then_inc(slopes, 1)
            for j in range(LEAD):
                split_lo(dve, 0, j)
            dve.wait_ge(par_in, 16 * 8)
            v.tensor_copy(ldt_r, ldt_in.rearrange("p (a b) -> p a b", b=1).to_broadcast([GP, 2, 64])).then_inc(prm_rows, 1)
            for kt in range(KT):
                dve.wait_ge(tile_hi, 2 * (kt // 2) + 2)
                v.scalar_tensor_tensor(out=xl[:, kt, :], in0=bank[4 + kt // 2 % 2][:, kt % 2 * T:(kt % 2 + 1) * T],
                                       scalar=e_col[:, kt:kt + 1], in1=xh[:, kt, :].bitcast(F32),
                                       op0=ALU.mult, op1=ALU.subtract).then_inc(tile_lo, 1)

            def diagonal():
                dve.wait_ge(r_done, 1)
                dve.wait_ge(pool_const, 1)
                for t in range(NT):
                    ins = v.tensor_scalar(rbc[:, t * P:(t + 1) * P], ident, r_tok[:, t:t + 1], None, ALU.mult)
                ins.then_inc(diag_done, 1)

            def rbc_out():
                dve.wait_ge(rbc_ps, 1)
                v.tensor_copy(rbc, yb[:, 0:T]).then_inc(rbc_done, 1)

            lr, li, ldt, dt, lrdt, th, n, a, b, _, turn, sn, cs, ab, den, t1, t2, kr, ki, nr = prm

            def angles_ready():
                dve.wait_ge(prm_ld, 1)
                v.tensor_copy(lr, xb[:, 64:96])
                v.tensor_copy(li, xb[:, 96:128])
                v.tensor_copy(ldt, xb[:, 128:160]).then_inc(prm_ang, 1)

            def turns():
                dve.wait_ge(prm_ang, 1)
                dve.wait_ge(prm_exp, 1)
                v.tensor_tensor(lrdt, lr, dt, ALU.mult).then_inc(prm_ang, 1)
                link(v.tensor_tensor(th, li, dt, ALU.mult))
                link(v.tensor_scalar(n, th, 1.0 / TWO_PI, MAGIC, ALU.mult, ALU.add))
                link(v.tensor_scalar(n, n, -MAGIC, None, ALU.add))
                link(v.scalar_tensor_tensor(out=a, in0=n, scalar=-PI_A, in1=th, op0=ALU.mult, op1=ALU.add))
                link(v.scalar_tensor_tensor(out=a, in0=n, scalar=-PI_B, in1=a, op0=ALU.mult, op1=ALU.add))
                link(v.tensor_scalar(phr[:, :], a, 1.0 / TWO_PI, None, ALU.mult))
                link(v.tensor_copy(phc[:, 0, :], phr[:, :].bitcast(F32)))
                link(v.scalar_tensor_tensor(out=b, in0=phc[:, 0, :], scalar=-PI_A, in1=a, op0=ALU.mult, op1=ALU.add))
                link(v.scalar_tensor_tensor(out=b, in0=phc[:, 0, :], scalar=-PI_B, in1=b, op0=ALU.mult, op1=ALU.add))
                link(v.tensor_tensor(n, n, phc[:, 0, :], ALU.add))
                link(v.scalar_tensor_tensor(out=b, in0=n, scalar=-PI_C, in1=b, op0=ALU.mult, op1=ALU.add))
                link(v.tensor_scalar(phc[:, 1, :], b, 1.0 / TWO_PI, None, ALU.mult))
                v.tensor_tensor(turn, phc[:, 0, :], phc[:, 1, :], ALU.add).then_inc(prm_ang, 1)

            def b_factors():
                link(v.tensor_tensor(t1, lr, lr, ALU.mult))
                link(v.tensor_tensor(t2, li, li, ALU.mult))
                link(v.tensor_tensor(den, t1, t2, ALU.add))
                link(v.reciprocal(den, den))
                dve.wait_ge(prm_exp, 2)
                dve.wait_ge(prm_trig, 3)
                mag = phc[:, 2, :]
                link(v.tensor_tensor(nr, mag, cs, ALU.mult))
                link(v.tensor_scalar(nr, nr, -1.0, None, ALU.add))
                link(v.tensor_tensor(sn, mag, sn, ALU.mult))
                link(v.tensor_tensor(t1, nr, lr, ALU.mult))
                link(v.tensor_tensor(t2, sn, li, ALU.mult))
                link(v.tensor_tensor(kr, t1, t2, ALU.add))
                link(v.tensor_tensor(kr, kr, den, ALU.mult))
                link(v.tensor_tensor(t1, sn, lr, ALU.mult))
                link(v.tensor_tensor(t2, nr, li, ALU.mult))
                link(v.tensor_tensor(ki, t1, t2, ALU.subtract))
                link(v.tensor_tensor(ki, ki, den, ALU.mult))
                v.memset(bd, 0.0).then_inc(prm_done, 1)

            def b_blocks():
                dve.wait_ge(s5_in, 16 * 4)

                def wide(x):
                    return x.rearrange("p (a b) -> p a b", b=1).to_broadcast([P, GP, 16])

                br, bi = b_n[:, 0, :, :], b_n[:, 1, :, :]
                v.tensor_tensor(bt[0], br, wide(kr), ALU.mult)
                v.tensor_tensor(bt[1], bi, wide(ki), ALU.mult)
                v.tensor_tensor(bt[2], bi, wide(kr), ALU.mult)
                link(v.tensor_tensor(bt[3], br, wide(ki), ALU.mult))
                dve.wait_ge(prm_done, 1)
                for g in range(2):
                    rows_ = slice(64 * g, 64 * g + 64)
                    for r, op in ((0, ALU.subtract), (1, ALU.add)):
                        ins = v.tensor_tensor(bd[rows_, r, :, 16 * g:16 * g + 16], bt[2 * r][rows_], bt[2 * r + 1][rows_], op)
                ins.then_inc(bd_done, 1)

            def c_blocks():
                dve.wait_ge(pool_const, 2)
                link(v.tensor_scalar(pint.bitcast(I32), pint.bitcast(I32), 16, None, ALU.bitwise_and))
                link(v.tensor_copy(par[:, 1:2], pint.bitcast(I32)))
                link(v.tensor_scalar(par[:, 1:2], par[:, 1:2], 1.0 / 16, None, ALU.mult))
                link(v.tensor_scalar(par[:, 0:1], par[:, 1:2], -1.0, 1.0, ALU.mult, ALU.add))
                for r, dst, sign in ((0, cb, 1.0), (1, cb2, -1.0)):
                    for g in range(2):
                        ins = v.tensor_scalar(dst[:, :, 64 * g:64 * g + 64], c_n[:, r, :, :], par[:, g:g + 1],
                                              sign, ALU.mult, ALU.mult)
                    ins.then_inc(cb_done, 1)

            def gains():
                dve.wait_ge(bc_in, 16 * 9)
                v.tensor_scalar(g_da[:, 0, :], g_da[:, 0, :], 64 ** -0.5, None, ALU.mult)
                v.tensor_scalar(g_fox[:, 0, :], g_fox[:, 0, :], float(HD) ** -0.5, None, ALU.mult)
                v.tensor_scalar(g_dao, g_dao, 1.0 - LAMBDA_INIT, None, ALU.mult).then_inc(slopes, 1)
                link(v.tensor_tensor(lamv[:, 0:4:2, :], lamv[:, 0:4:2, :], lamv[:, 1:4:2, :], ALU.mult))
                v.tensor_reduce(lt[:, 0:2], lamv[:, 0:4:2, :], AX.X, ALU.add).then_inc(lambda_done, 1)
                for h in range(2):
                    ins = v.memset(slope[:, h:h + 1], -(2.0 ** -(h + 1)))
                link(ins)

            def lam_end():
                dve.wait_ge(prm_exp, 3)
                link(v.tensor_tensor(nlam, lt[:, 2:3], lt[:, 3:4], ALU.subtract))
                link(v.tensor_scalar(nlam, nlam, LAMBDA_INIT, None, ALU.add))

            aside = {(0, 1): gains, (0, 3): diagonal, (0, 6): angles_ready, (1, 0): turns, (1, 3): b_factors,
                     (1, 4): b_blocks, (1, 5): c_blocks, (1, 6): lam_end}
            for c in range(4):
                for j in range(UNITS):
                    split_lo(dve, c, j + LEAD)
                    if (c, j) in aside:
                        aside[c, j]()
                if c == 0:
                    rbc_out()
                    dve.wait_ge(rbc_done, 1)
                dve.wait_ge(unit_used, UNITS * (c + 1) + 1)
                for half in range(2):
                    o = acc[c % 2][half][:, :].rearrange("p (a t) -> p a t", a=2)
                    ins = v.tensor_tensor(uz[:, 4 * c + 2 * half:4 * c + 2 * half + 2, :], o,
                                          rbc.rearrange("p (a t) -> p a t", a=1).to_broadcast([P, 2, T]), ALU.mult)
                ins.then_inc(acc_free[c % 2], 1)

            def rotate_in(i, j):
                dve.wait_ge(x_ps, i * GPI + (j + 1))
                dve.wait_ge(tab_done, i * (2 * GPI) + 2 * (j + 1))
                if j >= 2 or not (isinstance(i, int) and i == 0):
                    dve.wait_ge(y_ps, i * GPI + (j - 1))
                m1, m2, _ = rot[j % 2]
                x = xb[:, :].rearrange("p (r t) -> p r t", r=2)
                c, s = (tab[j % 2][:, k:k + 1, :].to_broadcast([P, 2, T]) for k in range(2))
                v.tensor_tensor(m1, x, c, ALU.mult)
                v.tensor_tensor(m2, x, s, ALU.mult).then_inc(x_read, 1)

            def scan(i, j):
                dve.wait_ge(g_done, i * GPI + (j + 1))
                m1, _, g = rot[j % 2]
                mag = cols[:, 2 * GPI + j:2 * GPI + j + 1].to_broadcast([P, T])
                for r in range(2):
                    ins = v.tensor_tensor_scan(m1[:, r, :], mag, g[:, r, :], 0.0, ALU.mult, ALU.add)
                ins.then_inc(scan_done, 1)
                dve.wait_ge(scan_done, i * GPI + (j + 1))
                c = tab[j % 2][:, 0:1, :].to_broadcast([P, 2, T])
                v.tensor_tensor(g, m1, c, ALU.mult).then_inc(n1_done, 1)

            def s5_out(i):
                dve.wait_ge(y_ps, i * GPI + GPI)
                for c in range(2):
                    ins = v.scalar_tensor_tensor(out=u_st[:, c, :], in0=u_st[:, c, :],
                                                 scalar=d_col[:, bass.ds(i * 2 + c, 1)],
                                                 in1=yb[:, c * T:(c + 1) * T], op0=ALU.mult, op1=ALU.add)
                ins.then_inc(y_read, 1)

            def s5_low(i):
                for k, c in enumerate((1, 0)):
                    dve.wait_ge(s5_hi, i * 2 + (k + 1))
                    at = bass.ds(i * 2 + c, 1)
                    v.tensor_tensor(yl[:, at, :], uz[:, at, :], yh[:, at, :].bitcast(F32), ALU.subtract).then_inc(s5_lo, 1)

            def qk_squares(layer, i):
                na = DA_PAIRS if layer else 0
                seg = 64 if layer == 0 else HD
                dve.wait_ge(acc_free[0], i + ((FREE_FOX if layer else FREE_DA) + 2))
                n = CW // seg
                for t in range(NT):
                    link(v.tensor_tensor(sq, qk[:, t, :], qk[:, t, :], ALU.mult))
                    ins = v.tensor_reduce(ssn[:, t * n:(t + 1) * n], sq.rearrange("p (s e) -> p s e", e=seg), AX.X, ALU.add)
                    link(ins)
                n *= NT
                v.tensor_scalar(ssn[:, 0:n], ssn[:, 0:n], 1.0 / seg, EPS, ALU.mult, ALU.add).then_inc(qk_ss, 1)

            def score_in(layer, a, k):
                h = k // 2 if layer == 0 else k
                s = k if layer == 0 else 2 * k
                dve.wait_ge(sc_ps, score_no(layer, a, k) + 1)
                if layer == 0:
                    link(v.scalar_tensor_tensor(out=s_sb[:, s, :], in0=dist, scalar=slope[:, h:h + 1],
                                                in1=scb[:, 0:3 * P], op0=ALU.mult, op1=ALU.add))
                else:
                    dve.wait_ge(fox_cq, 2 * a + (k + 1))
                    v.scalar_tensor_tensor(out=s_sb[:, s, 0:T], in0=mask[:, 0:T], scalar=cq[:, 2 * h + 1:2 * h + 2],
                                           in1=scb[:, 0:T], op0=ALU.add, op1=ALU.add)
                    link(v.scalar_tensor_tensor(out=s_sb[:, s, T:T + P], in0=mask[:, T:T + P], scalar=cq[:, 2 * h:2 * h + 1],
                                                in1=scb[:, T:T + P], op0=ALU.add, op1=ALU.add))
                v.tensor_reduce(nmax[:, 2 * s:2 * s + 1], s_sb[:, s, T:T + P], AX.X, ALU.max, negate=True)
                v.tensor_reduce(nmax[:, 2 * s + 1:2 * s + 2], s_sb[:, s, 0:T], AX.X, ALU.max, negate=True).then_inc(sc_max, 1)

            def combine(a, h):
                dve.wait_ge(p_exp, score_no(0, a, 2 * h + 1) + 1)
                k = 4 * h
                link(v.reciprocal(rec[:, k:k + 4], lsum[:, k:k + 4]))
                link(v.tensor_scalar(rec[:, k + 2:k + 4], rec[:, k + 2:k + 4], nlam, None, ALU.mult))
                for t, o, w in ((0, T, P), (1, 0, T)):
                    p1, p2 = s_sb[:, 2 * h, o:o + w], s_sb[:, 2 * h + 1, o:o + w]
                    ins = v.tensor_scalar(p2, p2, rec[:, k + 2 + t:k + 3 + t], None, ALU.mult)
                link(ins)
                for t, o, w in ((0, T, P), (1, 0, T)):
                    p1, p2 = s_sb[:, 2 * h, o:o + w], s_sb[:, 2 * h + 1, o:o + w]
                    ins = v.scalar_tensor_tensor(out=p1, in0=p1, scalar=rec[:, k + t:k + t + 1], in1=p2,
                                                 op0=ALU.mult, op1=ALU.subtract)
                ins.then_inc(p_ready, 1)

            def head_out(layer, a, h):
                n = head_no(layer, a, h)
                if layer == 0:
                    dve.wait_ge(pv_rn, n + 1)
                    scale = rno[:, 2 * h:2 * h + 2]
                else:
                    dve.wait_ge(pv_ps, n + 1)
                    link(v.reciprocal(rec[:, 4 * h:4 * h + 2], lsum[:, 4 * h:4 * h + 2]))
                    scale = rec[:, 4 * h:4 * h + 2]
                for t in range(NT):
                    ins = v.scalar_tensor_tensor(out=y_o[:, h, t, :], in0=scb[:, t * P:(t + 1) * P],
                                                 scalar=scale[:, t:t + 1], in1=vz[:, t, T + h * HD:T + (h + 1) * HD],
                                                 op0=ALU.mult, op1=ALU.mult)
                ins.then_inc(y_ready, 1)

            def yt_low(layer, a, h):
                n = head_no(layer, a, h)
                dve.wait_ge(yt_hi, n + 1)
                kt = bass.ds(2 * a + h + (8 if layer == 0 else 0), 1)
                v.tensor_tensor(yl[:, kt, :], trb[:, 0:T].rearrange("p (a t) -> p a t", a=1),
                                yh[:, kt, :].bitcast(F32), ALU.subtract).then_inc(yt_lo, 1)

            def fox_keys(a, h):
                if h == 0:
                    dve.wait_ge(sc_ps, score_no(1, a, 0))
                    dve.wait_ge(c_done, 2)
                v.tensor_scalar(nck[:, h, :], nct, ident[0:16, bass.ds(2 * a + h, 1)], None, ALU.mult).then_inc(fox_b, 1)

            def attention(layer, a, s):
                for h in range(2):
                    if QKT_SLOT[h] == s and layer:
                        fox_keys(a, h)
                for k, at in enumerate(SC_SLOT[layer]):
                    if at == s:
                        score_in(layer, a, k)
                if layer == 0 and s in (5, 7):
                    combine(a, 0 if s == 5 else 1)
                for h in range(2):
                    if PV_SLOT[h] + (1 if layer == 0 else 0) == s:
                        head_out(layer, a, h)
                    if YT_SLOT[h] == s:
                        yt_low(layer, a, h)
                if layer == 0 and s == 7:
                    link(v.tensor_scalar(slope, slope, 0.25, None, ALU.mult))

            def step(layer, i, ch, first, side=None):
                for c in range(2):
                    for j in range(UNITS):
                        s = c * UNITS + j
                        split_lo(dve, 2 * i + (ch + c), j + LEAD)
                        if layer == 0:
                            for g in range(GPI):
                                if X_SLOT[g] + 1 == s:
                                    scan(i, g)
                                if X_SLOT[g] == s:
                                    rotate_in(i, g)
                        if not first:
                            attention(layer, i - 1, s)
                        if side:
                            side(s)
                        if s == UNITS:
                            qk_squares(layer, i)
                if layer == 0:
                    s5_out(i)
                    s5_low(i)

            step(0, 0, CH_DA, True)
            with dve.Fori(1, DA_PAIRS) as i:
                dve_link.enter(i - 1, DA_LINKS)
                step(0, i, CH_DA, False)
            dve_link.leave(DA_PAIRS - 1)

            for s in (0, 1, 2, 3):
                attention(0, DA_PAIRS - 1, s)
            for j in range(UNITS):
                split_lo(dve, CH_GLU, j + LEAD)
                for s in ({0: [4], 1: [5], 2: [7], 3: [8], 4: [9], 5: [10, 11], 6: [12], 7: [13]}).get(j, []):
                    attention(0, DA_PAIRS - 1, s)
            attention(0, DA_PAIRS - 1, 14)

            def glu_mul(n):
                if n == 0:
                    dve.wait_ge(silu_done, 1)
                dve.wait_ge(glu_sig, n + 1)
                v.tensor_tensor(glu_s[:, n % 2, :], glu_s[:, n % 2, :], uz[:, CT + n, :], ALU.mult).then_inc(glu_y0, 1)
                dve.wait_ge(glu_y0, n + 1)
                ins = v.tensor_tensor(uz[:, n, :], uz[:, n, :], glu_s[:, n % 2, :], ALU.mult)
                ins.then_inc(glu_y, 1)

            def glu_low(n):
                dve.wait_ge(glu_hi, n + 1)
                v.tensor_tensor(yl[:, n, :], uz[:, n, :], yh[:, n, :].bitcast(F32), ALU.subtract).then_inc(glu_lo, 1)

            for n in range(CT):
                glu_mul(n)
                if n >= 1:
                    glu_low(n - 1)
            glu_low(CT - 1)

            def x1_low(n):
                for e in range(4):
                    kt = 4 * n + e
                    dve.wait_ge(x1_hi, 2 * (kt // 2) + 2)
                    v.scalar_tensor_tensor(out=xl[:, kt, :],
                                           in0=bank[4 + 2 * (n % 2) + e // 2][:, e % 2 * T:(e % 2 + 1) * T],
                                           scalar=o_col[:, kt:kt + 1], in1=xh[:, kt, :].bitcast(F32),
                                           op0=ALU.mult, op1=ALU.subtract).then_inc(x1_lo, 1)

            for n in range(4):
                for j in range(UNITS):
                    split_lo(dve, CH_OUT0 + n, j + LEAD)
                    if n and j == 2:
                        x1_low(n - 1)
                dve.wait_ge(unit_used, UNITS * (CH_OUT0 + n + 1) + 1)
                if n == 0:
                    dve.wait_ge(res_in, 16)
                if n >= 2:
                    dve.wait_ge(x1_ps, 2 * (n - 1))
                    dve.wait_ge(x1_kept, n - 1)
                    dve.wait_ge(x1_ssq, 2 * (n - 1))
                for t in range(NT):
                    v.tensor_tensor(x1_st[n % 2][:, t, :], res[:, t, n * CW:(n + 1) * CW], acc[n % 2][t][:, :], ALU.add)\
                        .then_inc(x1_done, 1)
            dve.wait_ge(x1_ssq, 8)
            v.tensor_reduce(ssr, ss1, AX.X, ALU.add).then_inc(r2_sum, 1)

            def side(s):
                if s == 0:
                    x1_low(3)
                if s == 2:
                    dve.wait_ge(wf_hi, 1)
                    v.tensor_tensor(wlf[:, :], wf.rearrange("p a b -> p (a b)"), whf[:, :].bitcast(F32), ALU.subtract).then_inc(wf_lo, 1)
                if s == 8:
                    dve.wait_ge(f_ps, 1)
                    dve.wait_ge(r2_done, 1)
                    for t in range(NT):
                        ins = v.scalar_tensor_tensor(out=ls[:, t, :], in0=yb[:, 16 * t:16 * t + 16], scalar=r2_tok[:, t:t + 1],
                                                     in1=bf, op0=ALU.mult, op1=ALU.add)
                    ins.then_inc(f_z, 1)
                if s == 9:
                    dve.wait_ge(f_abs, 2)
                    v.tensor_scalar(lsa, lsa, 1.0, None, ALU.add).then_inc(f_exp1, 1)
                if s == 11:
                    dve.wait_ge(f_ln, 1)
                    link(v.tensor_scalar(ls, ls, 0.0, None, ALU.min))
                    v.tensor_tensor(ls, ls, lsa, ALU.subtract).then_inc(f_ls, 1)

            step(1, 0, CH_FOX, True, side)
            with dve.Fori(1, FOX_PAIRS) as i:
                dve_link.enter(i - 1, FOX_LINKS)
                step(1, i, CH_FOX, False)
            dve_link.leave(FOX_PAIRS - 1)

            for n in range(4):
                for j in range(UNITS):
                    if UNITS * (CH_OUT1 + n) + j + LEAD < UNITS * CH_END:
                        split_lo(dve, CH_OUT1 + n, j + LEAD)
                    if n == 0:
                        for s in ({0: [0, 1, 2], 1: [4], 3: [10], 4: [11], 5: [13], 6: [14]}).get(j, []):
                            attention(1, FOX_PAIRS - 1, s)
                dve.wait_ge(unit_used, UNITS * (CH_OUT1 + n + 1) + 1)
                if n == 0:
                    dve.wait_ge(x1_kept, 4)
                for t in range(NT):
                    at = res[:, t, n * CW:(n + 1) * CW]
                    v.tensor_tensor(at, at, acc[n % 2][t][:, :], ALU.add).then_inc(x1_done, 1)

        @block.gpsimd
        def _(pool):
            g = nc.gpsimd

            def link(ins):
                pool_link.inc(ins)
                pool.wait_ge(pool_link.sem, pool_link.value())

            link(g.memset(ident, 0.0))
            link(g.affine_select(out=ident, in_=ident, compare_op=ALU.not_equal, fill=1.0, base=0,
                                 pattern=[[-1, P]], channel_multiplier=1))
            g.memset(ones, 1.0).then_inc(pool_const, 1)
            link(g.iota(pint.bitcast(I32), pattern=[[0, 1]], base=0, channel_multiplier=1))
            link(g.iota(iot[:, 0:T].bitcast(I32), pattern=[[1, T]], base=0, channel_multiplier=0))
            link(g.tensor_copy(steps, iot[:, 0:T].bitcast(I32)))
            link(g.iota(iot[:, T:2 * T].bitcast(I32), pattern=[[-1, T]], base=P, channel_multiplier=1))
            link(g.iota(iot[:, 2 * T:2 * T + P].bitcast(I32), pattern=[[-1, P]], base=0, channel_multiplier=1))
            link(g.tensor_copy(dist, iot[:, T:2 * T + P].bitcast(I32)))
            link(g.memset(mask, 0.0))
            link(g.memset(upto, 1.0))
            for o, w, base in ((0, T, P), (T, P, 0)):
                for m, fill in ((dist, FAR), (mask, -FAR)):
                    link(g.affine_select(out=m[:, o:o + w], in_=m[:, o:o + w], compare_op=ALU.is_ge, fill=fill,
                                         base=base, pattern=[[-1, w]], channel_multiplier=1))
            g.affine_select(out=upto, in_=upto, compare_op=ALU.is_ge, fill=0.0,
                            base=0, pattern=[[1, P]], channel_multiplier=-1).then_inc(pool_const, 1)
            pool.wait_ge(ssq_done, 2)
            pool.wait_ge(slopes, 1)
            link(g.tensor_scalar(ssq, ssq, 1.0 / D, EPS, ALU.mult, ALU.add))
            g.tensor_tensor(r_tok, ssq, expo[:, 0:2], ALU.pow).then_inc(r_done, 1)

            def angles(i, j):
                if j == 0:
                    pool.wait_ge(staged, i + 1)
                if j >= 2 or not (isinstance(i, int) and i == 0):
                    pool.wait_ge(tab_done, i * (2 * GPI) + 2 * (j - 1))
                hi, lo = cols[:, j:j + 1], cols[:, GPI + j:GPI + j + 1]
                p, q = ph
                w = ang[j % 2]
                if not (isinstance(i, int) and i * GPI + j == 0):
                    pool.wait_ge(ang_done, i * GPI + j)
                g.tensor_tensor(p, steps, hi.to_broadcast([P, T]), ALU.mult)
                link(g.tensor_tensor(q, steps, lo.to_broadcast([P, T]), ALU.mult))
                link(g.tensor_tensor(w, p, q, ALU.add))
                link(g.tensor_tensor(w, w, magic.to_broadcast([P, T]), ALU.add))
                link(g.tensor_tensor(w, w, magic.to_broadcast([P, T]), ALU.subtract))
                link(g.tensor_tensor(p, p, w, ALU.subtract))
                g.tensor_tensor(w, p, q, ALU.add).then_inc(ang_done, 1)

            def rotate_in(i, j):
                pool.wait_ge(x_read, i * GPI + (j + 1))
                m1, m2, gg = rot[j % 2]
                g.tensor_tensor(gg[:, 0, :], m1[:, 0, :], m2[:, 1, :], ALU.add)
                g.tensor_tensor(gg[:, 1, :], m1[:, 1, :], m2[:, 0, :], ALU.subtract).then_inc(g_done, 1)

            def rotate_out(i, j):
                pool.wait_ge(scan_done, i * GPI + (j + 1))
                m1, m2, gg = rot[j % 2]
                s = tab[j % 2][:, 1:2, :].to_broadcast([P, 2, T])
                link(g.tensor_tensor(m2, m1, s, ALU.mult))
                pool.wait_ge(n1_done, i * GPI + (j + 1))
                g.tensor_tensor(m1[:, 0, :], gg[:, 0, :], m2[:, 1, :], ALU.subtract)
                g.tensor_tensor(m1[:, 1, :], gg[:, 1, :], m2[:, 0, :], ALU.add).then_inc(h_done, 1)

            def qk_norm(layer, i):
                na = DA_PAIRS if layer else 0
                seg = 64 if layer == 0 else HD
                n = NT * CW // seg
                pool.wait_ge(qk_ss, i + (na + 1))
                if layer == 0 and isinstance(i, int) and i == 0:
                    pool.wait_ge(slopes, 2)
                link(g.tensor_tensor(rnn[:, 0:n], ssn[:, 0:n], expo[:, 0:n], ALU.pow))
                x = qk.rearrange("p t (s e) -> p (t s) e", e=seg)
                link(g.tensor_tensor(x, x, rnn[:, 0:n].rearrange("p (s e) -> p s e", e=1).to_broadcast([P, n, seg]), ALU.mult))
                gain = g_fox if layer else g_da
                for b in range(2):
                    for t in range(NT):
                        xx = qk[:, t, b * T:(b + 1) * T].rearrange("p (h e) -> p h e", h=2)
                        ins = g.tensor_tensor(xx, xx, gain[:, b:b + 1, :].to_broadcast([P, 2, P]), ALU.mult)
                ins.then_inc(qk_ready, 1)

            def vz_gain(layer, i):
                if layer == 0:
                    pool.wait_ge(acc_free[1], i + (FREE_DA + 2))
                    for t in range(NT):
                        z = vz[:, t, T:2 * T].rearrange("p (h e) -> p h e", h=2)
                        ins = g.tensor_tensor(z, z, g_dao.rearrange("p (a e) -> p a e", a=1).to_broadcast([P, 2, P]), ALU.mult)
                    ins.then_inc(vz_ready, 1)

            def out_norm(a, h):
                pool.wait_ge(pv_ssq, head_no(0, a, h) + 1)
                link(g.tensor_tensor(sso[:, 2 * h:2 * h + 2], sso[:, 2 * h:2 * h + 2], eps, ALU.add))
                g.tensor_tensor(rno[:, 2 * h:2 * h + 2], sso[:, 2 * h:2 * h + 2], expo[:, 0:2], ALU.pow).then_inc(pv_rn, 1)

            def step(layer, i, first):
                for s in range(2 * UNITS):
                    if layer == 0:
                        if s == 0:
                            angles(i, 0)
                            angles(i, 1)
                        for k in range(GPI):
                            if X_SLOT[k] == s:
                                rotate_in(i, k)
                                if k + 2 < GPI:
                                    angles(i, k + 2)
                            if X_SLOT[k] + 1 == s:
                                rotate_out(i, k)
                        if not first:
                            for h in range(2):
                                if PV_SLOT[h] == s:
                                    out_norm(i - 1, h)
                    if s == UNITS:
                        qk_norm(layer, i)
                vz_gain(layer, i)

            step(0, 0, True)
            with pool.Fori(1, DA_PAIRS) as i:
                pool_link.enter(i - 1, DA_POOL_LINKS)
                step(0, i, False)
            pool_link.leave(DA_PAIRS - 1)
            for h in range(2):
                out_norm(DA_PAIRS - 1, h)
            for n in range(4):
                pool.wait_ge(x1_done, 2 * (n + 1))
                for t in range(NT):
                    ins = g.tensor_copy(res[:, t, n * CW:(n + 1) * CW], x1_st[n % 2][:, t, :])
                ins.then_inc(x1_kept, 1)
            pool.wait_ge(r2_sum, 1)
            link(g.tensor_scalar(ssr, ssr, 1.0 / D, EPS, ALU.mult, ALU.add))
            g.tensor_tensor(r2_tok, ssr, expo[:, 0:2], ALU.pow).then_inc(r2_done, 1)
            step(1, 0, True)
            with pool.Fori(1, FOX_PAIRS) as i:
                pool_link.enter(i - 1, FOX_POOL_LINKS)
                step(1, i, False)
            pool_link.leave(FOX_PAIRS - 1)


_INS = ["x", "e_norm", "e_w_in", "e_w_out", "s5_lambda_re", "s5_lambda_im", "s5_log_dt", "s5_b_re", "s5_b_im",
        "s5_c_re", "s5_c_im", "s5_d", "s5_w_glu", "s5_b_glu", "da_q_norm", "da_k_norm", "da_lambda_q1",
        "da_lambda_k1", "da_lambda_q2", "da_lambda_k2", "da_out_norm", "o_norm", "o_w_in", "o_b_f", "o_w_out",
        "fox_q_norm", "fox_k_norm"]


def kernel(**inputs):
    import numpy as _np
    import concourse.bacc as _bacc
    from concourse import mybir as _mybir
    from concourse.bass_utils import run_bass_kernel_spmd as _run

    nc = _bacc.Bacc("TRN2", target_bir_lowering=False, num_devices=1)
    arrays, args = {}, {}
    for name in _INS:
        a = _np.ascontiguousarray(inputs[name])
        arrays[f"in_{name}"] = a
        args[name] = nc.dram_tensor(f"in_{name}", a.shape, _mybir.dt.from_np(a.dtype), kind="ExternalInput").ap()
    out = nc.dram_tensor("out_dram", (1, T, D), F32, kind="ExternalOutput").ap()
    build(nc, args, out)
    r = _run(nc, [arrays], core_ids=[0])
    return r.results[0]["out_dram"]
```

```python
from contextlib import ExitStack
import math

import numpy as np

import concourse.bass as bass
from concourse import mybir

F32 = mybir.dt.float32
F32R = mybir.dt.float32r
I32 = mybir.dt.int32
ALU = mybir.AluOpType
ACT = mybir.ActivationFunctionType
AX = mybir.AxisListType

P = 128
T = 256
NT = T // P
D = 2048
KT = D // P
CW = 512
UK = 2
UNITS = KT // UK
RING = 4
LEAD = 3
S5W = 1024
CT = S5W // P
GP = 32
GPI = 8
DA_PAIRS = 4
FOX_PAIRS = 8
HD = 128
EPS = 1e-6
FAR = 1e30
MAGIC = 1.5 * 2.0 ** 23

TWO_PI = 2.0 * math.pi
PI_A = 6.28125
PI_B = float(np.float32(round((TWO_PI - PI_A) * 2.0 ** 17) / 2.0 ** 17))
PI_C = float(np.float32(TWO_PI - PI_A - PI_B))
SIN_SCALE = 6.283185

CH_S5 = 0
CH_DA = CH_S5 + 4
CH_GLU = CH_DA + 2 * DA_PAIRS
CH_OUT0 = CH_GLU + 1
CH_FOX = CH_OUT0 + D // CW
CH_OUT1 = CH_FOX + 2 * FOX_PAIRS
CH_END = CH_OUT1 + D // CW
FREE_DA = 2
FREE_FOX = FREE_DA + DA_PAIRS
FREE_OUT1 = FREE_FOX + FOX_PAIRS
LAMBDA_INIT = 0.8 - 0.6 * math.exp(-0.3 * 0)
DA_LINKS, FOX_LINKS, DA_POOL_LINKS, FOX_POOL_LINKS = 47, 8, 19, 1

X_SLOT = [2 * g for g in range(GPI)]
Y_SLOT = [2 * g + 3 for g in range(GPI)]
QKT_SLOT = [0, 1]
SC_SLOT = {0: [2, 3, 4, 5], 1: [2, 4]}
PT_SLOT = [8, 9]
PV_SLOT = [10, 11]
YT_SLOT = [13, 14]
BEFORE_GLU = (0, 1)
WITH_GLU = {0: (2, 3), 1: (4,), 2: (5,), 3: (6, 7), 4: (8,), 5: (9,), 6: (10,), 7: (11,)}
AFTER_GLU = {0: (12, 13), 1: (14,)}


class Count:

    def __init__(self, sem):
        self.sem, self.base, self.local, self.it, self.per = sem, 0, 0, None, 0

    def enter(self, it, per):
        self.it, self.per, self.local = it, per, 0

    def leave(self, trips):
        assert self.local == self.per, (self.local, self.per)
        self.base += self.per * trips
        self.it, self.local = None, 0

    def inc(self, ins):
        ins.then_inc(self.sem, 1)
        if self.it is None:
            self.base += 1
        else:
            self.local += 1
        return ins

    def value(self):
        return self.base if self.it is None else self.it * self.per + (self.base + self.local)


def build(nc, d, out_dram):
    ctx = ExitStack()
    with ctx:
        def sb(name, shape, dt=F32):
            return ctx.enter_context(nc.sbuf_tensor(name, shape, dt))

        def sem(name):
            return ctx.enter_context(nc.semaphore(name))

        raw = sb("raw", [P, RING, UK * CW])
        wh = sb("wh", [P, RING, UK * CW], F32R)
        wl = sb("wl", [P, RING, UK * CW], F32R)
        xh = sb("xh", [P, KT, T], F32R)
        xl = sb("xl", [P, KT, T], F32R)
        yh = sb("yh", [P, KT, T], F32R)
        yl = sb("yl", [P, KT, T], F32R)
        res = sb("res", [P, NT, D])
        uz = sb("uz", [P, KT, T])
        scr = sb("scr", [P, 12864])
        con = sb("con", [P, 2880])

        used = {"scr": 0, "con": 0}

        def carve(name, *shape, parts=P):
            buf = scr if name == "scr" else con
            n = int(np.prod(shape))
            at = used[name]
            used[name] += n
            assert used[name] <= (12864 if name == "scr" else 2880), (name, used[name])
            v = buf[0:parts, at:at + n]
            if len(shape) == 2:
                v = v.rearrange("p (a b) -> p a b", a=shape[0])
            if len(shape) == 3:
                v = v.rearrange("p (a b c) -> p a b c", a=shape[0], b=shape[1])
            return v

        ident = carve("con", P)
        ones = carve("con", P)
        upto = carve("con", P)
        dist = carve("con", 3 * P)
        mask = carve("con", 3 * P)
        steps = carve("con", T)
        rbc = carve("con", T)
        colp = carve("con", 53)
        lamv = carve("con", 4, 64)
        small = carve("con", 256)
        e_col, o_col, d_col, bg_col = colp[:, 0:16], colp[:, 16:32], colp[:, 32:40], colp[:, 40:48]
        g_qk = (colp[:, 48:50], colp[:, 50:52])
        g_dao = colp[:, 52:53]

        def small_at(a, n):
            return small[:, a:a + n]

        ssq = small_at(0, 2)
        r_tok = small_at(2, 2)
        expo = small_at(4, 16)
        par = small_at(20, 2)
        nlam = small_at(22, 1)
        lt = small_at(23, 4)
        slope = small_at(27, 2)
        bf = small_at(29, 16)
        ss1 = small_at(45, 8).rearrange("p (t n) -> p t n", t=2)
        nmax = small_at(53, 8)
        lsum = small_at(61, 8)
        rec = small_at(69, 8)
        sso = small_at(77, 4)
        rno = small_at(81, 4)
        ssn = small_at(85, 16)
        rnn = small_at(101, 16)
        cq = small_at(117, 4)
        mag_st = small_at(121, GPI)
        r2_tok = small_at(145, 2)
        junk1 = small_at(160, 5)
        pint = small_at(150, 1)
        ssr = small_at(152, 2)
        half_pi = small_at(154, 1)
        eps = small_at(156, 2)

        qk = carve("scr", NT, CW)
        vz = carve("scr", NT, CW)
        sq = carve("scr", CW)
        qkt = carve("scr", 2, 2, T)
        s_sb = carve("scr", 4, 3 * P)
        p_t = carve("scr", 2, 3 * P)
        y_o = qkt.rearrange("p h b (t e) -> p h (b t) e", t=NT)[:, :, 0:NT, :]
        main0 = used["scr"]
        rot = [[carve("scr", 2, T) for _ in range(3)] for _ in range(2)]
        tab = [carve("scr", 2, T) for _ in range(2)]
        ang = [carve("scr", T) for _ in range(2)]
        ph = [carve("scr", T) for _ in range(2)]
        lb_st = carve("scr", 2, 2, P)
        cd_st = carve("scr", 2, 2, P)
        u_st = carve("scr", 2, T)
        main1 = used["scr"]
        used["scr"] = main0
        x1_st = [carve("scr", NT, CW) for _ in range(2)]
        wf = carve("scr", KT, 16)
        f_sb = carve("scr", T, parts=32)
        nct = carve("scr", T, parts=16)
        nck = carve("scr", 2, T, parts=16)
        c_sb = carve("scr", NT, 16)
        ls = carve("scr", NT, 16)
        lsa = carve("scr", NT, 16)
        used["scr"] = main0
        glu_s = carve("scr", CT, T)
        used["scr"] = 0
        rows = carve("scr", P, parts=53)
        lamr_r = carve("scr", P, parts=GP)
        lami_r = carve("scr", P, parts=GP)
        ldt_r = carve("scr", 2, 64, parts=GP)
        ldt_in = carve("scr", 2, parts=GP)
        b_n = carve("scr", 2, GP, 16)
        c_n = carve("scr", 2, CT, 64)
        bt = [carve("scr", GP, 16) for _ in range(4)]
        bd = carve("scr", 2, GP, 32)
        cb = carve("scr", CT, P)
        cb2 = carve("scr", CT, P)
        prm = [carve("scr", GP) for _ in range(20)]
        iot = carve("scr", 5 * P)
        junk = uz[:, 0:CT, :].rearrange("p a t -> p (a t)")
        used["scr"] = main1
        phc = carve("scr", 4, GP + 2)
        wf2 = sb("wf2", [P, KT, 32], F32R)
        phr = sb("phr", [P, GP], F32R)
        ph_hi, ph_lo, mag_all, ph_all = (phc[:, k, 0:GP] for k in range(4))

        lb = res[:, 0, :].rearrange("p (c r s) -> p c r s", c=CT, r=2)
        cd = res[:, 1, :].rearrange("p (r c s) -> p r c s", r=2, c=CT)

        bank = [ctx.enter_context(nc.psum_tensor(f"bank{i}", [P, CW], F32)) for i in range(8)]
        acc = [bank[0:2], bank[2:4]]
        trb, scb, xb, yb = bank[4], bank[5], bank[6], bank[7]

        raw_in = [sem(f"raw_in{i}") for i in range(RING)]
        hi_done = sem("hi_done")
        lo_done = sem("lo_done")
        unit_used = sem("unit_used")
        acc_free = [sem("acc_free0"), sem("acc_free1")]
        x_in = [sem(f"x_in{k}") for k in range(4)]
        rows_in, par_in, bc_in, s5_in, wf_in, res_in = (sem(n) for n in
            ("rows_in", "par_in", "bc_in", "s5_in", "wf_in", "res_in"))
        out_done = sem("out_done")
        pool_const, tile_ps, tile_hi, tile_lo = (sem(n) for n in
            ("pool_const", "tile_ps", "tile_hi", "tile_lo"))
        ssq_done, r_done, diag_done, rbc_ps, rbc_done = (sem(n) for n in
            ("ssq_done", "r_done", "diag_done", "rbc_ps", "rbc_done"))
        prm_rows, prm_ps, prm_ld, prm_exp, prm_ang, prm_trig, bd_done, cb_done = (sem(n) for n in
            ("prm_rows", "prm_ps", "prm_ld", "prm_exp", "prm_ang", "prm_trig", "bd_done", "cb_done"))
        mat_ps, mat_sb, prm_done = (sem(n) for n in ("mat_ps", "mat_sb", "prm_done"))
        staged, staged_c, slopes = sem("staged"), sem("staged_c"), sem("slopes")
        ang_done, tab_done, x_ps, x_read, g_done, scan_done, h_done, y_ps, y_read = (
            sem(n) for n in ("ang_done", "tab_done", "x_ps", "x_read", "g_done", "scan_done",
                             "h_done", "y_ps", "y_read"))
        gelu_done, s5_hi, s5_lo = sem("gelu_done"), sem("s5_hi"), sem("s5_lo")
        qk_ss, qk_ready = sem("qk_ss"), sem("qk_ready")
        qkt_ps, qkt_sb, sc_ps, sc_max, p_exp, p_ready, pt_ps, pt_sb = (sem(n) for n in
            ("qkt_ps", "qkt_sb", "sc_ps", "sc_max", "p_exp", "p_ready", "pt_ps", "pt_sb"))
        pv_ps, pv_ssq, pv_rn, y_ready, yt_ps, yt_hi, yt_lo = (sem(n) for n in
            ("pv_ps", "pv_ssq", "pv_rn", "y_ready", "yt_ps", "yt_hi", "yt_lo"))
        fox_b, fox_cq = sem("fox_b"), sem("fox_cq")
        glu_sig, glu_y0, glu_y, glu_hi, glu_lo, silu_done = (sem(n) for n in
            ("glu_sig", "glu_y0", "glu_y", "glu_hi", "glu_lo", "silu_done"))
        x1_done, x1_kept, x1_ps, x1_hi, x1_lo, x1_ssq, r2_done, r2_sum = (sem(n) for n in
            ("x1_done", "x1_kept", "x1_ps", "x1_hi", "x1_lo", "x1_ssq", "r2_done", "r2_sum"))
        f_sbuf, f_tps = sem("f_sbuf"), sem("f_tps")
        wf_hi, wf_lo, f_ps, f_z, f_abs, f_exp1, f_ln, f_ls, c_ps, c_done = (sem(n) for n in
            ("wf_hi", "wf_lo", "f_ps", "f_z", "f_abs", "f_exp1", "f_ln", "f_ls", "c_ps", "c_done"))
        dve_link, act_link, pool_link = (Count(sem(n)) for n in ("dve_link", "act_link", "pool_link"))
        lambda_done = sem("lambda_done")

        def head_no(layer, a, h):
            return 2 * a + h + (2 * DA_PAIRS if layer else 0)

        def score_no(layer, a, k):
            return (4 * DA_PAIRS + 2 * a if layer else 4 * a) + k

        def place(eng, at):
            return at if isinstance(at, int) else eng.snap(at)

        def unit_rows(w, kt0, n=UK):
            return w.rearrange("(k p) n -> p k n", p=P)[:, kt0:kt0 + n, :]

        block = ctx.enter_context(nc.Block())

        @block.sync
        def _(sp):
            def load(c, j, src):
                dst = raw[:, j % RING, :]
                if len(src.shape) == 3:
                    sp.dma_start(dst.rearrange("p (k n) -> p k n", k=src.shape[1]), src).then_inc(raw_in[j % RING], 32)
                else:
                    dst = dst.rearrange("p (k b n) -> p k b n", k=UK, b=2)
                    for k in range(UK):
                        sp.dma_start(dst[:, k, :, :], src[:, k, :, :]).then_inc(raw_in[j % RING], 16)

            def chunk(c, cols, rot_kt=0):
                for j in range(UNITS):
                    src = cols(j)
                    if isinstance(c, int):
                        if UNITS * c + j >= RING:
                            sp.wait_ge(lo_done, UNITS * c + j - RING + 1)
                    load(c, j, src)

            w_e, w_eo, w_o, w_oo, w_g = d["e_w_in"][0], d["e_w_out"][0], d["o_w_in"][0], d["o_w_out"][0], d["s5_w_glu"][0]
            for k in range(4):
                sp.dma_start(res[:, :, k * CW:(k + 1) * CW], d["x"][0].rearrange("(t p) n -> p t n", p=P)[:, :, k * CW:(k + 1) * CW])\
                    .then_inc(x_in[k], 16)
            for c in range(4):
                chunk(CH_S5 + c, lambda j: unit_rows(w_e, UK * j)[:, :, CW * c:CW * (c + 1)])

            def pair_cols(w, base, width, j, at):
                v = unit_rows(w, UK * j)[:, :, base:base + 2 * width]
                return v.rearrange("p k (b s) -> p k b s", b=2)[:, :, :, bass.ds(at, 2 * HD)]

            def steps_of(w, base, width, ch, trips):
                for c in (0, 1):
                    chunk(ch + c, lambda j: pair_cols(w, base + 2 * width * c, width, j, 0))
                with sp.Fori(1, trips) as i:
                    at = sp.snap(i * (2 * HD))
                    for c in (0, 1):
                        for j in range(UNITS):
                            need = sp.snap(i * (2 * UNITS) + (UNITS * (ch + c) + j - RING + 1))
                            sp.wait_ge(lo_done, need)
                            load(None, j, pair_cols(w, base + 2 * width * c, width, j, at))

            steps_of(w_e, 2 * S5W, S5W, CH_DA, DA_PAIRS)
            chunk(CH_GLU, lambda j: w_g.rearrange("(k p) n -> p k n", p=P)[:, j:j + 1, :])
            sp.wait_ge(staged, DA_PAIRS)
            sp.wait_ge(staged_c, DA_PAIRS)
            sp.dma_start(res[:, :, :], d["x"][0].rearrange("(t p) n -> p t n", p=P)).then_inc(res_in, 16)
            for c in range(4):
                chunk(CH_OUT0 + c, lambda j: unit_rows(w_eo, (8 + UK * j) % KT)[:, :, CW * c:CW * (c + 1)])
            steps_of(w_o, 0, D, CH_FOX, FOX_PAIRS)
            for c in range(4):
                chunk(CH_OUT1 + c, lambda j: unit_rows(w_oo, UK * j)[:, :, CW * c:CW * (c + 1)])
            sp.wait_ge(out_done, 16 * 4)

        @block.tensor
        def _(pe):
            def unit_ready(c, j):
                pe.wait_ge(lo_done, (c * UNITS) + (j + 1))

            def rows_unit(c, j, left, kts, pair):
                lh, ll = left
                unit_ready(c, j)
                for a, kt in enumerate(kts):
                    w_hi, w_lo = wh[:, j % RING, a * CW:(a + 1) * CW], wl[:, j % RING, a * CW:(a + 1) * CW]
                    first, last = j == 0 and a == 0, j == UNITS - 1 and a == UK - 1
                    for t in range(NT):
                        o = acc[pair][t][:, :]
                        l_hi, l_lo = lh[:, kt, t * P:(t + 1) * P], ll[:, kt, t * P:(t + 1) * P]
                        nc.tensor.matmul(o, l_hi, w_hi, start=first, stop=False)
                        nc.tensor.matmul(o, l_hi, w_lo, start=False, stop=False)
                        mm = nc.tensor.matmul(o, l_lo, w_hi, start=False, stop=last)
                mm.then_inc(unit_used, 1)

            def cols_unit(c, j, right, kt_of, banks, nk, width):
                rh, rl = right
                unit_ready(c, j)
                for a in range(nk):
                    kt = kt_of(a)
                    first, last = j == 0 and a == 0, j == UNITS - 1 and a == nk - 1
                    for n in range(width // P):
                        o = banks[n // 2][:, (n % 2) * T:(n % 2 + 1) * T]
                        at = a * width + n * P
                        w_hi, w_lo = wh[:, j % RING, at:at + P], wl[:, j % RING, at:at + P]
                        nc.tensor.matmul(o, w_hi, rh[:, kt, :], start=first and n % 2 == 0, stop=False, skip_group_check=True)
                        nc.tensor.matmul(o, w_hi, rl[:, kt, :], start=False, stop=False, skip_group_check=True)
                        mm = nc.tensor.matmul(o, w_lo, rh[:, kt, :], start=False, stop=last, skip_group_check=True)
                mm.then_inc(unit_used, 1)

            def chunk_start(pair, free):
                pe.wait_ge(acc_free[pair], free + 1)

            def qk_turn(layer, a, h):
                if h == 0:
                    pe.wait_ge(qk_ready, 2 * a + 2 + 2 * (DA_PAIRS if layer else 0))
                n = head_no(layer, a, h)
                if h:
                    pe.wait_ge(qkt_sb, n)
                else:
                    pe.wait_ge(yt_lo, n + 1)
                for b in range(2):
                    for t in range(NT):
                        at = b * T + h * HD
                        mm = nc.tensor.transpose(trb[:, b * T + t * P:b * T + (t + 1) * P],
                                                 qk[:, t, at:at + HD], ident)
                mm.then_inc(qkt_ps, 1)

            def scores(layer, a, h, comp):
                k = (2 * h + comp) if layer == 0 else h
                n = score_no(layer, a, k)
                if comp == 0:
                    pe.wait_ge(qkt_sb, head_no(layer, a, h) + 1)
                if k:
                    pe.wait_ge(sc_max, n)
                else:
                    pe.wait_ge(y_ready, head_no(layer, a, 0) + 1)
                lo, hi = (64 * comp, 64 * comp + 64) if layer == 0 else (0, P)
                if layer:
                    pe.wait_ge(fox_b, n - 4 * DA_PAIRS + 1)
                for o, t, w in ((0, 1, T), (T, 0, P)):
                    mm = nc.tensor.matmul(scb[:, o:o + w], qkt[lo:hi, h, 0, t * P:(t + 1) * P],
                                          qkt[lo:hi, h, 1, 0:w], start=True, stop=layer == 0)
                    if layer:
                        mm = nc.tensor.matmul(scb[:, o:o + w], ones[0:16, :], nck[:, h, 0:w],
                                              start=False, stop=True)
                mm.then_inc(sc_ps, 1)

            def p_turn(layer, a, h):
                n = head_no(layer, a, h)
                pe.wait_ge(p_ready, n + 1)
                if h == 0:
                    pe.wait_ge(qkt_sb, head_no(layer, a, 1) + 1)
                else:
                    pe.wait_ge(pt_sb, n)
                for b in range(3):
                    mm = nc.tensor.transpose(trb[:, b * P:(b + 1) * P],
                                             s_sb[:, 2 * h, b * P:(b + 1) * P], ident)
                mm.then_inc(pt_ps, 1)

            def values(layer, a, h):
                n = head_no(layer, a, h)
                pe.wait_ge(pt_sb, n + 1)
                if h == 0:
                    pe.wait_ge(acc_free[1], a + ((FREE_FOX if layer else FREE_DA) + 2))
                    pe.wait_ge(sc_max, score_no(layer, a, 3 if layer == 0 else 1) + 1)
                else:
                    pe.wait_ge(y_ready, n + 1)
                v = [vz[:, t, h * HD:(h + 1) * HD] for t in range(NT)]
                nc.tensor.matmul(scb[:, 0:P], p_t[:, h, 2 * P:3 * P], v[0], start=True, stop=True)
                nc.tensor.matmul(scb[:, P:2 * P], p_t[:, h, 0:P], v[0], start=True, stop=False)
                nc.tensor.matmul(scb[:, P:2 * P], p_t[:, h, P:2 * P], v[1], start=False, stop=True)\
                    .then_inc(pv_ps, 1)

            def y_turn(layer, a, h):
                n = head_no(layer, a, h)
                pe.wait_ge(y_ready, n + 2)
                if h == 0:
                    pe.wait_ge(pt_sb, head_no(layer, a, 1) + 1)
                else:
                    pe.wait_ge(yt_lo, n + 1)
                for t in range(NT):
                    mm = nc.tensor.transpose(trb[:, t * P:(t + 1) * P], y_o[:, h, t, :], ident)
                mm.then_inc(yt_ps, 1)

            def attention(layer, a, s):
                for h in range(2):
                    if QKT_SLOT[h] == s:
                        qk_turn(layer, a, h)
                for k, at in enumerate(SC_SLOT[layer]):
                    if at == s:
                        scores(layer, a, *((k // 2, k % 2) if layer == 0 else (k, 0)))
                for h in range(2):
                    if PT_SLOT[h] == s:
                        p_turn(layer, a, h)
                    if PV_SLOT[h] == s:
                        values(layer, a, h)
                    if YT_SLOT[h] == s:
                        y_turn(layer, a, h)

            def s5_in_x(i, j):
                c, q = j // 4, j % 4
                if j == 0:
                    pe.wait_ge(staged, i + 1)
                if not (isinstance(i, int) and i == 0 and j == 0):
                    pe.wait_ge(x_read, i * GPI + j)
                for r in range(2):
                    mm = nc.tensor.matmul(xb[:, r * T:(r + 1) * T], lb_st[32 * q:32 * q + 32, c, r, :],
                                          u_st[32 * q:32 * q + 32, c, :], start=True, stop=True)
                mm.then_inc(x_ps, 1)

            def s5_out_y(i, j):
                c, q = j // 4, j % 4
                pe.wait_ge(h_done, i * GPI + (j + 1))
                if j == 0:
                    pe.wait_ge(staged_c, i + 1)
                if j == 0 and not (isinstance(i, int) and i == 0):
                    pe.wait_ge(y_read, i)
                for r in range(2):
                    mm = nc.tensor.matmul(yb[32 * q:32 * q + 32, c * T:(c + 1) * T],
                                          cd_st[:, r, c, 32 * q:32 * q + 32], rot[j % 2][0][:, r, :],
                                          start=r == 0, stop=r == 1)
                mm.then_inc(y_ps, 1)

            pe.wait_ge(pool_const, 1)
            pe.wait_ge(rows_in, 16 * 9)
            nc.tensor.transpose(xb[:, 0:53], rows, ident[0:53, 0:53]).then_inc(prm_ps, 1)
            for b in range(KT // 2):
                if b % 2 == 0:
                    pe.wait_ge(x_in[b // 2], 16)
                if b >= 2:
                    pe.wait_ge(tile_lo, 2 * (b - 1))
                for e in range(2):
                    for t in range(NT):
                        kt = 2 * b + e
                        mm = nc.tensor.transpose(bank[4 + b % 2][:, e * T + t * P:e * T + (t + 1) * P],
                                                 res[:, t, kt * P:(kt + 1) * P], ident)
                mm.then_inc(tile_ps, 1)

            def s5_matrix(m):
                if m >= 2:
                    pe.wait_ge(mat_sb, m - 1)
                if m == 0:
                    pe.wait_ge(bd_done, 1)
                if m == 8:
                    pe.wait_ge(cb_done, 2)
                for r in range(2):
                    src = bd[:, r, 4 * m:4 * m + 4, :].rearrange("p a b -> p (a b)") if m < 8 else (cb, cb2)[r][:, m - 8, :]
                    mm = nc.tensor.transpose(bank[4 + m % 2][:, r * P:(r + 1) * P], src, ident)
                mm.then_inc(mat_ps, 1)

            pe.wait_ge(par_in, 16 * 4)
            pe.wait_ge(prm_ld, 1)
            nc.tensor.transpose(xb[:, 64:96], lamr_r, ident[0:GP, 0:GP])
            nc.tensor.transpose(xb[:, 96:128], lami_r, ident[0:GP, 0:GP])
            pe.wait_ge(prm_rows, 1)
            nc.tensor.transpose(xb[:, 128:160], ldt_r.rearrange("p a b -> p (a b)"), ident[0:GP, 0:GP])\
                .then_inc(prm_ps, 1)

            for c in range(4):
                chunk_start(c % 2, c // 2)
                for j in range(UNITS):
                    if c == 0:
                        pe.wait_ge(tile_lo, UK * (j + 1))
                    cols_unit(CH_S5 + c, j, (xh, xl), lambda a: UK * j + a, acc[c % 2], UK, CW)
                    if c == 0 and j == 5:
                        pe.wait_ge(diag_done, 1)
                        nc.tensor.matmul(yb[:, 0:T], ones, rbc, start=True, stop=True).then_inc(rbc_ps, 1)
                    if c == 2:
                        s5_matrix(2 * j)
                        s5_matrix(2 * j + 1)

            def step(layer, i, ch, use, first, side=None):
                for c in range(2):
                    chunk_start(c, i + use)
                    for j in range(UNITS):
                        s = c * UNITS + j
                        rows_unit(2 * i + (ch + c), j, (xh, xl), (UK * j, UK * j + 1), c)
                        if layer == 0:
                            for g in range(GPI):
                                if X_SLOT[g] == s:
                                    s5_in_x(i, g)
                                if Y_SLOT[g] == s:
                                    s5_out_y(i, g)
                            if not first and Y_SLOT[GPI - 1] - 2 * UNITS == s:
                                s5_out_y(i - 1, GPI - 1)
                        if not first:
                            attention(layer, i - 1, s)
                        if side:
                            side(s)

            step(0, 0, CH_DA, FREE_DA, True)
            with pe.Fori(1, DA_PAIRS) as i:
                step(0, i, CH_DA, FREE_DA, False)

            glu_banks = [acc[0][0], acc[0][1], acc[1][0], acc[1][1]]
            s5_out_y(DA_PAIRS - 1, GPI - 1)
            for s in BEFORE_GLU:
                attention(0, DA_PAIRS - 1, s)
            pe.wait_ge(s5_lo, 2 * DA_PAIRS - 2)
            chunk_start(0, FREE_FOX)
            chunk_start(1, FREE_FOX)
            for j in range(UNITS):
                if j == UNITS - 2:
                    pe.wait_ge(s5_lo, 2 * DA_PAIRS)
                cols_unit(CH_GLU, j, (yh, yl), lambda a: j, glu_banks, 1, S5W)
                for s in WITH_GLU[j]:
                    attention(0, DA_PAIRS - 1, s)

            def x1_turn(n):
                pe.wait_ge(x1_done, 2 * (n + 1))
                if n == 0:
                    pe.wait_ge(yt_lo, 2 * DA_PAIRS + 1)
                for b in range(2):
                    o = bank[4 + 2 * (n % 2) + b]
                    if n >= 2:
                        pe.wait_ge(x1_lo, 4 * (n - 2) + 2 * b + 2)
                    for e in range(2):
                        for t in range(NT):
                            at = (2 * b + e) * P
                            mm = nc.tensor.transpose(o[:, e * T + t * P:e * T + (t + 1) * P],
                                                     x1_st[n % 2][:, t, at:at + P], ident)
                    mm.then_inc(x1_ps, 1)

            for n in range(4):
                if n < 2:
                    pe.wait_ge(glu_sig, 4 * n + 4)
                else:
                    pe.wait_ge(x1_done, 2 * (n - 1))
                for j in range(UNITS):
                    if n == 0 and j == 0:
                        pe.wait_ge(yt_lo, 2 * DA_PAIRS - 1)
                    if n == 0 and j == 3:
                        pe.wait_ge(yt_lo, 2 * DA_PAIRS + 1)
                    if n == 0 and j >= 4:
                        pe.wait_ge(glu_lo, UK * (j - 4) + 2)
                    kt = (8 + UK * j) % KT
                    rows_unit(CH_OUT0 + n, j, (yh, yl), (kt, kt + 1), n % 2)
                    if n == 0:
                        for s in AFTER_GLU.get(j, ()):
                            attention(0, DA_PAIRS - 1, s)
                    if n and j == 2:
                        x1_turn(n - 1)

            def fox_gates():
                pe.wait_ge(wf_lo, 1)
                for kt in range(KT):
                    for x, first, last in ((xh, kt == 0, False), (xl, False, kt == KT - 1)):
                        mm = nc.tensor.matmul(yb[0:32, 0:T], wf2[:, kt, :], x[:, kt, :], start=first, stop=last)
                mm.then_inc(f_ps, 1)

            def fox_turn():
                pe.wait_ge(f_sbuf, 1)
                for t in range(NT):
                    mm = nc.tensor.transpose(yb[:, 400 + 32 * t:432 + 32 * t], f_sb[:, t * P:(t + 1) * P], ident[0:32, 0:32])
                mm.then_inc(f_tps, 1)

            def fox_sums():
                pe.wait_ge(f_ls, 1)
                nc.tensor.matmul(yb[:, 64:80], upto, ls[:, 0, :], start=True, stop=True)
                nc.tensor.matmul(yb[:, 80:96], ones, ls[:, 0, :], start=True, stop=False)
                nc.tensor.matmul(yb[:, 80:96], upto, ls[:, 1, :], start=False, stop=True)
                nc.tensor.matmul(yb[0:16, 128:256], ls[:, 0, :], upto, start=True, stop=True)
                nc.tensor.matmul(yb[0:16, 256:384], ls[:, 0, :], ones, start=True, stop=False)
                nc.tensor.matmul(yb[0:16, 256:384], ls[:, 1, :], upto, start=False, stop=True)\
                    .then_inc(c_ps, 1)

            def side(s):
                if s == 0:
                    x1_turn(3)
                if s == 5:
                    pe.wait_ge(x1_lo, KT)
                if s == 8:
                    fox_gates()
                if s == 9:
                    fox_turn()
                if s == 13:
                    fox_sums()

            pe.wait_ge(x1_lo, 12)
            def fox_first():
                for c in range(2):
                    pe.wait_ge(x1_done, 6 + 2 * c)
                    for j in range(UNITS):
                        s = c * UNITS + j
                        if s == 6:
                            pe.wait_ge(x1_lo, KT)
                        rows_unit(CH_FOX + c, j, (xh, xl), (UK * j, UK * j + 1), c)
                        side(s)

            fox_first()
            with pe.Fori(1, FOX_PAIRS) as i:
                step(1, i, CH_FOX, FREE_FOX, False)

            for n in range(4):
                if n < 2:
                    chunk_start(n, FREE_OUT1)
                else:
                    pe.wait_ge(x1_done, 8 + 2 * (n - 1))
                for j in range(UNITS):
                    if n == 0 and j == 0:
                        pe.wait_ge(yt_lo, 2 * (DA_PAIRS + FOX_PAIRS) - 1)
                    if n == 0 and j == UNITS - 1:
                        pe.wait_ge(yt_lo, 2 * (DA_PAIRS + FOX_PAIRS) + 1)
                    rows_unit(CH_OUT1 + n, j, (yh, yl), (UK * j, UK * j + 1), n % 2)
                    if n == 0:
                        for s in ({0: [0, 1, 2], 1: [4], 2: [8], 3: [9, 10], 4: [11], 5: [13], 6: [14]}).get(j, []):
                            attention(1, FOX_PAIRS - 1, s)

        def split_hi(act, c, j):
            if j >= UNITS:
                c, j = c + 1, j - UNITS
            act.wait_ge(raw_in[j % RING], c * 64 + (32 * (j // RING) + 32))
            act.wait_ge(unit_used, c * UNITS + (j - RING + 2)) if not (isinstance(c, int) and c * UNITS + j < RING) else None
            nc.scalar.activation(wh[:, j % RING, :], raw[:, j % RING, :], ACT.Copy).then_inc(hi_done, 1)

        def split_lo(dve, c, j):
            if j >= UNITS:
                c, j = c + 1, j - UNITS
            dve.wait_ge(hi_done, c * UNITS + (j + 1))
            nc.vector.tensor_tensor(wl[:, j % RING, :], raw[:, j % RING, :],
                                    wh[:, j % RING, :].bitcast(F32), ALU.subtract).then_inc(lo_done, 1)

        @block.scalar
        def _(act):
            link = act_link.inc

            def bc(src, n):
                return src.rearrange("(a n) -> a n", a=1).to_broadcast([P, n])

            for at, name, n in ((0, "e_norm", 16), (16, "o_norm", 16), (32, "s5_d", 8), (40, "s5_b_glu", 8),
                                (48, "da_q_norm", 1), (49, "da_k_norm", 1), (50, "fox_q_norm", 1),
                                (51, "fox_k_norm", 1), (52, "da_out_norm", 1)):
                act.dma_start(rows[at:at + n, :], d[name][0].rearrange("(a n) -> a n", n=P)).then_inc(rows_in, 16)
            act.dma_start(lamr_r, d["s5_lambda_re"][0].rearrange("(a b) p -> a (b p)", b=2)).then_inc(par_in, 16)
            act.dma_start(lami_r, d["s5_lambda_im"][0].rearrange("(a b) p -> a (b p)", b=2)).then_inc(par_in, 16)
            act.dma_start(ldt_in, d["s5_log_dt"][0].rearrange("(a b) -> a b", b=2)).then_inc(par_in, 16)
            act.dma_start(bf, bc(d["o_b_f"][0], 16)).then_inc(par_in, 16)
            for at, name in ((0, "s5_b_re"), (1, "s5_b_im")):
                act.dma_start(b_n[:, at, :, :], d[name][0].rearrange("(a b) p h -> (b p) a h", b=2)).then_inc(s5_in, 16)
            for at, name in ((0, "s5_c_re"), (1, "s5_c_im")):
                act.dma_start(c_n[:, at, :, :], d[name][0].rearrange("(a b) h p -> (b h) a p", b=8)).then_inc(s5_in, 16)
            for k, name in enumerate(("da_lambda_q1", "da_lambda_k1", "da_lambda_q2", "da_lambda_k2")):
                act.dma_start(lamv[:, k, :], bc(d[name][0], 64)).then_inc(bc_in, 16)

            for j in range(LEAD):
                split_hi(act, 0, j)
            act.wait_ge(prm_ps, 1)
            nc.scalar.activation(colp, xb[:, 0:53], ACT.Copy).then_inc(prm_ld, 1)
            act.wait_ge(prm_ld, 1)
            for kt in range(KT):
                if kt % 2 == 0:
                    act.wait_ge(tile_ps, kt // 2 + 1)
                nc.scalar.activation(xh[:, kt, :], bank[4 + kt // 2 % 2][:, kt % 2 * T:(kt % 2 + 1) * T],
                                     ACT.Copy, scale=e_col[:, kt:kt + 1]).then_inc(tile_hi, 1)
            for t in range(NT):
                ins = nc.scalar.activation(junk, res[:, t, :], ACT.Square, accum_out=ssq[:, t:t + 1])
                ins.then_inc(ssq_done, 1)
                act.wait_ge(ssq_done, t + 1)

            def params(c, j):
                if (c, j) == (0, 7):
                    act.wait_ge(prm_ang, 1)
                    nc.scalar.activation(prm[3], prm[2], ACT.Exp).then_inc(prm_exp, 1)
                if (c, j) == (1, 1):
                    act.wait_ge(prm_ang, 2)
                    nc.scalar.activation(mag_all, prm[4], ACT.Exp).then_inc(prm_exp, 1)
                    act.wait_ge(lambda_done, 1)
                    nc.scalar.activation(lt[:, 2:4], lt[:, 0:2], ACT.Exp).then_inc(prm_exp, 1)
                    act.wait_ge(prm_ang, 3)
                    nc.scalar.activation(prm[11], prm[10], ACT.Sin, scale=SIN_SCALE).then_inc(prm_trig, 1)
                    nc.scalar.activation(prm[13], prm[10], ACT.Abs).then_inc(prm_trig, 1)
                    act.wait_ge(prm_trig, 2)
                    nc.scalar.activation(prm[12], prm[13], ACT.Sin, scale=-SIN_SCALE, bias=half_pi).then_inc(prm_trig, 1)
                if c == 2:
                    for m in (2 * j, 2 * j + 1):
                        act.wait_ge(mat_ps, m + 1)
                        o = bank[4 + m % 2][:, 0:2 * P].rearrange("p (r s) -> p r s", r=2)
                        dst = lb[:, m, :, :] if m < 8 else cd[:, :, m - 8, :]
                        nc.scalar.activation(dst, o, ACT.Copy).then_inc(mat_sb, 1)

            for c in range(4):
                for j in range(UNITS):
                    split_hi(act, c, j + LEAD)
                    params(c, j)
            act.wait_ge(acc_free[1], FREE_DA + 1)
            nc.scalar.activation(uz[:, CT:2 * CT, :], uz[:, CT:2 * CT, :], ACT.Silu).then_inc(silu_done, 1)

            def stage(i):
                if isinstance(i, int) and i == 0:
                    act.wait_ge(mat_sb, 16)
                    act.wait_ge(prm_done, 1)
                    act.wait_ge(prm_exp, 2)
                    act.wait_ge(acc_free[1], FREE_DA)
                else:
                    act.wait_ge(x_ps, i * GPI)
                    act.wait_ge(scan_done, i * GPI)
                nc.scalar.activation(mag_st, phc[:, 2, bass.ds(place(act, i * GPI), GPI)], ACT.Copy)
                c = place(act, i * 2)
                nc.scalar.activation(lb_st, lb[:, bass.ds(c, 2), :, :], ACT.Copy)
                nc.scalar.activation(u_st, uz[:, bass.ds(c, 2), :], ACT.Copy).then_inc(staged, 1)

            def stage_c(i):
                if not (isinstance(i, int) and i == 0):
                    act.wait_ge(y_ps, i * GPI)
                nc.scalar.activation(cd_st, cd[:, :, bass.ds(place(act, i * 2), 2), :], ACT.Copy).then_inc(staged_c, 1)

            def table(n, j):
                act.wait_ge(ang_done, n + 1)
                if not (isinstance(n, int) and n < 2):
                    act.wait_ge(h_done, n - 1)
                a = ang[j % 2]
                nc.scalar.activation(tab[j % 2][:, 1, :], a, ACT.Sin, scale=SIN_SCALE).then_inc(tab_done, 1)
                link(nc.scalar.activation(a, a, ACT.Abs))
                act.wait_ge(act_link.sem, act_link.value())
                nc.scalar.activation(tab[j % 2][:, 0, :], a, ACT.Sin, scale=-SIN_SCALE, bias=half_pi).then_inc(tab_done, 1)

            def gelus(i):
                act.wait_ge(y_read, i + 1)
                for c in (1, 0):
                    at = uz[:, bass.ds(place(act, i * 2 + c), 1), :].rearrange("p a t -> p (a t)")
                    nc.scalar.activation(at, at, ACT.Gelu_apprx_tanh).then_inc(gelu_done, 1)
                for k, c in enumerate((1, 0)):
                    act.wait_ge(gelu_done, i * 2 + (k + 1))
                    at = bass.ds(place(act, i * 2 + c), 1)
                    nc.scalar.activation(yh[:, at, :], uz[:, at, :], ACT.Copy).then_inc(s5_hi, 1)

            def qk_out(layer, i):
                r = r2_tok if layer else r_tok
                na = DA_PAIRS if layer else 0
                act.wait_ge(unit_used, i * (2 * UNITS) + (UNITS * ((CH_FOX if layer else CH_DA) + 1) + 1))
                if layer and isinstance(i, int):
                    act.wait_ge(r2_done, 1)
                if not (isinstance(i, int) and i == 0 and layer == 0):
                    act.wait_ge(qkt_ps, i * 2 + 2 * na)
                nc.scalar.activation(qk[:, 0, :], acc[0][0][:, :], ACT.Copy, scale=r[:, 0:1])
                nc.scalar.activation(qk[:, 1, :], acc[0][1][:, :], ACT.Copy, scale=r[:, 1:2]).then_inc(acc_free[0], 1)

            def vz_out(layer, i):
                r = r2_tok if layer else r_tok
                na = DA_PAIRS if layer else 0
                act.wait_ge(unit_used, i * (2 * UNITS) + (UNITS * ((CH_FOX if layer else CH_DA) + 2) + 1))
                if not (isinstance(i, int) and i == 0 and layer == 0):
                    act.wait_ge(y_ready, i * 2 + (2 * na + 1))
                for t in range(NT):
                    nc.scalar.activation(vz[:, t, 0:T], acc[1][t][:, 0:T], ACT.Copy, scale=r[:, t:t + 1])
                for t in range(NT):
                    ins = nc.scalar.activation(vz[:, t, T:2 * T], acc[1][t][:, T:2 * T], ACT.Silu, scale=r[:, t:t + 1])
                ins.then_inc(acc_free[1], 1)

            def qkt_out(layer, a, h):
                act.wait_ge(qkt_ps, head_no(layer, a, h) + 1)
                for b in range(2):
                    ins = nc.scalar.activation(qkt[:, h, b, :], trb[:, b * T:(b + 1) * T], ACT.Copy,
                                               scale=g_qk[layer][:, b:b + 1])
                ins.then_inc(qkt_sb, 1)

            def exps(layer, a, k):
                s = k if layer == 0 else 2 * k
                act.wait_ge(sc_max, score_no(layer, a, k) + 1)
                for t, o, w in ((0, T, P), (1, 0, T)):
                    ins = nc.scalar.activation(s_sb[:, s, o:o + w], s_sb[:, s, o:o + w], ACT.Exp,
                                               bias=nmax[:, 2 * s + t:2 * s + t + 1],
                                               accum_out=lsum[:, 2 * s + t:2 * s + t + 1])
                ins.then_inc(p_exp if layer == 0 else p_ready, 1)

            def pt_out(layer, a, h):
                n = head_no(layer, a, h)
                act.wait_ge(pt_ps, n + 1)
                nc.scalar.activation(p_t[:, h, :], trb[:, 0:3 * P], ACT.Copy).then_inc(pt_sb, 1)

            def out_squares(a, h):
                act.wait_ge(pv_ps, head_no(0, a, h) + 1)
                for t in range(NT):
                    ins = nc.scalar.activation(y_o[:, h, t, :], scb[:, t * P:(t + 1) * P], ACT.Square, scale=HD ** -0.5,
                                               accum_out=sso[:, 2 * h + t:2 * h + t + 1])
                ins.then_inc(pv_ssq, 1)

            def yt_out(layer, a, h):
                n = head_no(layer, a, h)
                act.wait_ge(yt_ps, n + 1)
                kt = place(act, 2 * a + h + (8 if layer == 0 else 0))
                nc.scalar.activation(yh[:, bass.ds(kt, 1), :], trb[:, 0:T].rearrange("p (a t) -> p a t", a=1), ACT.Copy,
                                     scale=g_dao if layer == 0 else 1.0).then_inc(yt_hi, 1)

            def fox_cols(a, h):
                n = 2 * a + h
                if h == 0:
                    act.wait_ge(sc_max, score_no(1, a, 0))
                    act.wait_ge(c_done, 2)
                nc.scalar.activation(cq[:, 2 * h:2 * h + 2].rearrange("p (a b) -> p a b", b=1),
                                     c_sb[:, :, bass.ds(place(act, n), 1)], ACT.Copy).then_inc(fox_cq, 1)

            def attention(layer, a, s):
                for h in range(2):
                    if QKT_SLOT[h] == s:
                        qkt_out(layer, a, h)
                        if layer:
                            fox_cols(a, h)
                for k, at in enumerate(SC_SLOT[layer]):
                    if at + 1 == s:
                        exps(layer, a, k)
                for h in range(2):
                    if PT_SLOT[h] == s:
                        pt_out(layer, a, h)
                    if PV_SLOT[h] == s and layer == 0:
                        out_squares(a, h)
                    if YT_SLOT[h] == s:
                        yt_out(layer, a, h)

            def step(layer, i, ch, first, side=None):
                for c in range(2):
                    for j in range(UNITS):
                        s = c * UNITS + j
                        split_hi(act, 2 * i + (ch + c), j + LEAD)
                        if layer == 0:
                            if s == 0:
                                stage(i)
                            for g in range(GPI):
                                if X_SLOT[g] + 1 == s:
                                    table(i * GPI + (g + 1), g + 1)
                            if s == 2:
                                stage_c(i)
                            if s == 4 and not first:
                                gelus(i - 1)
                        if not first:
                            attention(layer, i - 1, s)
                        if side:
                            side(s)
                    if c == 0:
                        qk_out(layer, i)
                    else:
                        vz_out(layer, i)

            act.wait_ge(slopes, 2)
            table(0, 0)
            step(0, 0, CH_DA, True)
            with act.Fori(1, DA_PAIRS) as i:
                act_link.enter(i - 1, GPI)
                step(0, i, CH_DA, False)
            act_link.leave(DA_PAIRS - 1)

            gelus(DA_PAIRS - 1)
            for s in BEFORE_GLU:
                attention(0, DA_PAIRS - 1, s)
            for j in range(UNITS):
                split_hi(act, CH_GLU, j + LEAD)
                for s in WITH_GLU[j]:
                    attention(0, DA_PAIRS - 1, s)

            def glu_up(n):
                act.wait_ge(glu_y, n + 1)
                nc.scalar.activation(yh[:, n, :], uz[:, n, :], ACT.Copy).then_inc(glu_hi, 1)

            act.wait_ge(unit_used, UNITS * (CH_GLU + 1) + 1)
            for n in range(CT):
                nc.scalar.activation(glu_s[:, n, :], acc[n // 4][n // 2 % 2][:, n % 2 * T:(n % 2 + 1) * T],
                                     ACT.Sigmoid, bias=bg_col[:, n:n + 1]).then_inc(glu_sig, 1)

            def x1_up(n):
                for e in range(4):
                    kt = 4 * n + e
                    if e % 2 == 0:
                        act.wait_ge(x1_ps, 2 * n + e // 2 + 1)
                    nc.scalar.activation(xh[:, kt, :], bank[4 + 2 * (n % 2) + e // 2][:, e % 2 * T:(e % 2 + 1) * T],
                                         ACT.Copy, scale=o_col[:, kt:kt + 1]).then_inc(x1_hi, 1)

            def x1_keep(n):
                for t in range(NT):
                    act.wait_ge(x1_done, 2 * n + t + 1)
                    if n or t:
                        act.wait_ge(x1_ssq, 2 * n + t)
                    nc.scalar.activation(sq, x1_st[n % 2][:, t, :], ACT.Square,
                                         accum_out=ss1[:, t, n:n + 1]).then_inc(x1_ssq, 1)

            for n in range(4):
                for j in range(UNITS):
                    split_hi(act, CH_OUT0 + n, j + LEAD)
                    if n == 0:
                        for s in AFTER_GLU.get(j, ()):
                            attention(0, DA_PAIRS - 1, s)
                        if j < 4:
                            glu_up(2 * j)
                            glu_up(2 * j + 1)
                    if n and j == 2:
                        x1_up(n - 1)
                x1_keep(n)

            act.dma_start(wf, d["o_w_in"][0].rearrange("(k p) n -> p k n", p=P)[:, :, 4 * D:4 * D + 16]).then_inc(wf_in, 16)

            def side(s):
                if s == 0:
                    x1_up(3)
                if s == 2:
                    act.wait_ge(wf_in, 16)
                    nc.scalar.activation(wf2[:, :, 0:16], wf, ACT.Copy).then_inc(wf_hi, 1)
                if s == 8:
                    act.wait_ge(f_ps, 1)
                    nc.scalar.activation(f_sb, yb[0:32, 0:T], ACT.Copy).then_inc(f_sbuf, 1)
                if s == 10:
                    act.wait_ge(f_z, 1)
                    nc.scalar.activation(lsa, ls, ACT.Abs).then_inc(f_abs, 1)
                    act.wait_ge(f_abs, 1)
                    nc.scalar.activation(lsa, lsa, ACT.Exp, scale=-1.0).then_inc(f_abs, 1)
                if s == 11:
                    act.wait_ge(f_exp1, 1)
                    nc.scalar.activation(lsa, lsa, ACT.Ln).then_inc(f_ln, 1)
                if s == 13:
                    act.wait_ge(c_ps, 1)
                    nc.scalar.activation(c_sb, yb[:, 64:96].rearrange("p (a b) -> p a b", a=2), ACT.Copy).then_inc(c_done, 1)
                    nc.scalar.mul(nct, yb[0:16, 128:384], -1.0).then_inc(c_done, 1)

            step(1, 0, CH_FOX, True, side)
            with act.Fori(1, FOX_PAIRS) as i:
                step(1, i, CH_FOX, False)

            for n in range(4):
                for j in range(UNITS):
                    if UNITS * (CH_OUT1 + n) + j + LEAD < UNITS * CH_END:
                        split_hi(act, CH_OUT1 + n, j + LEAD)
                    if n == 0:
                        for s in ({0: [0, 1, 2, 3], 1: [4, 5], 2: [8], 3: [9, 10], 4: [11], 5: [13], 6: [14]}).get(j, []):
                            attention(1, FOX_PAIRS - 1, s)
                act.wait_ge(x1_done, 8 + 2 * (n + 1))
                act.dma_start(out_dram[0, :, n * CW:(n + 1) * CW].rearrange("(t p) n -> p t n", p=P),
                              res[:, :, n * CW:(n + 1) * CW]).then_inc(out_done, 16)

        @block.vector
        def _(dve):
            def link(ins):
                dve_link.inc(ins)
                dve.wait_ge(dve_link.sem, dve_link.value())

            v = nc.vector

            v.memset(half_pi, 0.5 * math.pi)
            link(v.memset(eps, EPS))
            for k, first in enumerate((yt_lo, y_ready, acc_free[0], acc_free[1], unit_used)):
                v.memset(junk1[:, k:k + 1], 0.0).then_inc(first, 1)
            v.memset(expo, -0.5).then_inc(slopes, 1)
            for j in range(LEAD):
                split_lo(dve, 0, j)
            dve.wait_ge(par_in, 16 * 4)
            v.tensor_copy(ldt_r, ldt_in.rearrange("p (a b) -> p a b", b=1).to_broadcast([GP, 2, 64])).then_inc(prm_rows, 1)
            for kt in range(KT):
                dve.wait_ge(tile_hi, 2 * (kt // 2) + 2)
                v.scalar_tensor_tensor(out=xl[:, kt, :], in0=bank[4 + kt // 2 % 2][:, kt % 2 * T:(kt % 2 + 1) * T],
                                       scalar=e_col[:, kt:kt + 1], in1=xh[:, kt, :].bitcast(F32),
                                       op0=ALU.mult, op1=ALU.subtract).then_inc(tile_lo, 1)

            def diagonal():
                dve.wait_ge(r_done, 1)
                dve.wait_ge(pool_const, 1)
                for t in range(NT):
                    ins = v.tensor_scalar(rbc[:, t * P:(t + 1) * P], ident, r_tok[:, t:t + 1], None, ALU.mult)
                ins.then_inc(diag_done, 1)

            def rbc_out():
                dve.wait_ge(rbc_ps, 1)
                v.tensor_copy(rbc, yb[:, 0:T]).then_inc(rbc_done, 1)

            lr, li, ldt, dt, lrdt, th, n, a, b, _, turn, sn, cs, ab, den, t1, t2, kr, ki, nr = prm

            def angles_ready():
                dve.wait_ge(prm_ps, 2)
                v.tensor_copy(lr, xb[:, 64:96])
                v.tensor_copy(li, xb[:, 96:128])
                v.tensor_copy(ldt, xb[:, 128:160]).then_inc(prm_ang, 1)

            def turns():
                dve.wait_ge(prm_ang, 1)
                dve.wait_ge(prm_exp, 1)
                link(v.memset(phc[:, :, GP:GP + 2], 0.0))
                v.tensor_tensor(lrdt, lr, dt, ALU.mult).then_inc(prm_ang, 1)
                link(v.tensor_tensor(th, li, dt, ALU.mult))
                link(v.tensor_scalar(n, th, 1.0 / TWO_PI, MAGIC, ALU.mult, ALU.add))
                link(v.tensor_scalar(n, n, -MAGIC, None, ALU.add))
                link(v.scalar_tensor_tensor(out=a, in0=n, scalar=-PI_A, in1=th, op0=ALU.mult, op1=ALU.add))
                link(v.scalar_tensor_tensor(out=a, in0=n, scalar=-PI_B, in1=a, op0=ALU.mult, op1=ALU.add))
                link(v.tensor_scalar(phr[:, :], a, 1.0 / TWO_PI, None, ALU.mult))
                link(v.tensor_copy(ph_hi, phr[:, :].bitcast(F32)))
                link(v.scalar_tensor_tensor(out=b, in0=ph_hi, scalar=-PI_A, in1=a, op0=ALU.mult, op1=ALU.add))
                link(v.scalar_tensor_tensor(out=b, in0=ph_hi, scalar=-PI_B, in1=b, op0=ALU.mult, op1=ALU.add))
                link(v.tensor_tensor(n, n, ph_hi, ALU.add))
                link(v.scalar_tensor_tensor(out=b, in0=n, scalar=-PI_C, in1=b, op0=ALU.mult, op1=ALU.add))
                link(v.tensor_scalar(ph_lo, b, 1.0 / TWO_PI, None, ALU.mult))
                link(v.tensor_tensor(turn, ph_hi, ph_lo, ALU.add))
                v.tensor_copy(ph_all, turn).then_inc(prm_ang, 1)

            def b_factors():
                link(v.tensor_tensor(t1, lr, lr, ALU.mult))
                link(v.tensor_tensor(t2, li, li, ALU.mult))
                link(v.tensor_tensor(den, t1, t2, ALU.add))
                link(v.reciprocal(den, den))
                dve.wait_ge(prm_exp, 2)
                dve.wait_ge(prm_trig, 3)
                mag = mag_all
                link(v.tensor_tensor(nr, mag, cs, ALU.mult))
                link(v.tensor_scalar(nr, nr, -1.0, None, ALU.add))
                link(v.tensor_tensor(sn, mag, sn, ALU.mult))
                link(v.tensor_tensor(t1, nr, lr, ALU.mult))
                link(v.tensor_tensor(t2, sn, li, ALU.mult))
                link(v.tensor_tensor(kr, t1, t2, ALU.add))
                link(v.tensor_tensor(kr, kr, den, ALU.mult))
                link(v.tensor_tensor(t1, sn, lr, ALU.mult))
                link(v.tensor_tensor(t2, nr, li, ALU.mult))
                link(v.tensor_tensor(ki, t1, t2, ALU.subtract))
                link(v.tensor_tensor(ki, ki, den, ALU.mult))
                v.memset(bd, 0.0).then_inc(prm_done, 1)

            def b_blocks():
                dve.wait_ge(s5_in, 16 * 4)

                def wide(x):
                    return x.rearrange("p (a b) -> p a b", b=1).to_broadcast([P, GP, 16])

                br, bi = b_n[:, 0, :, :], b_n[:, 1, :, :]
                v.tensor_tensor(bt[0], br, wide(kr), ALU.mult)
                v.tensor_tensor(bt[1], bi, wide(ki), ALU.mult)
                v.tensor_tensor(bt[2], bi, wide(kr), ALU.mult)
                link(v.tensor_tensor(bt[3], br, wide(ki), ALU.mult))
                dve.wait_ge(prm_done, 1)
                for g in range(2):
                    rows_ = slice(64 * g, 64 * g + 64)
                    for r, op in ((0, ALU.subtract), (1, ALU.add)):
                        ins = v.tensor_tensor(bd[rows_, r, :, 16 * g:16 * g + 16], bt[2 * r][rows_], bt[2 * r + 1][rows_], op)
                ins.then_inc(bd_done, 1)

            def c_blocks():
                dve.wait_ge(pool_const, 2)
                link(v.tensor_scalar(pint.bitcast(I32), pint.bitcast(I32), 16, None, ALU.bitwise_and))
                link(v.tensor_copy(par[:, 1:2], pint.bitcast(I32)))
                link(v.tensor_scalar(par[:, 1:2], par[:, 1:2], 1.0 / 16, None, ALU.mult))
                link(v.tensor_scalar(par[:, 0:1], par[:, 1:2], -1.0, 1.0, ALU.mult, ALU.add))
                for r, dst, sign in ((0, cb, 1.0), (1, cb2, -1.0)):
                    for g in range(2):
                        ins = v.tensor_scalar(dst[:, :, 64 * g:64 * g + 64], c_n[:, r, :, :], par[:, g:g + 1],
                                              sign, ALU.mult, ALU.mult)
                    ins.then_inc(cb_done, 1)

            def gains():
                dve.wait_ge(bc_in, 16 * 4)
                dve.wait_ge(prm_ld, 1)
                v.tensor_scalar(g_qk[0][:, 0:1], g_qk[0][:, 0:1], 64 ** -0.5, None, ALU.mult)
                v.tensor_scalar(g_qk[1][:, 0:1], g_qk[1][:, 0:1], float(HD) ** -0.5, None, ALU.mult)
                v.tensor_scalar(g_dao, g_dao, 1.0 - LAMBDA_INIT, None, ALU.mult).then_inc(slopes, 1)
                link(v.tensor_tensor(lamv[:, 0:4:2, :], lamv[:, 0:4:2, :], lamv[:, 1:4:2, :], ALU.mult))
                v.tensor_reduce(lt[:, 0:2], lamv[:, 0:4:2, :], AX.X, ALU.add).then_inc(lambda_done, 1)
                for h in range(2):
                    ins = v.memset(slope[:, h:h + 1], -(2.0 ** -(h + 1)))
                link(ins)

            def lam_end():
                dve.wait_ge(prm_exp, 3)
                link(v.tensor_tensor(nlam, lt[:, 2:3], lt[:, 3:4], ALU.subtract))
                link(v.tensor_scalar(nlam, nlam, LAMBDA_INIT, None, ALU.add))

            aside = {(0, 1): gains, (0, 3): diagonal, (0, 6): angles_ready, (1, 0): turns, (1, 3): b_factors,
                     (1, 4): b_blocks, (1, 5): c_blocks, (1, 6): lam_end}
            for c in range(4):
                for j in range(UNITS):
                    split_lo(dve, c, j + LEAD)
                    if (c, j) in aside:
                        aside[c, j]()
                if c == 0:
                    rbc_out()
                    dve.wait_ge(rbc_done, 1)
                dve.wait_ge(unit_used, UNITS * (c + 1) + 1)
                for half in range(2):
                    o = acc[c % 2][half][:, :].rearrange("p (a t) -> p a t", a=2)
                    ins = v.tensor_tensor(uz[:, 4 * c + 2 * half:4 * c + 2 * half + 2, :], o,
                                          rbc.rearrange("p (a t) -> p a t", a=1).to_broadcast([P, 2, T]), ALU.mult)
                ins.then_inc(acc_free[c % 2], 1)

            def rotate_in(i, j):
                dve.wait_ge(x_ps, i * GPI + (j + 1))
                dve.wait_ge(tab_done, i * (2 * GPI) + 2 * (j + 1))
                if j >= 2 or not (isinstance(i, int) and i == 0):
                    dve.wait_ge(y_ps, i * GPI + (j - 1))
                m1, m2, _ = rot[j % 2]
                x = xb[:, :].rearrange("p (r t) -> p r t", r=2)
                c, s = (tab[j % 2][:, k:k + 1, :].to_broadcast([P, 2, T]) for k in range(2))
                v.tensor_tensor(m1, x, c, ALU.mult)
                v.tensor_tensor(m2, x, s, ALU.mult).then_inc(x_read, 1)

            def scan(i, j):
                dve.wait_ge(g_done, i * GPI + (j + 1))
                m1, _, g = rot[j % 2]
                mag = mag_st[:, j:j + 1].to_broadcast([P, T])
                for r in range(2):
                    ins = v.tensor_tensor_scan(m1[:, r, :], mag, g[:, r, :], 0.0, ALU.mult, ALU.add)
                ins.then_inc(scan_done, 1)

            def angles(n, j):
                p_n, p_r = ph
                w = ang[j % 2]
                if not (isinstance(n, int) and n == 0):
                    dve.wait_ge(ang_done, n)
                hi, lo, whole = (phc[:, k, bass.ds(n, 1)] for k in (0, 1, 3))
                link(v.tensor_scalar(p_n, steps, whole, MAGIC, ALU.mult, ALU.add))
                link(v.tensor_scalar(p_n, p_n, -MAGIC, None, ALU.add))
                link(v.scalar_tensor_tensor(out=p_r, in0=steps, scalar=hi, in1=p_n, op0=ALU.mult, op1=ALU.subtract))
                link(v.scalar_tensor_tensor(out=p_r, in0=steps, scalar=lo, in1=p_r, op0=ALU.mult, op1=ALU.add))
                v.tensor_scalar(w, p_r, 0.5, -0.5, ALU.min, ALU.max).then_inc(ang_done, 1)

            def s5_out(i):
                dve.wait_ge(y_ps, i * GPI + GPI)
                for c in range(2):
                    u = uz[:, bass.ds(i * 2 + c, 1), :].rearrange("p a t -> p (a t)")
                    ins = v.scalar_tensor_tensor(out=u, in0=u,
                                                 scalar=d_col[:, bass.ds(i * 2 + c, 1)],
                                                 in1=yb[:, c * T:(c + 1) * T], op0=ALU.mult, op1=ALU.add)
                ins.then_inc(y_read, 1)

            def s5_low(i):
                for k, c in enumerate((1, 0)):
                    dve.wait_ge(s5_hi, i * 2 + (k + 1))
                    at = bass.ds(i * 2 + c, 1)
                    v.tensor_tensor(yl[:, at, :], uz[:, at, :], yh[:, at, :].bitcast(F32), ALU.subtract).then_inc(s5_lo, 1)

            def qk_squares(layer, i):
                na = DA_PAIRS if layer else 0
                seg = 64 if layer == 0 else HD
                dve.wait_ge(acc_free[0], i + ((FREE_FOX if layer else FREE_DA) + 2))
                n = CW // seg
                for t in range(NT):
                    link(v.tensor_tensor(sq, qk[:, t, :], qk[:, t, :], ALU.mult))
                    ins = v.tensor_reduce(ssn[:, t * n:(t + 1) * n], sq.rearrange("p (s e) -> p s e", e=seg), AX.X, ALU.add)
                    link(ins)
                n *= NT
                v.tensor_scalar(ssn[:, 0:n], ssn[:, 0:n], 1.0 / seg, EPS, ALU.mult, ALU.add).then_inc(qk_ss, 1)

            def score_in(layer, a, k):
                h = k // 2 if layer == 0 else k
                s = k if layer == 0 else 2 * k
                dve.wait_ge(sc_ps, score_no(layer, a, k) + 1)
                if layer == 0:
                    link(v.scalar_tensor_tensor(out=s_sb[:, s, :], in0=dist, scalar=slope[:, h:h + 1],
                                                in1=scb[:, 0:3 * P], op0=ALU.mult, op1=ALU.add))
                else:
                    dve.wait_ge(fox_cq, 2 * a + (k + 1))
                    v.scalar_tensor_tensor(out=s_sb[:, s, 0:T], in0=mask[:, 0:T], scalar=cq[:, 2 * h + 1:2 * h + 2],
                                           in1=scb[:, 0:T], op0=ALU.add, op1=ALU.add)
                    link(v.scalar_tensor_tensor(out=s_sb[:, s, T:T + P], in0=mask[:, T:T + P], scalar=cq[:, 2 * h:2 * h + 1],
                                                in1=scb[:, T:T + P], op0=ALU.add, op1=ALU.add))
                v.tensor_reduce(nmax[:, 2 * s:2 * s + 1], s_sb[:, s, T:T + P], AX.X, ALU.max, negate=True)
                v.tensor_reduce(nmax[:, 2 * s + 1:2 * s + 2], s_sb[:, s, 0:T], AX.X, ALU.max, negate=True).then_inc(sc_max, 1)

            def combine(a, h):
                dve.wait_ge(p_exp, score_no(0, a, 2 * h + 1) + 1)
                k = 4 * h
                link(v.reciprocal(rec[:, k:k + 4], lsum[:, k:k + 4]))
                link(v.tensor_scalar(rec[:, k + 2:k + 4], rec[:, k + 2:k + 4], nlam, None, ALU.mult))
                for t, o, w in ((0, T, P), (1, 0, T)):
                    p1, p2 = s_sb[:, 2 * h, o:o + w], s_sb[:, 2 * h + 1, o:o + w]
                    ins = v.tensor_scalar(p2, p2, rec[:, k + 2 + t:k + 3 + t], None, ALU.mult)
                link(ins)
                for t, o, w in ((0, T, P), (1, 0, T)):
                    p1, p2 = s_sb[:, 2 * h, o:o + w], s_sb[:, 2 * h + 1, o:o + w]
                    ins = v.scalar_tensor_tensor(out=p1, in0=p1, scalar=rec[:, k + t:k + t + 1], in1=p2,
                                                 op0=ALU.mult, op1=ALU.subtract)
                ins.then_inc(p_ready, 1)

            def head_out(layer, a, h):
                n = head_no(layer, a, h)
                if layer == 0:
                    dve.wait_ge(pv_rn, n + 1)
                    scale = rno[:, 2 * h:2 * h + 2]
                else:
                    dve.wait_ge(pv_ps, n + 1)
                    link(v.reciprocal(rec[:, 4 * h:4 * h + 2], lsum[:, 4 * h:4 * h + 2]))
                    scale = rec[:, 4 * h:4 * h + 2]
                for t in range(NT):
                    ins = v.scalar_tensor_tensor(out=y_o[:, h, t, :], in0=scb[:, t * P:(t + 1) * P],
                                                 scalar=scale[:, t:t + 1], in1=vz[:, t, T + h * HD:T + (h + 1) * HD],
                                                 op0=ALU.mult, op1=ALU.mult)
                ins.then_inc(y_ready, 1)

            def yt_low(layer, a, h):
                n = head_no(layer, a, h)
                dve.wait_ge(yt_hi, n + 1)
                kt = bass.ds(2 * a + h + (8 if layer == 0 else 0), 1)
                v.scalar_tensor_tensor(out=yl[:, kt, :], in0=trb[:, 0:T].rearrange("p (a t) -> p a t", a=1),
                                       scalar=g_dao if layer == 0 else 1.0, in1=yh[:, kt, :].bitcast(F32),
                                       op0=ALU.mult, op1=ALU.subtract).then_inc(yt_lo, 1)

            def fox_keys(a, h):
                if h == 0:
                    dve.wait_ge(sc_ps, score_no(1, a, 0))
                    dve.wait_ge(c_done, 2)
                v.tensor_scalar(nck[:, h, :], nct, ident[0:16, bass.ds(2 * a + h, 1)], None, ALU.mult).then_inc(fox_b, 1)

            def attention(layer, a, s):
                for h in range(2):
                    if QKT_SLOT[h] == s and layer:
                        fox_keys(a, h)
                for k, at in enumerate(SC_SLOT[layer]):
                    if at == s:
                        score_in(layer, a, k)
                if layer == 0 and s in (5, 7):
                    combine(a, 0 if s == 5 else 1)
                for h in range(2):
                    if PV_SLOT[h] + (1 if layer == 0 else 0) == s:
                        head_out(layer, a, h)
                    if YT_SLOT[h] == s:
                        yt_low(layer, a, h)
                if layer == 0 and s == 7:
                    link(v.tensor_scalar(slope, slope, 0.25, None, ALU.mult))

            def step(layer, i, ch, first, side=None):
                for c in range(2):
                    for j in range(UNITS):
                        s = c * UNITS + j
                        split_lo(dve, 2 * i + (ch + c), j + LEAD)
                        if layer == 0:
                            for g in range(GPI):
                                if X_SLOT[g] + 1 == s:
                                    scan(i, g)
                                if X_SLOT[g] == s:
                                    rotate_in(i, g)
                                    angles(i * GPI + (g + 2), g)
                            if s == 2 and not first:
                                s5_out(i - 1)
                            if s == 5 and not first:
                                s5_low(i - 1)
                        if not first:
                            attention(layer, i - 1, s)
                        if side:
                            side(s)
                        if s == UNITS:
                            qk_squares(layer, i)

            angles(0, 0)
            angles(1, 1)
            step(0, 0, CH_DA, True)
            with dve.Fori(1, DA_PAIRS) as i:
                dve_link.enter(i - 1, DA_LINKS)
                step(0, i, CH_DA, False)
            dve_link.leave(DA_PAIRS - 1)

            s5_out(DA_PAIRS - 1)
            for s in BEFORE_GLU:
                attention(0, DA_PAIRS - 1, s)
            s5_low(DA_PAIRS - 1)
            for j in range(UNITS):
                split_lo(dve, CH_GLU, j + LEAD)
                for s in WITH_GLU[j]:
                    attention(0, DA_PAIRS - 1, s)

            def glu_mul(n):
                if n == 0:
                    dve.wait_ge(silu_done, 1)
                dve.wait_ge(glu_sig, n + 1)
                v.tensor_tensor(glu_s[:, n, :], glu_s[:, n, :], uz[:, CT + n, :], ALU.mult).then_inc(glu_y0, 1)
                dve.wait_ge(glu_y0, n + 1)
                v.tensor_tensor(uz[:, n, :], uz[:, n, :], glu_s[:, n, :], ALU.mult).then_inc(glu_y, 1)

            def glu_low(n):
                dve.wait_ge(glu_hi, n + 1)
                v.tensor_tensor(yl[:, n, :], uz[:, n, :], yh[:, n, :].bitcast(F32), ALU.subtract).then_inc(glu_lo, 1)

            def x1_low(n):
                for e in range(4):
                    kt = 4 * n + e
                    dve.wait_ge(x1_hi, 2 * (kt // 2) + 2)
                    v.scalar_tensor_tensor(out=xl[:, kt, :],
                                           in0=bank[4 + 2 * (n % 2) + e // 2][:, e % 2 * T:(e % 2 + 1) * T],
                                           scalar=o_col[:, kt:kt + 1], in1=xh[:, kt, :].bitcast(F32),
                                           op0=ALU.mult, op1=ALU.subtract).then_inc(x1_lo, 1)

            for n in range(4):
                for j in range(UNITS):
                    split_lo(dve, CH_OUT0 + n, j + LEAD)
                    if n == 0:
                        if j < 4:
                            glu_mul(2 * j)
                            glu_mul(2 * j + 1)
                        for s in AFTER_GLU.get(j, ()):
                            attention(0, DA_PAIRS - 1, s)
                        if j < 4:
                            glu_low(2 * j)
                            glu_low(2 * j + 1)
                    if n and j == 2:
                        x1_low(n - 1)
                dve.wait_ge(unit_used, UNITS * (CH_OUT0 + n + 1) + 1)
                if n == 0:
                    dve.wait_ge(res_in, 16)
                if n >= 2:
                    dve.wait_ge(x1_ps, 2 * (n - 1))
                    dve.wait_ge(x1_kept, n - 1)
                    dve.wait_ge(x1_ssq, 2 * (n - 1))
                for t in range(NT):
                    v.tensor_tensor(x1_st[n % 2][:, t, :], res[:, t, n * CW:(n + 1) * CW], acc[n % 2][t][:, :], ALU.add)\
                        .then_inc(x1_done, 1)
            dve.wait_ge(x1_ssq, 8)
            v.tensor_reduce(ssr, ss1, AX.X, ALU.add).then_inc(r2_sum, 1)

            def side(s):
                if s == 0:
                    x1_low(3)
                if s == 2:
                    dve.wait_ge(wf_hi, 1)
                    v.tensor_tensor(wf2[:, :, 16:32], wf, wf2[:, :, 0:16].bitcast(F32), ALU.subtract).then_inc(wf_lo, 1)
                if s == 9:
                    dve.wait_ge(f_tps, 1)
                    dve.wait_ge(r2_done, 1)
                    for part in range(2):
                        for t in range(NT):
                            at = 400 + 32 * t + 16 * part
                            ins = v.scalar_tensor_tensor(out=ls[:, t, :], in0=yb[:, at:at + 16], scalar=r2_tok[:, t:t + 1],
                                                         in1=ls[:, t, :] if part else bf, op0=ALU.mult, op1=ALU.add)
                        if part == 0:
                            link(ins)
                    ins.then_inc(f_z, 1)
                if s == 10:
                    dve.wait_ge(f_abs, 2)
                    v.tensor_scalar(lsa, lsa, 1.0, None, ALU.add).then_inc(f_exp1, 1)
                if s == 12:
                    dve.wait_ge(f_ln, 1)
                    link(v.tensor_scalar(ls, ls, 0.0, None, ALU.min))
                    v.tensor_tensor(ls, ls, lsa, ALU.subtract).then_inc(f_ls, 1)

            step(1, 0, CH_FOX, True, side)
            with dve.Fori(1, FOX_PAIRS) as i:
                dve_link.enter(i - 1, FOX_LINKS)
                step(1, i, CH_FOX, False)
            dve_link.leave(FOX_PAIRS - 1)

            for n in range(4):
                for j in range(UNITS):
                    if UNITS * (CH_OUT1 + n) + j + LEAD < UNITS * CH_END:
                        split_lo(dve, CH_OUT1 + n, j + LEAD)
                    if n == 0:
                        for s in ({0: [0, 1, 2], 1: [4], 3: [10], 4: [11], 5: [13], 6: [14]}).get(j, []):
                            attention(1, FOX_PAIRS - 1, s)
                dve.wait_ge(unit_used, UNITS * (CH_OUT1 + n + 1) + 1)
                if n == 0:
                    dve.wait_ge(x1_kept, 4)
                for t in range(NT):
                    at = res[:, t, n * CW:(n + 1) * CW]
                    v.tensor_tensor(at, at, acc[n % 2][t][:, :], ALU.add).then_inc(x1_done, 1)

        @block.gpsimd
        def _(pool):
            g = nc.gpsimd

            def link(ins):
                pool_link.inc(ins)
                pool.wait_ge(pool_link.sem, pool_link.value())

            link(g.memset(ident, 0.0))
            link(g.affine_select(out=ident, in_=ident, compare_op=ALU.not_equal, fill=1.0, base=0,
                                 pattern=[[-1, P]], channel_multiplier=1))
            g.memset(ones, 1.0).then_inc(pool_const, 1)
            link(g.iota(pint.bitcast(I32), pattern=[[0, 1]], base=0, channel_multiplier=1))
            link(g.iota(iot[:, 0:T].bitcast(I32), pattern=[[1, T]], base=0, channel_multiplier=0))
            link(g.tensor_copy(steps, iot[:, 0:T].bitcast(I32)))
            link(g.iota(iot[:, T:2 * T].bitcast(I32), pattern=[[-1, T]], base=P, channel_multiplier=1))
            link(g.iota(iot[:, 2 * T:2 * T + P].bitcast(I32), pattern=[[-1, P]], base=0, channel_multiplier=1))
            link(g.tensor_copy(dist, iot[:, T:2 * T + P].bitcast(I32)))
            link(g.memset(mask, 0.0))
            link(g.memset(upto, 1.0))
            for o, w, base in ((0, T, P), (T, P, 0)):
                for m, fill in ((dist, FAR), (mask, -FAR)):
                    link(g.affine_select(out=m[:, o:o + w], in_=m[:, o:o + w], compare_op=ALU.is_ge, fill=fill,
                                         base=base, pattern=[[-1, w]], channel_multiplier=1))
            g.affine_select(out=upto, in_=upto, compare_op=ALU.is_ge, fill=0.0,
                            base=0, pattern=[[1, P]], channel_multiplier=-1).then_inc(pool_const, 1)
            pool.wait_ge(ssq_done, 2)
            pool.wait_ge(slopes, 1)
            link(g.tensor_scalar(ssq, ssq, 1.0 / D, EPS, ALU.mult, ALU.add))
            g.tensor_tensor(r_tok, ssq, expo[:, 0:2], ALU.pow).then_inc(r_done, 1)

            def rotate_in(i, j):
                pool.wait_ge(x_read, i * GPI + (j + 1))
                m1, m2, gg = rot[j % 2]
                g.tensor_tensor(gg[:, 0, :], m1[:, 0, :], m2[:, 1, :], ALU.add)
                g.tensor_tensor(gg[:, 1, :], m1[:, 1, :], m2[:, 0, :], ALU.subtract).then_inc(g_done, 1)

            def rotate_out(i, j):
                pool.wait_ge(scan_done, i * GPI + (j + 1))
                m1, m2, gg = rot[j % 2]
                c, s = (tab[j % 2][:, k:k + 1, :].to_broadcast([P, 2, T]) for k in range(2))
                link(g.tensor_tensor(m2, m1, s, ALU.mult))
                link(g.tensor_tensor(gg, m1, c, ALU.mult))
                g.tensor_tensor(m1[:, 0, :], gg[:, 0, :], m2[:, 1, :], ALU.subtract)
                g.tensor_tensor(m1[:, 1, :], gg[:, 1, :], m2[:, 0, :], ALU.add).then_inc(h_done, 1)

            def qk_norm(layer, i, t):
                na = DA_PAIRS if layer else 0
                seg = 64 if layer == 0 else HD
                n = CW // seg
                if t == 0:
                    pool.wait_ge(qk_ss, i + (na + 1))
                    link(g.tensor_tensor(rnn[:, 0:2 * n], ssn[:, 0:2 * n], expo[:, 0:2 * n], ALU.pow))
                x = qk[:, t, :].rearrange("p (s e) -> p s e", e=seg)
                rn = rnn[:, t * n:(t + 1) * n].rearrange("p (s e) -> p s e", e=1)
                g.tensor_tensor(x, x, rn.to_broadcast([P, n, seg]), ALU.mult).then_inc(qk_ready, 1)

            def out_norm(a, h):
                pool.wait_ge(pv_ssq, head_no(0, a, h) + 1)
                link(g.tensor_tensor(sso[:, 2 * h:2 * h + 2], sso[:, 2 * h:2 * h + 2], eps, ALU.add))
                g.tensor_tensor(rno[:, 2 * h:2 * h + 2], sso[:, 2 * h:2 * h + 2], expo[:, 0:2], ALU.pow).then_inc(pv_rn, 1)

            def step(layer, i, first):
                for s in range(2 * UNITS):
                    if layer == 0:
                        for k in range(GPI):
                            if X_SLOT[k] == s:
                                rotate_in(i, k)
                            if X_SLOT[k] + 1 == s:
                                rotate_out(i, k)
                        if not first:
                            for h in range(2):
                                if PV_SLOT[h] == s:
                                    out_norm(i - 1, h)
                    if s in (10, 12):
                        qk_norm(layer, i, (s - 10) // 2)

            step(0, 0, True)
            with pool.Fori(1, DA_PAIRS) as i:
                pool_link.enter(i - 1, DA_POOL_LINKS)
                step(0, i, False)
            pool_link.leave(DA_PAIRS - 1)
            for h in range(2):
                out_norm(DA_PAIRS - 1, h)
            for n in range(4):
                pool.wait_ge(x1_done, 2 * (n + 1))
                for t in range(NT):
                    ins = g.tensor_copy(res[:, t, n * CW:(n + 1) * CW], x1_st[n % 2][:, t, :])
                ins.then_inc(x1_kept, 1)
            pool.wait_ge(r2_sum, 1)
            link(g.tensor_scalar(ssr, ssr, 1.0 / D, EPS, ALU.mult, ALU.add))
            g.tensor_tensor(r2_tok, ssr, expo[:, 0:2], ALU.pow).then_inc(r2_done, 1)
            step(1, 0, True)
            with pool.Fori(1, FOX_PAIRS) as i:
                pool_link.enter(i - 1, FOX_POOL_LINKS)
                step(1, i, False)
            pool_link.leave(FOX_PAIRS - 1)


_INS = ["x", "e_norm", "e_w_in", "e_w_out", "s5_lambda_re", "s5_lambda_im", "s5_log_dt", "s5_b_re", "s5_b_im",
        "s5_c_re", "s5_c_im", "s5_d", "s5_w_glu", "s5_b_glu", "da_q_norm", "da_k_norm", "da_lambda_q1",
        "da_lambda_k1", "da_lambda_q2", "da_lambda_k2", "da_out_norm", "o_norm", "o_w_in", "o_b_f", "o_w_out",
        "fox_q_norm", "fox_k_norm"]


def kernel(**inputs):
    import numpy as _np
    import concourse.bacc as _bacc
    from concourse import mybir as _mybir
    from concourse.bass_utils import run_bass_kernel_spmd as _run

    nc = _bacc.Bacc("TRN2", target_bir_lowering=False, num_devices=1)
    arrays, args = {}, {}
    for name in _INS:
        a = _np.ascontiguousarray(inputs[name])
        arrays[f"in_{name}"] = a
        args[name] = nc.dram_tensor(f"in_{name}", a.shape, _mybir.dt.from_np(a.dtype), kind="ExternalInput").ap()
    out = nc.dram_tensor("out_dram", (1, T, D), F32, kind="ExternalOutput").ap()
    build(nc, args, out)
    r = _run(nc, [arrays], core_ids=[0])
    return r.results[0]["out_dram"]
```

```python
from contextlib import ExitStack
import math

import numpy as np

import concourse.bass as bass
from concourse import mybir

F32 = mybir.dt.float32
F32R = mybir.dt.float32r
I32 = mybir.dt.int32
ALU = mybir.AluOpType
ACT = mybir.ActivationFunctionType
AX = mybir.AxisListType

P = 128
T = 256
NT = T // P
D = 2048
KT = D // P
CW = 512
UK = 2
UNITS = KT // UK
RING = 4
LEAD = 3
S5W = 1024
CT = S5W // P
GP = 32
GPI = 8
DA_PAIRS = 4
FOX_PAIRS = 8
HD = 128
EPS = 1e-6
FAR = 1e30
MAGIC = 1.5 * 2.0 ** 23

TWO_PI = 2.0 * math.pi
PI_A = 6.28125
PI_B = float(np.float32(round((TWO_PI - PI_A) * 2.0 ** 17) / 2.0 ** 17))
PI_C = float(np.float32(TWO_PI - PI_A - PI_B))
SIN_SCALE = 6.283185

CH_S5 = 0
CH_DA = CH_S5 + 4
CH_GLU = CH_DA + 2 * DA_PAIRS
CH_OUT0 = CH_GLU + 1
CH_FOX = CH_OUT0 + D // CW
CH_OUT1 = CH_FOX + 2 * FOX_PAIRS
CH_END = CH_OUT1 + D // CW
FREE_DA = 2
FREE_FOX = FREE_DA + DA_PAIRS
FREE_OUT1 = FREE_FOX + FOX_PAIRS
SCR, CON = 13192, 2246
LAMBDA_INIT = 0.8 - 0.6 * math.exp(-0.3 * 0)
DA_LINKS, FOX_LINKS, DA_POOL_LINKS, FOX_POOL_LINKS = 29, 6, 20, 2

MAT_UNIT = 18

X_SLOT = [2 * g for g in range(GPI)]
Y_SLOT = [2 * g + 5 for g in range(GPI)]
QKT_SLOT = [1, 2]
SC_SLOT = {0: [3, 4, 5, 6], 1: [3, 5]}
EXP_SLOT = {0: [5, 5, 6, 7], 1: [4, 6]}
PT_SLOT = [7, 9]
PV_SLOT = [8, 11]
YT_SLOT = [12, 14]
WITH_GLU = {0: (1, 2), 1: (3,), 2: (4,), 3: (5, 6), 4: (7, 8), 5: (9,), 6: (10,), 7: (11,)}
AFTER_GLU = {0: (12, 13), 1: (14,)}
WITH_OUT1 = {0: (1, 2), 1: (3, 4), 2: (5, 6), 3: (7, 8), 4: (9, 10), 5: (11, 12), 6: (13, 14)}
OUT0_KT = (8, 10, 12, 0, 2, 4, 6, 14)


class Count:

    def __init__(self, sem):
        self.sem, self.base, self.local, self.it, self.per = sem, 0, 0, None, 0

    def enter(self, it, per):
        self.it, self.per, self.local = it, per, 0

    def leave(self, trips):
        assert self.local == self.per, (self.local, self.per)
        self.base += self.per * trips
        self.it, self.local = None, 0

    def inc(self, ins):
        ins.then_inc(self.sem, 1)
        if self.it is None:
            self.base += 1
        else:
            self.local += 1
        return ins

    def value(self):
        return self.base if self.it is None else self.it * self.per + (self.base + self.local)


def build(nc, d, out_dram):
    ctx = ExitStack()
    with ctx:
        def sb(name, shape, dt=F32):
            return ctx.enter_context(nc.sbuf_tensor(name, shape, dt))

        def sem(name):
            return ctx.enter_context(nc.semaphore(name))

        raw = sb("raw", [P, RING, UK * CW])
        wh = sb("wh", [P, RING, UK * CW], F32R)
        wl = sb("wl", [P, RING, UK * CW], F32R)
        xh = sb("xh", [P, KT, T], F32R)
        xl = sb("xl", [P, KT, T], F32R)
        yh = sb("yh", [P, KT, T], F32R)
        yl = sb("yl", [P, KT, T], F32R)
        res = sb("res", [P, NT, D])
        uz = sb("uz", [P, KT, T])
        scr = sb("scr", [P, SCR])
        con = sb("con", [P, CON])

        used = {"scr": 0, "con": 0}

        def carve(name, *shape, parts=P):
            buf = scr if name == "scr" else con
            n = int(np.prod(shape))
            at = used[name]
            used[name] += n
            assert used[name] <= (SCR if name == "scr" else CON), (name, used[name])
            v = buf[0:parts, at:at + n]
            if len(shape) == 2:
                v = v.rearrange("p (a b) -> p a b", a=shape[0])
            if len(shape) == 3:
                v = v.rearrange("p (a b c) -> p a b c", a=shape[0], b=shape[1])
            return v

        ident = carve("con", P)
        ones = carve("con", P)
        upto = carve("con", P)
        dist = carve("con", 3 * P)
        mask = carve("con", 3 * P)
        steps = carve("con", T)
        rbc = carve("con", T)
        colp = carve("con", 53)
        lamv = carve("con", 4, 64)
        small = carve("con", 256)
        e_col, o_col, d_col, bg_col = colp[:, 0:16], colp[:, 16:32], colp[:, 32:40], colp[:, 40:48]
        g_qk = (colp[:, 48:50], colp[:, 50:52])
        g_dao = colp[:, 52:53]

        def small_at(a, n):
            return small[:, a:a + n]

        ssq = small_at(0, 2)
        r_tok = small_at(2, 2)
        expo = small_at(4, 16)
        par = small_at(20, 2)
        nlam = small_at(22, 1)
        lt = small_at(23, 4)
        slope = small_at(27, 2)
        bf = small_at(29, 16)
        ss1 = small_at(45, 8).rearrange("p (t n) -> p t n", t=2)
        nmax = small_at(53, 8)
        lsum = small_at(61, 8)
        rec = small_at(69, 8)
        sso = small_at(77, 4)
        rno = small_at(81, 4)
        ssn = small_at(85, 16)
        rnn = small_at(101, 16)
        cq = small_at(117, 4)
        mag_st = small_at(121, GPI)
        r2_tok = small_at(145, 2)
        junk1 = small_at(160, 5)
        pint = small_at(150, 1)
        ssr = small_at(152, 2)
        half_pi = small_at(154, 1)
        magic, eps = small_at(155, 1), small_at(156, 2)

        qk = carve("scr", NT, CW)
        vz = carve("scr", NT, CW)
        qkt = carve("scr", 2, 2, T)
        s_sb = carve("scr", 4, 3 * P)
        p_t = carve("scr", 2, 3 * P)
        y_o = qkt.rearrange("p h b (t e) -> p h (b t) e", t=NT)[:, :, 0:NT, :]
        main0 = used["scr"]
        hs = [carve("scr", 2, T) for _ in range(4)]
        rot = [[carve("scr", 2, T) for _ in range(2)] for _ in range(2)]
        tab = [carve("scr", 2, T) for _ in range(2)]
        ang = [carve("scr", T) for _ in range(2)]
        ph = [carve("scr", T) for _ in range(2)]
        lb_st = carve("scr", 2, 2, P)
        cd_st = carve("scr", 2, 2, P)
        u_st = carve("scr", 2, T)
        main1 = used["scr"]
        used["scr"] = main0
        x1_st = [carve("scr", NT, CW) for _ in range(2)]
        wf = carve("scr", KT, 16)
        f_sb = carve("scr", T, parts=32)
        nct = carve("scr", T, parts=16)
        nks = carve("scr", T, parts=48)
        sel = carve("scr", 16, parts=48)
        c_sb = carve("scr", NT, 16)
        ls = carve("scr", NT, 16)
        lsa = carve("scr", NT, 16)
        used["scr"] = main0
        glu_s = carve("scr", CT, T)
        used["scr"] = 0
        rows_e = carve("scr", P, parts=16)
        rows = carve("scr", P, parts=37)
        lamr_r = carve("scr", P, parts=GP)
        lami_r = carve("scr", P, parts=GP)
        ldt_r = carve("scr", 2, 64, parts=GP)
        ldt_in = carve("scr", 2, parts=GP)
        b_n = carve("scr", 2, GP, 16)
        c_n = carve("scr", 2, CT, 64)
        bt = [carve("scr", GP, 16) for _ in range(4)]
        bd = carve("scr", 2, GP, 32)
        cb = carve("scr", CT, P)
        cb2 = carve("scr", CT, P)
        prm = [carve("scr", GP) for _ in range(20)]
        iot = carve("scr", 5 * P)
        junk = uz[:, 0:CT, :].rearrange("p a t -> p (a t)")
        used["scr"] = main1
        phc = carve("scr", 4, GP + 2)
        wf2 = sb("wf2", [P, KT, 32], F32R)
        nck = wf2[0:48, :, :].rearrange("p a b -> p (a b)").rearrange("p (h t) -> p h t", h=2)
        ones_r = sb("ones_r", [48, P], F32R)
        phr = sb("phr", [P, GP], F32R)
        ph_hi, ph_lo, mag_all, ph_all = (phc[:, k, 0:GP] for k in range(4))

        lb = res.rearrange("p t n -> p (t n)").rearrange("p (c r s) -> p c r s", c=2 * CT, r=2)
        cd = res[:, 1, :].rearrange("p (r c s) -> p r c s", r=2, c=CT)

        bank = [ctx.enter_context(nc.psum_tensor(f"bank{i}", [P, CW], F32)) for i in range(8)]
        acc = [bank[0:2], bank[2:4]]
        trb, scb, xb, yb = bank[4], bank[5], bank[6], bank[7]

        raw_in = [sem(f"raw_in{i}") for i in range(RING)]
        hi_done = sem("hi_done")
        lo_done = sem("lo_done")
        unit_used = sem("unit_used")
        acc_free = [sem("acc_free0"), sem("acc_free1")]
        x_in = [sem(f"x_in{k}") for k in range(4)]
        rows_in, par_in, bc_in, s5_in, wf_in, res_in = (sem(n) for n in
            ("rows_in", "par_in", "bc_in", "s5_in", "wf_in", "res_in"))
        out_done = sem("out_done")
        pool_const, tile_ps, tile_hi, tile_lo = (sem(n) for n in
            ("pool_const", "tile_ps", "tile_hi", "tile_lo"))
        ssq_done, r_done, diag_done, rbc_ps, rbc_done = (sem(n) for n in
            ("ssq_done", "r_done", "diag_done", "rbc_ps", "rbc_done"))
        prm_rows, prm_ps, prm_ld, prm_exp, prm_ang, prm_trig, bd_done, cb_done = (sem(n) for n in
            ("prm_rows", "prm_ps", "prm_ld", "prm_exp", "prm_ang", "prm_trig", "bd_done", "cb_done"))
        mat_ps, mat_sb, prm_done = (sem(n) for n in ("mat_ps", "mat_sb", "prm_done"))
        staged, staged_mag, staged_c, slopes = (sem(n) for n in ("staged", "staged_mag", "staged_c", "slopes"))
        phase_up = sem("phase_up")
        ang_done, tab_done, x_ps, x_read, g_done, scan_done, h_done, y_ps, y_read = (
            sem(n) for n in ("ang_done", "tab_done", "x_ps", "x_read", "g_done", "scan_done",
                             "h_done", "y_ps", "y_read"))
        gelu_done, s5_hi, s5_lo = sem("gelu_done"), sem("s5_hi"), sem("s5_lo")
        qk_sq, qk_ss, qk_ready = sem("qk_sq"), sem("qk_ss"), sem("qk_ready")
        qkt_ps, qkt_sb, sc_ps, sc_max, p_exp, p_ready, pt_ps, pt_sb = (sem(n) for n in
            ("qkt_ps", "qkt_sb", "sc_ps", "sc_max", "p_exp", "p_ready", "pt_ps", "pt_sb"))
        pv_ps, pv_ssq, pv_rn, y_ready, yt_ps, yt_hi, yt_lo = (sem(n) for n in
            ("pv_ps", "pv_ssq", "pv_rn", "y_ready", "yt_ps", "yt_hi", "yt_lo"))
        fox_b, fox_cq, c_split = sem("fox_b"), sem("fox_cq"), sem("c_split")
        glu_sig, glu_y0, glu_y, glu_hi, glu_lo, silu_done = (sem(n) for n in
            ("glu_sig", "glu_y0", "glu_y", "glu_hi", "glu_lo", "silu_done"))
        x1_done, x1_kept, x1_ps, x1_hi, x1_lo, x1_ssq, r2_done, r2_sum = (sem(n) for n in
            ("x1_done", "x1_kept", "x1_ps", "x1_hi", "x1_lo", "x1_ssq", "r2_done", "r2_sum"))
        f_sbuf, f_tps = sem("f_sbuf"), sem("f_tps")
        wf_hi, wf_lo, f_ps, f_z, f_abs, f_exp1, f_ln, f_ls, c_ps, c_done = (sem(n) for n in
            ("wf_hi", "wf_lo", "f_ps", "f_z", "f_abs", "f_exp1", "f_ln", "f_ls", "c_ps", "c_done"))
        dve_link, act_link, pool_link = (Count(sem(n)) for n in ("dve_link", "act_link", "pool_link"))
        lambda_done = sem("lambda_done")

        def head_no(layer, a, h):
            return 2 * a + h + (2 * DA_PAIRS if layer else 0)

        def score_no(layer, a, k):
            return (4 * DA_PAIRS + 2 * a if layer else 4 * a) + k

        def place(eng, at):
            return at if isinstance(at, int) else eng.snap(at)

        def unit_rows(w, kt0, n=UK):
            return w.rearrange("(k p) n -> p k n", p=P)[:, kt0:kt0 + n, :]

        block = ctx.enter_context(nc.Block())

        @block.sync
        def _(sp):
            def load(j, src):
                dst = raw[:, j % RING, :]
                if len(src.shape) == 3:
                    sp.dma_start(dst.rearrange("p (k n) -> p k n", k=src.shape[1]), src).then_inc(raw_in[j % RING], 32)
                else:
                    dst = dst.rearrange("p (k b n) -> p k b n", k=UK, b=2)
                    for k in range(UK):
                        sp.dma_start(dst[:, k, :, :], src[:, k, :, :]).then_inc(raw_in[j % RING], 16)

            def chunk(c, cols):
                for j in range(UNITS):
                    src = cols(j)
                    if UNITS * c + j >= RING:
                        sp.wait_ge(lo_done, UNITS * c + j - RING + 1)
                    load(j, src)

            w_e, w_eo, w_o, w_oo, w_g = d["e_w_in"][0], d["e_w_out"][0], d["o_w_in"][0], d["o_w_out"][0], d["s5_w_glu"][0]
            def s5_cols(j):
                if c == 0 and j < 4:
                    q = slice(j * CW, (j + 1) * CW)
                    sp.dma_start(res[:, :, q], d["x"][0].rearrange("(t p) n -> p t n", p=P)[:, :, q]).then_inc(x_in[j], 16)
                return unit_rows(w_e, UK * j)[:, :, CW * c:CW * (c + 1)]

            for c in range(4):
                chunk(CH_S5 + c, s5_cols)

            def pair_cols(w, base, width, j, at):
                v = unit_rows(w, UK * j)[:, :, base:base + 2 * width]
                return v.rearrange("p k (b s) -> p k b s", b=2)[:, :, :, bass.ds(at, 2 * HD)]

            def steps_of(w, base, width, ch, trips):
                for c in (0, 1):
                    chunk(ch + c, lambda j: pair_cols(w, base + 2 * width * c, width, j, 0))
                with sp.Fori(1, trips) as i:
                    at = sp.snap(i * (2 * HD))
                    for c in (0, 1):
                        for j in range(UNITS):
                            need = sp.snap(i * (2 * UNITS) + (UNITS * (ch + c) + j - RING + 1))
                            sp.wait_ge(lo_done, need)
                            load(j, pair_cols(w, base + 2 * width * c, width, j, at))

            steps_of(w_e, 2 * S5W, S5W, CH_DA, DA_PAIRS)
            chunk(CH_GLU, lambda j: w_g.rearrange("(k p) n -> p k n", p=P)[:, j:j + 1, :])
            sp.wait_ge(staged, DA_PAIRS + 1)
            sp.wait_ge(staged_c, DA_PAIRS)
            sp.dma_start(res[:, :, :], d["x"][0].rearrange("(t p) n -> p t n", p=P)).then_inc(res_in, 16)
            for c in range(4):
                chunk(CH_OUT0 + c, lambda j: unit_rows(w_eo, OUT0_KT[j])[:, :, CW * c:CW * (c + 1)])
            steps_of(w_o, 0, D, CH_FOX, FOX_PAIRS)
            for c in range(4):
                chunk(CH_OUT1 + c, lambda j: unit_rows(w_oo, UK * j)[:, :, CW * c:CW * (c + 1)])
            sp.wait_ge(out_done, 16 * 4)

        @block.tensor
        def _(pe):
            def unit_ready(c, j):
                pe.wait_ge(lo_done, (c * UNITS) + (j + 1))

            def rows_unit(c, j, left, kts, pair):
                lh, ll = left
                unit_ready(c, j)
                for a, kt in enumerate(kts):
                    w_hi, w_lo = wh[:, j % RING, a * CW:(a + 1) * CW], wl[:, j % RING, a * CW:(a + 1) * CW]
                    first, last = j == 0 and a == 0, j == UNITS - 1 and a == UK - 1
                    for t in range(NT):
                        o = acc[pair][t][:, :]
                        l_hi, l_lo = lh[:, kt, t * P:(t + 1) * P], ll[:, kt, t * P:(t + 1) * P]
                        nc.tensor.matmul(o, l_hi, w_hi, start=first, stop=False)
                        nc.tensor.matmul(o, l_hi, w_lo, start=False, stop=False)
                        mm = nc.tensor.matmul(o, l_lo, w_hi, start=False, stop=last)
                mm.then_inc(unit_used, 1)

            def cols_unit(c, j, right, kt_of, banks, nk, width, late=False):
                rh, rl = right
                unit_ready(c, j)
                for a in range(nk):
                    kt = kt_of(a)
                    first, last = j == 0 and a == 0, j == UNITS - 1 and a == nk - 1
                    for n in range(width // P):
                        if late and n == 4:
                            attention(0, DA_PAIRS - 1, 1)
                            chunk_start(1, FREE_FOX)
                        o = banks[n // 2][:, (n % 2) * T:(n % 2 + 1) * T]
                        at = a * width + n * P
                        w_hi, w_lo = wh[:, j % RING, at:at + P], wl[:, j % RING, at:at + P]
                        nc.tensor.matmul(o, w_hi, rh[:, kt, :], start=first and n % 2 == 0, stop=False, skip_group_check=True)
                        nc.tensor.matmul(o, w_hi, rl[:, kt, :], start=False, stop=False, skip_group_check=True)
                        mm = nc.tensor.matmul(o, w_lo, rh[:, kt, :], start=False, stop=last, skip_group_check=True)
                mm.then_inc(unit_used, 1)

            def chunk_start(pair, free):
                pe.wait_ge(acc_free[pair], free + 1)

            def qk_turn(layer, a, h):
                if h == 0:
                    pe.wait_ge(qk_ready, 2 * a + 2 + 2 * (DA_PAIRS if layer else 0))
                n = head_no(layer, a, h)
                if h:
                    pe.wait_ge(qkt_sb, n)
                else:
                    pe.wait_ge(yt_lo, n + 1)
                for b in range(2):
                    for t in range(NT):
                        at = b * T + h * HD
                        mm = nc.tensor.transpose(trb[:, b * T + t * P:b * T + (t + 1) * P],
                                                 qk[:, t, at:at + HD], ident)
                mm.then_inc(qkt_ps, 1)

            def scores(layer, a, h, comp):
                k = (2 * h + comp) if layer == 0 else h
                n = score_no(layer, a, k)
                if comp == 0:
                    pe.wait_ge(qkt_sb, head_no(layer, a, h) + 1)
                if k:
                    pe.wait_ge(sc_max, n)
                else:
                    pe.wait_ge(y_ready, head_no(layer, a, 0) + 1)
                lo, hi = (64 * comp, 64 * comp + 64) if layer == 0 else (0, P)
                if layer:
                    pe.wait_ge(fox_b, n - 4 * DA_PAIRS + 1)
                for o, t, w in ((0, 1, T), (T, 0, P)):
                    mm = nc.tensor.matmul(scb[:, o:o + w], qkt[lo:hi, h, 0, t * P:(t + 1) * P],
                                          qkt[lo:hi, h, 1, 0:w], start=True, stop=layer == 0)
                    if layer:
                        mm = nc.tensor.matmul(scb[:, o:o + w], ones_r[:, :], nck[:, h, 0:w],
                                              start=False, stop=True)
                mm.then_inc(sc_ps, 1)

            def p_turn(layer, a, h):
                n = head_no(layer, a, h)
                pe.wait_ge(p_ready, n + 1)
                if h == 0:
                    pe.wait_ge(qkt_sb, head_no(layer, a, 1) + 1)
                else:
                    pe.wait_ge(pt_sb, n)
                for b in range(3):
                    mm = nc.tensor.transpose(trb[:, b * P:(b + 1) * P],
                                             s_sb[:, 2 * h, b * P:(b + 1) * P], ident)
                mm.then_inc(pt_ps, 1)

            def values(layer, a, h):
                n = head_no(layer, a, h)
                pe.wait_ge(pt_sb, n + 1)
                if h == 0:
                    pe.wait_ge(acc_free[1], a + ((FREE_FOX if layer else FREE_DA) + 2))
                    pe.wait_ge(sc_max, score_no(layer, a, 3 if layer == 0 else 1) + 1)
                else:
                    pe.wait_ge(y_ready, n + 1)
                v = [vz[:, t, h * HD:(h + 1) * HD] for t in range(NT)]
                nc.tensor.matmul(scb[:, 0:P], p_t[:, h, 2 * P:3 * P], v[0], start=True, stop=True)
                nc.tensor.matmul(scb[:, P:2 * P], p_t[:, h, 0:P], v[0], start=True, stop=False)
                nc.tensor.matmul(scb[:, P:2 * P], p_t[:, h, P:2 * P], v[1], start=False, stop=True)\
                    .then_inc(pv_ps, 1)

            def y_turn(layer, a, h):
                n = head_no(layer, a, h)
                pe.wait_ge(y_ready, n + 2)
                if h == 0:
                    pe.wait_ge(pt_sb, head_no(layer, a, 1) + 1)
                else:
                    pe.wait_ge(yt_lo, n + 1)
                for t in range(NT):
                    mm = nc.tensor.transpose(trb[:, t * P:(t + 1) * P], y_o[:, h, t, :], ident)
                mm.then_inc(yt_ps, 1)

            def attention(layer, a, s):
                for h in range(2):
                    if QKT_SLOT[h] == s:
                        qk_turn(layer, a, h)
                for k, at in enumerate(SC_SLOT[layer]):
                    if at == s:
                        scores(layer, a, *((k // 2, k % 2) if layer == 0 else (k, 0)))
                for h in range(2):
                    if PT_SLOT[h] == s:
                        p_turn(layer, a, h)
                    if PV_SLOT[h] == s:
                        values(layer, a, h)
                    if YT_SLOT[h] == s:
                        y_turn(layer, a, h)

            def s5_in_x(i, j):
                c, q = j // 4, j % 4
                if j == 0:
                    pe.wait_ge(staged, i + 1)
                if not (isinstance(i, int) and i == 0 and j == 0):
                    pe.wait_ge(x_read, i * GPI + j)
                for r in range(2):
                    mm = nc.tensor.matmul(xb[:, r * T:(r + 1) * T], lb_st[32 * q:32 * q + 32, c, r, :],
                                          u_st[32 * q:32 * q + 32, c, :], start=True, stop=True)
                mm.then_inc(x_ps, 1)

            def s5_out_y(i, j):
                c, q = j // 4, j % 4
                pe.wait_ge(h_done, i * GPI + (j + 1))
                if j == 0:
                    pe.wait_ge(staged_c, i + 1)
                if j == 0 and not (isinstance(i, int) and i == 0):
                    pe.wait_ge(y_read, i)
                for r in range(2):
                    mm = nc.tensor.matmul(yb[32 * q:32 * q + 32, c * T:(c + 1) * T],
                                          cd_st[:, r, c, 32 * q:32 * q + 32], hs[j % 4][:, r, :],
                                          start=r == 0, stop=r == 1)
                mm.then_inc(y_ps, 1)

            pe.wait_ge(pool_const, 1)
            pe.wait_ge(rows_in, 16)
            nc.tensor.transpose(xb[:, 0:16], rows_e, ident[0:16, 0:16]).then_inc(prm_ps, 1)

            def tiles(b):
                if b % 2 == 0:
                    pe.wait_ge(x_in[b // 2], 16)
                if b >= 2:
                    pe.wait_ge(tile_lo, 2 * (b - 1))
                for e in range(2):
                    for t in range(NT):
                        kt = 2 * b + e
                        mm = nc.tensor.transpose(bank[4 + b % 2][:, e * T + t * P:e * T + (t + 1) * P],
                                                 res[:, t, kt * P:(kt + 1) * P], ident)
                mm.then_inc(tile_ps, 1)

            def parameters():
                pe.wait_ge(par_in, 16 * 12)
                pe.wait_ge(prm_ld, 1)
                nc.tensor.transpose(xb[:, 64:96], lamr_r, ident[0:GP, 0:GP])
                nc.tensor.transpose(xb[:, 96:128], lami_r, ident[0:GP, 0:GP])
                nc.tensor.transpose(xb[:, 160:197], rows, ident[0:37, 0:37])
                pe.wait_ge(prm_rows, 1)
                nc.tensor.transpose(xb[:, 128:160], ldt_r.rearrange("p a b -> p (a b)"), ident[0:GP, 0:GP])\
                    .then_inc(prm_ps, 1)

            def s5_matrix(m):
                if m >= 2:
                    pe.wait_ge(mat_sb, m - 1)
                if m == 0:
                    pe.wait_ge(bd_done, 1)
                if m == 8:
                    pe.wait_ge(cb_done, 2)
                for r in range(2):
                    src = bd[:, r, 4 * m:4 * m + 4, :].rearrange("p a b -> p (a b)") if m < 8 else (cb, cb2)[r][:, m - 8, :]
                    mm = nc.tensor.transpose(bank[4 + m % 2][:, r * P:(r + 1) * P], src, ident)
                mm.then_inc(mat_ps, 1)

            for b in range(LEAD):
                tiles(b)

            for c in range(4):
                chunk_start(c % 2, c // 2)
                for j in range(UNITS):
                    if c == 0:
                        pe.wait_ge(tile_lo, UK * (j + 1))
                    cols_unit(CH_S5 + c, j, (xh, xl), lambda a: UK * j + a, acc[c % 2], UK, CW)
                    if c == 0 and j + LEAD < UNITS:
                        tiles(j + LEAD)
                    if c == 1 and j == 0:
                        pe.wait_ge(diag_done, 1)
                        nc.tensor.matmul(yb[:, 0:T], ones, rbc, start=True, stop=True).then_inc(rbc_ps, 1)
                    if c == 1 and j == 1:
                        parameters()
                    if 0 <= c * UNITS + j - MAT_UNIT < 8:
                        s5_matrix(2 * (c * UNITS + j - MAT_UNIT))
                        s5_matrix(2 * (c * UNITS + j - MAT_UNIT) + 1)

            def step(layer, i, ch, use, first, side=None):
                for c in range(2):
                    chunk_start(c, i + use)
                    for j in range(UNITS):
                        s = c * UNITS + j
                        rows_unit(2 * i + (ch + c), j, (xh, xl), (UK * j, UK * j + 1), c)
                        if not first:
                            attention(layer, i - 1, s)
                        if layer == 0:
                            for g in range(GPI):
                                if X_SLOT[g] == s:
                                    s5_in_x(i, g)
                                if Y_SLOT[g] == s:
                                    s5_out_y(i, g)
                                if not first and Y_SLOT[g] - 2 * UNITS == s:
                                    s5_out_y(i - 1, g)
                        if side:
                            side(s)

            step(0, 0, CH_DA, FREE_DA, True)
            with pe.Fori(1, DA_PAIRS) as i:
                step(0, i, CH_DA, FREE_DA, False)

            glu_banks = [acc[0][0], acc[0][1], acc[1][0], acc[1][1]]
            pe.wait_ge(s5_lo, 2 * DA_PAIRS - 2)
            chunk_start(0, FREE_FOX)
            for j in range(UNITS):
                if j == UNITS - 2:
                    pe.wait_ge(s5_lo, 2 * DA_PAIRS)
                cols_unit(CH_GLU, j, (yh, yl), lambda a: j, glu_banks, 1, S5W, late=j == 0)
                if j < 2:
                    s5_out_y(DA_PAIRS - 1, GPI - 2 + j)
                for s in WITH_GLU[j][1 if j == 0 else 0:]:
                    attention(0, DA_PAIRS - 1, s)

            def x1_turn(n):
                pe.wait_ge(x1_done, 2 * (n + 1))
                if n == 0:
                    pe.wait_ge(yt_lo, 2 * DA_PAIRS + 1)
                for b in range(2):
                    o = bank[4 + 2 * (n % 2) + b]
                    if n >= 2:
                        pe.wait_ge(x1_lo, 4 * (n - 2) + 2 * b + 2)
                    for e in range(2):
                        for t in range(NT):
                            at = (2 * b + e) * P
                            mm = nc.tensor.transpose(o[:, e * T + t * P:e * T + (t + 1) * P],
                                                     x1_st[n % 2][:, t, at:at + P], ident)
                    mm.then_inc(x1_ps, 1)

            for n in range(4):
                if n < 2:
                    pe.wait_ge(glu_sig, 4 * n + 4)
                else:
                    pe.wait_ge(x1_done, 2 * (n - 1))
                for j in range(UNITS):
                    if n == 0 and j == 0:
                        pe.wait_ge(yt_lo, 2 * DA_PAIRS - 1)
                    if n == 0 and j == UNITS - 1:
                        pe.wait_ge(yt_lo, 2 * DA_PAIRS + 1)
                    if n == 0 and 3 <= j < UNITS - 1:
                        pe.wait_ge(glu_lo, OUT0_KT[j] + UK)
                    kt = OUT0_KT[j]
                    rows_unit(CH_OUT0 + n, j, (yh, yl), (kt, kt + 1), n % 2)
                    if n == 0:
                        for s in AFTER_GLU.get(j, ()):
                            attention(0, DA_PAIRS - 1, s)
                    if n and j == 2:
                        x1_turn(n - 1)

            def fox_gates():
                pe.wait_ge(wf_lo, 1)
                for kt in range(KT):
                    for x, first, last in ((xh, kt == 0, False), (xl, False, kt == KT - 1)):
                        mm = nc.tensor.matmul(yb[0:32, 0:T], wf2[:, kt, :], x[:, kt, :], start=first, stop=last)
                mm.then_inc(f_ps, 1)

            def fox_turn():
                pe.wait_ge(f_sbuf, 1)
                for t in range(NT):
                    mm = nc.tensor.transpose(yb[:, 400 + 32 * t:432 + 32 * t], f_sb[:, t * P:(t + 1) * P], ident[0:32, 0:32])
                mm.then_inc(f_tps, 1)

            def fox_sums():
                pe.wait_ge(f_ls, 1)
                nc.tensor.matmul(yb[:, 64:80], upto, ls[:, 0, :], start=True, stop=True)
                nc.tensor.matmul(yb[:, 80:96], ones, ls[:, 0, :], start=True, stop=False)
                nc.tensor.matmul(yb[:, 80:96], upto, ls[:, 1, :], start=False, stop=True)
                nc.tensor.matmul(yb[0:16, 128:256], ls[:, 0, :], upto, start=True, stop=True)
                nc.tensor.matmul(yb[0:16, 256:384], ls[:, 0, :], ones, start=True, stop=False)
                nc.tensor.matmul(yb[0:16, 256:384], ls[:, 1, :], upto, start=False, stop=True)\
                    .then_inc(c_ps, 1)

            def side(s):
                if s == 0:
                    x1_turn(3)
                if s == 5:
                    pe.wait_ge(x1_lo, KT)
                if s == 8:
                    fox_gates()
                if s == 9:
                    fox_turn()
                if s == 13:
                    fox_sums()

            pe.wait_ge(x1_lo, 12)
            def fox_first():
                for c in range(2):
                    pe.wait_ge(x1_done, 6 + 2 * c)
                    for j in range(UNITS):
                        s = c * UNITS + j
                        if s == 6:
                            pe.wait_ge(x1_lo, KT)
                        rows_unit(CH_FOX + c, j, (xh, xl), (UK * j, UK * j + 1), c)
                        side(s)

            fox_first()
            with pe.Fori(1, FOX_PAIRS) as i:
                step(1, i, CH_FOX, FREE_FOX, False)

            for n in range(4):
                if n < 2:
                    chunk_start(n, FREE_OUT1)
                else:
                    pe.wait_ge(x1_done, 8 + 2 * (n - 1))
                for j in range(UNITS):
                    if n == 0 and j == 0:
                        pe.wait_ge(yt_lo, 2 * (DA_PAIRS + FOX_PAIRS) - 1)
                    if n == 0 and j == UNITS - 1:
                        pe.wait_ge(yt_lo, 2 * (DA_PAIRS + FOX_PAIRS) + 1)
                    rows_unit(CH_OUT1 + n, j, (yh, yl), (UK * j, UK * j + 1), n % 2)
                    if n == 0:
                        for s in WITH_OUT1.get(j, ()):
                            attention(1, FOX_PAIRS - 1, s)

        def split_hi(act, c, j):
            if j >= UNITS:
                c, j = c + 1, j - UNITS
            act.wait_ge(raw_in[j % RING], c * 64 + (32 * (j // RING) + 32))
            if not (isinstance(c, int) and c * UNITS + j < RING):
                act.wait_ge(unit_used, c * UNITS + (j - RING + 2))
            nc.scalar.activation(wh[:, j % RING, :], raw[:, j % RING, :], ACT.Copy).then_inc(hi_done, 1)

        def split_lo(dve, c, j):
            if j >= UNITS:
                c, j = c + 1, j - UNITS
            dve.wait_ge(hi_done, c * UNITS + (j + 1))
            nc.vector.tensor_tensor(wl[:, j % RING, :], raw[:, j % RING, :],
                                    wh[:, j % RING, :].bitcast(F32), ALU.subtract).then_inc(lo_done, 1)

        @block.scalar
        def _(act):
            link = act_link.inc

            def bc(src, n):
                return src.rearrange("(a n) -> a n", a=1).to_broadcast([P, n])

            act.dma_start(rows_e, d["e_norm"][0].rearrange("(a n) -> a n", n=P)).then_inc(rows_in, 16)

            small = [(rows[at:at + n, :], d[name][0].rearrange("(a n) -> a n", n=P), par_in) for at, name, n in
                     ((0, "o_norm", 16), (16, "s5_d", 8), (24, "s5_b_glu", 8), (32, "da_q_norm", 1),
                      (33, "da_k_norm", 1), (34, "fox_q_norm", 1), (35, "fox_k_norm", 1), (36, "da_out_norm", 1))]
            small += [(lamr_r, d["s5_lambda_re"][0].rearrange("(a b) p -> a (b p)", b=2), par_in),
                      (lami_r, d["s5_lambda_im"][0].rearrange("(a b) p -> a (b p)", b=2), par_in),
                      (ldt_in, d["s5_log_dt"][0].rearrange("(a b) -> a b", b=2), par_in),
                      (bf, bc(d["o_b_f"][0], 16), par_in)]
            small += [(b_n[:, at, :, :], d[name][0].rearrange("(a b) p h -> (b p) a h", b=2), s5_in)
                      for at, name in ((0, "s5_b_re"), (1, "s5_b_im"))]
            small += [(lamv[:, k, :], bc(d[name][0], 64), bc_in) for k, name in
                      enumerate(("da_lambda_q1", "da_lambda_k1", "da_lambda_q2", "da_lambda_k2"))]
            small += [(c_n[:, at, :, :], d[name][0].rearrange("(a b) h p -> (b h) a p", b=8), s5_in)
                      for at, name in ((0, "s5_c_re"), (1, "s5_c_im"))]

            def tiles_up(b):
                act.wait_ge(tile_ps, b + 1)
                for e in range(2):
                    kt = 2 * b + e
                    nc.scalar.activation(xh[:, kt, :], bank[4 + b % 2][:, e * T:(e + 1) * T],
                                         ACT.Copy, scale=e_col[:, kt:kt + 1]).then_inc(tile_hi, 1)

            def squares(t):
                nc.scalar.activation(junk, res[:, t, :], ACT.Square, accum_out=ssq[:, t:t + 1]).then_inc(ssq_done, 1)
                act.wait_ge(ssq_done, t + 1)

            act.wait_ge(prm_ps, 1)
            nc.scalar.activation(e_col, xb[:, 0:16], ACT.Copy).then_inc(prm_ld, 1)
            act.wait_ge(prm_ld, 1)
            for j in range(LEAD):
                tiles_up(j)
                split_hi(act, 0, j)

            def phases(n, j):
                if isinstance(n, int) and n == 0:
                    act.wait_ge(prm_ang, 3)
                    act.wait_ge(pool_const, 2)
                if not (isinstance(n, int) and n < 2):
                    act.wait_ge(tab_done, n * 2 - 2)
                at, w = place(act, n), ang[j % 2]
                nc.scalar.activation(w, steps, ACT.Identity, scale=phc[:, 3, bass.ds(at, 1)], bias=magic)
                nc.scalar.activation(ph[j % 2], steps, ACT.Copy, scale=phc[:, 0, bass.ds(at, 1)]).then_inc(phase_up, 1)

            def params(c, j):
                if (c, j) == (1, 2):
                    act.wait_ge(prm_ps, 2)
                    nc.scalar.activation(colp[:, 16:53], xb[:, 160:197], ACT.Copy).then_inc(prm_ld, 1)
                if (c, j) == (1, 4):
                    act.wait_ge(prm_ang, 1)
                    nc.scalar.activation(prm[3], prm[2], ACT.Exp).then_inc(prm_exp, 1)
                if (c, j) == (1, 5):
                    act.wait_ge(prm_ang, 2)
                    nc.scalar.activation(mag_all, prm[4], ACT.Exp).then_inc(prm_exp, 1)
                    act.wait_ge(lambda_done, 1)
                    nc.scalar.activation(lt[:, 2:4], lt[:, 0:2], ACT.Exp).then_inc(prm_exp, 1)
                    act.wait_ge(prm_ang, 3)
                    nc.scalar.activation(prm[11], prm[10], ACT.Sin, scale=SIN_SCALE).then_inc(prm_trig, 1)
                    nc.scalar.activation(prm[13], prm[10], ACT.Abs).then_inc(prm_trig, 1)
                    act.wait_ge(prm_trig, 2)
                    nc.scalar.activation(prm[12], prm[13], ACT.Sin, scale=-SIN_SCALE, bias=half_pi).then_inc(prm_trig, 1)
                if 0 <= c * UNITS + j - MAT_UNIT < 8:
                    for m in range(2 * (c * UNITS + j - MAT_UNIT), 2 * (c * UNITS + j - MAT_UNIT) + 2):
                        act.wait_ge(mat_ps, m + 1)
                        o = bank[4 + m % 2][:, 0:2 * P].rearrange("p (r s) -> p r s", r=2)
                        dst = lb[:, m, :, :] if m < 8 else cd[:, :, m - 8, :]
                        nc.scalar.activation(dst, o, ACT.Copy).then_inc(mat_sb, 1)

            for c in range(4):
                for j in range(UNITS):
                    if c == 0 and j + LEAD < UNITS:
                        tiles_up(j + LEAD)
                    split_hi(act, c, j + LEAD)
                    if c == 0:
                        for dst, src, arrived in small[3 * j:3 * j + 3]:
                            act.dma_start(dst, src).then_inc(arrived, 16)
                        if 4 <= j < 4 + NT:
                            squares(j - 4)
                    params(c, j)
                    if (c, j) in ((3, 3), (3, 5)):
                        phases((j - 3) // 2, (j - 3) // 2)

            def gate(s):
                if s == 7:
                    act.wait_ge(acc_free[1], FREE_DA + 1)
                    nc.scalar.activation(uz[:, CT:2 * CT, :], uz[:, CT:2 * CT, :], ACT.Silu).then_inc(silu_done, 1)

            def stage_mag(i):
                if isinstance(i, int) and i == 0:
                    act.wait_ge(prm_exp, 2)
                else:
                    act.wait_ge(scan_done, i * GPI)
                nc.scalar.activation(mag_st, phc[:, 2, bass.ds(place(act, i * GPI), GPI)], ACT.Copy).then_inc(staged_mag, 1)

            def stage_c(i):
                if isinstance(i, int) and i == 0:
                    act.wait_ge(mat_sb, 16)
                else:
                    act.wait_ge(y_ps, i * GPI)
                nc.scalar.activation(cd_st, cd[:, :, bass.ds(place(act, i * 2), 2), :], ACT.Copy).then_inc(staged_c, 1)

            def table(n, j):
                act.wait_ge(ang_done, n + 1)
                if not (isinstance(n, int) and n < 2):
                    act.wait_ge(h_done, n - 1)
                a = ang[j % 2]
                nc.scalar.activation(tab[j % 2][:, 1, :], a, ACT.Sin, scale=SIN_SCALE).then_inc(tab_done, 1)
                link(nc.scalar.activation(a, a, ACT.Abs))
                act.wait_ge(act_link.sem, act_link.value())
                nc.scalar.activation(tab[j % 2][:, 0, :], a, ACT.Sin, scale=-SIN_SCALE, bias=half_pi).then_inc(tab_done, 1)

            def gelus(i):
                act.wait_ge(y_read, i + 1)
                for c in (1, 0):
                    at = uz[:, bass.ds(place(act, i * 2 + c), 1), :].rearrange("p a t -> p (a t)")
                    nc.scalar.activation(at, at, ACT.Gelu_apprx_tanh).then_inc(gelu_done, 1)
                for k, c in enumerate((1, 0)):
                    act.wait_ge(gelu_done, i * 2 + (k + 1))
                    at = bass.ds(place(act, i * 2 + c), 1)
                    nc.scalar.activation(yh[:, at, :], uz[:, at, :], ACT.Copy).then_inc(s5_hi, 1)

            def qk_out(layer, i):
                r = r2_tok if layer else r_tok
                na = DA_PAIRS if layer else 0
                act.wait_ge(unit_used, i * (2 * UNITS) + (UNITS * ((CH_FOX if layer else CH_DA) + 1) + 1))
                if layer and isinstance(i, int):
                    act.wait_ge(r2_done, 1)
                if not (isinstance(i, int) and i == 0 and layer == 0):
                    act.wait_ge(qkt_ps, i * 2 + 2 * na)
                nc.scalar.activation(qk[:, 0, :], acc[0][0][:, :], ACT.Copy, scale=r[:, 0:1])
                nc.scalar.activation(qk[:, 1, :], acc[0][1][:, :], ACT.Copy, scale=r[:, 1:2]).then_inc(acc_free[0], 1)

            def qk_square(layer, i, t):
                na = DA_PAIRS if layer else 0
                first = isinstance(i, int) and i == 0
                act.wait_ge(acc_free[0], i + ((FREE_FOX if layer else FREE_DA) + 2))
                if t or layer or not first:
                    act.wait_ge(qk_ss, i * NT + (NT * na + t))
                if t == 0 and (layer == 0) != first:
                    act.wait_ge(p_ready, (2 * DA_PAIRS if layer else i * 2))
                nc.scalar.activation(s_sb[:, 1:4:2, 0:T], qk[:, t, :].rearrange("p (a b) -> p a b", a=2), ACT.Square)\
                    .then_inc(qk_sq, 1)

            def vz_out(layer, i):
                r = r2_tok if layer else r_tok
                na = DA_PAIRS if layer else 0
                act.wait_ge(unit_used, i * (2 * UNITS) + (UNITS * ((CH_FOX if layer else CH_DA) + 2) + 1))
                if not (isinstance(i, int) and i == 0 and layer == 0):
                    act.wait_ge(y_ready, i * 2 + (2 * na + 1))
                for t in range(NT):
                    nc.scalar.activation(vz[:, t, T:2 * T], acc[1][t][:, T:2 * T], ACT.Silu, scale=r[:, t:t + 1])
                for t in range(NT):
                    ins = nc.scalar.activation(vz[:, t, 0:T], acc[1][t][:, 0:T], ACT.Copy, scale=r[:, t:t + 1])
                ins.then_inc(acc_free[1], 1)

            def qkt_out(layer, a, h):
                act.wait_ge(qkt_ps, head_no(layer, a, h) + 1)
                for b in range(2):
                    ins = nc.scalar.activation(qkt[:, h, b, :], trb[:, b * T:(b + 1) * T], ACT.Copy,
                                               scale=g_qk[layer][:, b:b + 1])
                ins.then_inc(qkt_sb, 1)

            def exps(layer, a, k):
                s = k if layer == 0 else 2 * k
                act.wait_ge(sc_max, score_no(layer, a, k) + 1)
                for t, o, w in ((0, T, P), (1, 0, T)):
                    ins = nc.scalar.activation(s_sb[:, s, o:o + w], s_sb[:, s, o:o + w], ACT.Exp,
                                               bias=nmax[:, 2 * s + t:2 * s + t + 1],
                                               accum_out=lsum[:, 2 * s + t:2 * s + t + 1])
                ins.then_inc(p_exp if layer == 0 else p_ready, 1)

            def pt_out(layer, a, h):
                n = head_no(layer, a, h)
                act.wait_ge(pt_ps, n + 1)
                nc.scalar.activation(p_t[:, h, :], trb[:, 0:3 * P], ACT.Copy).then_inc(pt_sb, 1)

            def out_squares(a, h):
                act.wait_ge(pv_ps, head_no(0, a, h) + 1)
                for t in range(NT):
                    ins = nc.scalar.activation(y_o[:, h, t, :], scb[:, t * P:(t + 1) * P], ACT.Square, scale=HD ** -0.5,
                                               accum_out=sso[:, 2 * h + t:2 * h + t + 1])
                ins.then_inc(pv_ssq, 1)

            def yt_out(layer, a, h):
                n = head_no(layer, a, h)
                act.wait_ge(yt_ps, n + 1)
                kt = place(act, 2 * a + h + (8 if layer == 0 else 0))
                nc.scalar.activation(yh[:, bass.ds(kt, 1), :], trb[:, 0:T].rearrange("p (a t) -> p a t", a=1), ACT.Copy,
                                     scale=g_dao if layer == 0 else 1.0).then_inc(yt_hi, 1)

            def fox_cols(a, h):
                n = 2 * a + h
                if h == 0:
                    act.wait_ge(sc_max, score_no(1, a, 0))
                    act.wait_ge(c_done, 2)
                nc.scalar.activation(cq[:, 2 * h:2 * h + 2].rearrange("p (a b) -> p a b", b=1),
                                     c_sb[:, :, bass.ds(place(act, n), 1)], ACT.Copy).then_inc(fox_cq, 1)

            def attention(layer, a, s):
                for h in range(2):
                    if QKT_SLOT[h] == s:
                        qkt_out(layer, a, h)
                        if layer:
                            fox_cols(a, h)
                for k, at in enumerate(EXP_SLOT[layer]):
                    if at == s:
                        exps(layer, a, k)
                for h in range(2):
                    if PT_SLOT[h] == s:
                        pt_out(layer, a, h)
                    if PV_SLOT[h] == s and layer == 0:
                        out_squares(a, h)
                    if YT_SLOT[h] == s:
                        yt_out(layer, a, h)

            def step(layer, i, ch, first, side=None):
                for c in range(2):
                    for j in range(UNITS):
                        s = c * UNITS + j
                        split_hi(act, 2 * i + (ch + c), j + LEAD)
                        if layer == 0 and s == 0:
                            stage_mag(i)
                        if s == UNITS:
                            qk_out(layer, i)
                            qk_square(layer, i, 0)
                        if s == UNITS + 2:
                            qk_square(layer, i, 1)
                        if s == 1 and not first:
                            vz_out(layer, i - 1)
                        if not first and s != 5:
                            attention(layer, i - 1, s)
                        if layer == 0:
                            for g in range(GPI):
                                if X_SLOT[g] == s:
                                    phases(i * GPI + (g + 2), g)
                                if X_SLOT[g] + 1 == s:
                                    table(i * GPI + (g + 1), g + 1)
                            if s == 4:
                                stage_c(i)
                            if s == 5 and not first:
                                gelus(i - 1)
                        if not first and s == 5:
                            attention(layer, i - 1, s)
                        if side:
                            side(s)

            act.wait_ge(slopes, 2)
            table(0, 0)
            step(0, 0, CH_DA, True, gate)
            with act.Fori(1, DA_PAIRS) as i:
                act_link.enter(i - 1, GPI)
                step(0, i, CH_DA, False)
            act_link.leave(DA_PAIRS - 1)

            vz_out(0, DA_PAIRS - 1)
            for j in range(UNITS):
                split_hi(act, CH_GLU, j + LEAD)
                if j == 3:
                    gelus(DA_PAIRS - 1)
                for s in WITH_GLU[j]:
                    attention(0, DA_PAIRS - 1, s)

            def glu_up(n):
                act.wait_ge(glu_y, n + 1)
                nc.scalar.activation(yh[:, n, :], uz[:, n, :], ACT.Copy).then_inc(glu_hi, 1)

            act.wait_ge(unit_used, UNITS * (CH_GLU + 1) + 1)
            for n in range(CT):
                nc.scalar.activation(glu_s[:, n, :], acc[n // 4][n // 2 % 2][:, n % 2 * T:(n % 2 + 1) * T],
                                     ACT.Sigmoid, bias=bg_col[:, n:n + 1]).then_inc(glu_sig, 1)

            def x1_up(n):
                for e in range(4):
                    kt = 4 * n + e
                    if e % 2 == 0:
                        act.wait_ge(x1_ps, 2 * n + e // 2 + 1)
                    nc.scalar.activation(xh[:, kt, :], bank[4 + 2 * (n % 2) + e // 2][:, e % 2 * T:(e % 2 + 1) * T],
                                         ACT.Copy, scale=o_col[:, kt:kt + 1]).then_inc(x1_hi, 1)

            def x1_keep(n):
                for t in range(NT):
                    act.wait_ge(x1_done, 2 * n + t + 1)
                    if n or t:
                        act.wait_ge(x1_ssq, 2 * n + t)
                    nc.scalar.activation(qk[:, 1, :], x1_st[n % 2][:, t, :], ACT.Square,
                                         accum_out=ss1[:, t, n:n + 1]).then_inc(x1_ssq, 1)

            for n in range(4):
                for j in range(UNITS):
                    split_hi(act, CH_OUT0 + n, j + LEAD)
                    if n == 0:
                        for s in AFTER_GLU.get(j, ()):
                            attention(0, DA_PAIRS - 1, s)
                        if j < 4:
                            glu_up(2 * j)
                            glu_up(2 * j + 1)
                    if n and j == 2:
                        x1_up(n - 1)
                x1_keep(n)

            act.dma_start(wf, d["o_w_in"][0].rearrange("(k p) n -> p k n", p=P)[:, :, 4 * D:4 * D + 16]).then_inc(wf_in, 16)

            def side(s):
                if s == 0:
                    x1_up(3)
                if s == 2:
                    act.wait_ge(wf_in, 16)
                    nc.scalar.activation(wf2[:, :, 0:16], wf, ACT.Copy).then_inc(wf_hi, 1)
                if s == 8:
                    act.wait_ge(f_ps, 1)
                    nc.scalar.activation(f_sb, yb[0:32, 0:T], ACT.Copy).then_inc(f_sbuf, 1)
                if s == 10:
                    act.wait_ge(f_z, 1)
                    nc.scalar.activation(lsa, ls, ACT.Abs).then_inc(f_abs, 1)
                    act.wait_ge(f_abs, 1)
                    nc.scalar.activation(lsa, lsa, ACT.Exp, scale=-1.0).then_inc(f_abs, 1)
                if s == 11:
                    act.wait_ge(f_exp1, 1)
                    nc.scalar.activation(lsa, lsa, ACT.Ln).then_inc(f_ln, 1)
                if s == 13:
                    act.wait_ge(c_ps, 1)
                    nc.scalar.activation(c_sb, yb[:, 64:96].rearrange("p (a b) -> p a b", a=2), ACT.Copy).then_inc(c_done, 1)
                    nc.scalar.mul(nct, yb[0:16, 128:384], -1.0).then_inc(c_done, 1)

            step(1, 0, CH_FOX, True, side)
            with act.Fori(1, FOX_PAIRS) as i:
                step(1, i, CH_FOX, False)

            for n in range(4):
                for j in range(UNITS):
                    if UNITS * (CH_OUT1 + n) + j + LEAD < UNITS * CH_END:
                        split_hi(act, CH_OUT1 + n, j + LEAD)
                    if n == 0 and j == 0:
                        vz_out(1, FOX_PAIRS - 1)
                    if n == 0:
                        for s in WITH_OUT1.get(j, ()):
                            attention(1, FOX_PAIRS - 1, s)
                act.wait_ge(x1_done, 8 + 2 * (n + 1))
                act.dma_start(out_dram[0, :, n * CW:(n + 1) * CW].rearrange("(t p) n -> p t n", p=P),
                              res[:, :, n * CW:(n + 1) * CW]).then_inc(out_done, 16)

        @block.vector
        def _(dve):
            def link(ins):
                dve_link.inc(ins)
                dve.wait_ge(dve_link.sem, dve_link.value())

            v = nc.vector

            v.memset(half_pi, 0.5 * math.pi)
            v.memset(magic, MAGIC)
            link(v.memset(eps, EPS))
            for k, first in enumerate((yt_lo, y_ready, acc_free[0], acc_free[1], unit_used)):
                v.memset(junk1[:, k:k + 1], 0.0).then_inc(first, 1)
            v.memset(expo, -0.5).then_inc(slopes, 1)
            def tiles_low(b):
                dve.wait_ge(tile_hi, 2 * b + 2)
                for e in range(2):
                    kt = 2 * b + e
                    v.scalar_tensor_tensor(out=xl[:, kt, :], in0=bank[4 + b % 2][:, e * T:(e + 1) * T],
                                           scalar=e_col[:, kt:kt + 1], in1=xh[:, kt, :].bitcast(F32),
                                           op0=ALU.mult, op1=ALU.subtract).then_inc(tile_lo, 1)

            for j in range(LEAD):
                tiles_low(j)
                split_lo(dve, 0, j)

            def diagonal():
                dve.wait_ge(r_done, 1)
                dve.wait_ge(pool_const, 1)
                for t in range(NT):
                    ins = v.tensor_scalar(rbc[:, t * P:(t + 1) * P], ident, r_tok[:, t:t + 1], None, ALU.mult)
                ins.then_inc(diag_done, 1)

            def rbc_out():
                dve.wait_ge(rbc_ps, 1)
                v.tensor_copy(rbc, yb[:, 0:T]).then_inc(rbc_done, 1)

            lr, li, ldt, dt, lrdt, th, n, a, b, _, turn, sn, cs, ab, den, t1, t2, kr, ki, nr = prm

            def angles_ready():
                dve.wait_ge(prm_ld, 2)
                v.tensor_copy(lr, xb[:, 64:96])
                v.tensor_copy(li, xb[:, 96:128])
                v.tensor_copy(ldt, xb[:, 128:160]).then_inc(prm_ang, 1)

            def turns():
                dve.wait_ge(prm_ang, 1)
                dve.wait_ge(prm_exp, 1)
                link(v.memset(phc[:, :, GP:GP + 2], 0.0))
                v.tensor_tensor(lrdt, lr, dt, ALU.mult).then_inc(prm_ang, 1)
                link(v.tensor_tensor(th, li, dt, ALU.mult))
                link(v.tensor_scalar(n, th, 1.0 / TWO_PI, MAGIC, ALU.mult, ALU.add))
                link(v.tensor_scalar(n, n, -MAGIC, None, ALU.add))
                link(v.scalar_tensor_tensor(out=a, in0=n, scalar=-PI_A, in1=th, op0=ALU.mult, op1=ALU.add))
                link(v.scalar_tensor_tensor(out=a, in0=n, scalar=-PI_B, in1=a, op0=ALU.mult, op1=ALU.add))
                link(v.tensor_scalar(phr[:, :], a, 1.0 / TWO_PI, None, ALU.mult))
                link(v.tensor_copy(ph_hi, phr[:, :].bitcast(F32)))
                link(v.scalar_tensor_tensor(out=b, in0=ph_hi, scalar=-PI_A, in1=a, op0=ALU.mult, op1=ALU.add))
                link(v.scalar_tensor_tensor(out=b, in0=ph_hi, scalar=-PI_B, in1=b, op0=ALU.mult, op1=ALU.add))
                link(v.tensor_tensor(n, n, ph_hi, ALU.add))
                link(v.scalar_tensor_tensor(out=b, in0=n, scalar=-PI_C, in1=b, op0=ALU.mult, op1=ALU.add))
                link(v.tensor_scalar(ph_lo, b, 1.0 / TWO_PI, None, ALU.mult))
                link(v.tensor_tensor(turn, ph_hi, ph_lo, ALU.add))
                v.tensor_copy(ph_all, turn).then_inc(prm_ang, 1)

            def b_factors():
                link(v.tensor_tensor(t1, lr, lr, ALU.mult))
                link(v.tensor_tensor(t2, li, li, ALU.mult))
                link(v.tensor_tensor(den, t1, t2, ALU.add))
                link(v.reciprocal(den, den))
                dve.wait_ge(prm_exp, 2)
                dve.wait_ge(prm_trig, 3)
                mag = mag_all
                link(v.tensor_tensor(nr, mag, cs, ALU.mult))
                link(v.tensor_scalar(nr, nr, -1.0, None, ALU.add))
                link(v.tensor_tensor(sn, mag, sn, ALU.mult))
                link(v.tensor_tensor(t1, nr, lr, ALU.mult))
                link(v.tensor_tensor(t2, sn, li, ALU.mult))
                link(v.tensor_tensor(kr, t1, t2, ALU.add))
                link(v.tensor_tensor(kr, kr, den, ALU.mult))
                link(v.tensor_tensor(t1, sn, lr, ALU.mult))
                link(v.tensor_tensor(t2, nr, li, ALU.mult))
                link(v.tensor_tensor(ki, t1, t2, ALU.subtract))
                link(v.tensor_tensor(ki, ki, den, ALU.mult))
                v.memset(bd, 0.0).then_inc(prm_done, 1)

            def b_blocks():
                dve.wait_ge(s5_in, 16 * 4)

                def wide(x):
                    return x.rearrange("p (a b) -> p a b", b=1).to_broadcast([P, GP, 16])

                br, bi = b_n[:, 0, :, :], b_n[:, 1, :, :]
                v.tensor_tensor(bt[0], br, wide(kr), ALU.mult)
                v.tensor_tensor(bt[1], bi, wide(ki), ALU.mult)
                v.tensor_tensor(bt[2], bi, wide(kr), ALU.mult)
                link(v.tensor_tensor(bt[3], br, wide(ki), ALU.mult))
                dve.wait_ge(prm_done, 1)
                for g in range(2):
                    rows_ = slice(64 * g, 64 * g + 64)
                    for r, op in ((0, ALU.subtract), (1, ALU.add)):
                        ins = v.tensor_tensor(bd[rows_, r, :, 16 * g:16 * g + 16], bt[2 * r][rows_], bt[2 * r + 1][rows_], op)
                ins.then_inc(bd_done, 1)

            def c_blocks():
                dve.wait_ge(pool_const, 2)
                link(v.tensor_scalar(pint.bitcast(I32), pint.bitcast(I32), 16, None, ALU.bitwise_and))
                link(v.tensor_copy(par[:, 1:2], pint.bitcast(I32)))
                link(v.tensor_scalar(par[:, 1:2], par[:, 1:2], 1.0 / 16, None, ALU.mult))
                link(v.tensor_scalar(par[:, 0:1], par[:, 1:2], -1.0, 1.0, ALU.mult, ALU.add))
                for r, dst, sign in ((0, cb, 1.0), (1, cb2, -1.0)):
                    for g in range(2):
                        ins = v.tensor_scalar(dst[:, :, 64 * g:64 * g + 64], c_n[:, r, :, :], par[:, g:g + 1],
                                              sign, ALU.mult, ALU.mult)
                    ins.then_inc(cb_done, 1)

            def gains():
                dve.wait_ge(bc_in, 16 * 4)
                dve.wait_ge(prm_ld, 2)
                v.tensor_scalar(g_qk[0][:, 0:1], g_qk[0][:, 0:1], 64 ** -0.5, None, ALU.mult)
                v.tensor_scalar(g_qk[1][:, 0:1], g_qk[1][:, 0:1], float(HD) ** -0.5, None, ALU.mult)
                v.tensor_scalar(g_dao, g_dao, 1.0 - LAMBDA_INIT, None, ALU.mult).then_inc(slopes, 1)
                link(v.tensor_tensor(lamv[:, 0:4:2, :], lamv[:, 0:4:2, :], lamv[:, 1:4:2, :], ALU.mult))
                v.tensor_reduce(lt[:, 0:2], lamv[:, 0:4:2, :], AX.X, ALU.add).then_inc(lambda_done, 1)
                for h in range(2):
                    ins = v.memset(slope[:, h:h + 1], -(2.0 ** -(h + 1)))
                link(ins)

            def lam_end():
                dve.wait_ge(prm_exp, 3)
                link(v.tensor_tensor(nlam, lt[:, 2:3], lt[:, 3:4], ALU.subtract))
                link(v.tensor_scalar(nlam, nlam, LAMBDA_INIT, None, ALU.add))

            def angles(n, j):
                w = ang[j % 2]
                dve.wait_ge(phase_up, n + 1)
                link(v.scalar_tensor_tensor(out=w, in0=w, scalar=-MAGIC, in1=ph[j % 2], op0=ALU.add, op1=ALU.subtract))
                link(v.scalar_tensor_tensor(out=w, in0=steps, scalar=phc[:, 1, bass.ds(n, 1)], in1=w,
                                            op0=ALU.mult, op1=ALU.subtract))
                v.tensor_scalar(w, w, 0.5, -0.5, ALU.min, ALU.max).then_inc(ang_done, 1)

            def log_steps():
                dve.wait_ge(par_in, 16 * 12)
                v.tensor_copy(ldt_r, ldt_in.rearrange("p (a b) -> p a b", b=1).to_broadcast([GP, 2, 64])).then_inc(prm_rows, 1)

            aside = {(0, 6): diagonal, (1, 0): log_steps, (1, 2): angles_ready, (1, 3): gains, (1, 4): turns,
                     (1, 5): b_factors, (1, 6): b_blocks, (2, 1): c_blocks, (2, 2): lam_end}
            for c in range(4):
                for j in range(UNITS):
                    if c == 0 and j + LEAD < UNITS:
                        tiles_low(j + LEAD)
                    split_lo(dve, c, j + LEAD)
                    if (c, j) in aside:
                        aside[c, j]()
                    if (c, j) in ((3, 4), (3, 6)):
                        angles((j - 4) // 2, (j - 4) // 2)
                if c == 0:
                    rbc_out()
                    dve.wait_ge(rbc_done, 1)
                dve.wait_ge(unit_used, UNITS * (c + 1) + 1)
                for half in range(2):
                    o = acc[c % 2][half][:, :].rearrange("p (a t) -> p a t", a=2)
                    ins = v.tensor_tensor(uz[:, 4 * c + 2 * half:4 * c + 2 * half + 2, :], o,
                                          rbc.rearrange("p (a t) -> p a t", a=1).to_broadcast([P, 2, T]), ALU.mult)
                ins.then_inc(acc_free[c % 2], 1)

            def stage(i):
                if isinstance(i, int) and i == 0:
                    dve.wait_ge(mat_sb, 16)
                else:
                    dve.wait_ge(x_ps, i * GPI)
                v.tensor_copy(lb_st, lb[:, bass.ds(i * 2, 2), :, :])
                v.tensor_copy(u_st, uz[:, bass.ds(i * 2, 2), :]).then_inc(staged, 1)

            def rotate_in(i, j):
                dve.wait_ge(x_ps, i * GPI + (j + 1))
                dve.wait_ge(tab_done, i * (2 * GPI) + 2 * (j + 1))
                if j >= 4 or not (isinstance(i, int) and i == 0):
                    dve.wait_ge(y_ps, i * GPI + (j - 3))
                if j >= 2 or not (isinstance(i, int) and i == 0):
                    dve.wait_ge(h_done, i * GPI + (j - 1))
                m1, (m2, _) = hs[j % 4], rot[j % 2]
                x = xb[:, :].rearrange("p (r t) -> p r t", r=2)
                c, s = (tab[j % 2][:, k:k + 1, :].to_broadcast([P, 2, T]) for k in range(2))
                v.tensor_tensor(m1, x, c, ALU.mult)
                v.tensor_tensor(m2, x, s, ALU.mult).then_inc(x_read, 1)

            def scan(i, j):
                dve.wait_ge(g_done, i * GPI + (j + 1))
                if j == 0:
                    dve.wait_ge(staged_mag, i + 1)
                m1, g = hs[j % 4], rot[j % 2][1]
                mag = mag_st[:, j:j + 1].to_broadcast([P, T])
                for r in range(2):
                    ins = v.tensor_tensor_scan(m1[:, r, :], mag, g[:, r, :], 0.0, ALU.mult, ALU.add)
                ins.then_inc(scan_done, 1)

            def s5_out(i):
                dve.wait_ge(y_ps, i * GPI + GPI)
                for c in range(2):
                    u = uz[:, bass.ds(i * 2 + c, 1), :].rearrange("p a t -> p (a t)")
                    ins = v.scalar_tensor_tensor(out=u, in0=u,
                                                 scalar=d_col[:, bass.ds(i * 2 + c, 1)],
                                                 in1=yb[:, c * T:(c + 1) * T], op0=ALU.mult, op1=ALU.add)
                ins.then_inc(y_read, 1)

            def s5_low(i):
                for k, c in enumerate((1, 0)):
                    dve.wait_ge(s5_hi, i * 2 + (k + 1))
                    at = bass.ds(i * 2 + c, 1)
                    v.tensor_tensor(yl[:, at, :], uz[:, at, :], yh[:, at, :].bitcast(F32), ALU.subtract).then_inc(s5_lo, 1)

            def qk_squares(layer, i, t):
                na = DA_PAIRS if layer else 0
                seg = 64 if layer == 0 else HD
                n = CW // seg
                dve.wait_ge(qk_sq, i * NT + (NT * na + t + 1))
                link(v.tensor_reduce(ssn[:, t * n:(t + 1) * n].rearrange("p (a s) -> p a s", a=2),
                                     s_sb[:, 1:4:2, 0:T].rearrange("p a (s e) -> p a s e", e=seg), AX.X, ALU.add))
                at = ssn[:, t * n:(t + 1) * n]
                v.tensor_scalar(at, at, 1.0 / seg, EPS, ALU.mult, ALU.add).then_inc(qk_ss, 1)

            def score_in(layer, a, k):
                h = k // 2 if layer == 0 else k
                s = k if layer == 0 else 2 * k
                dve.wait_ge(sc_ps, score_no(layer, a, k) + 1)
                if layer == 0:
                    link(v.scalar_tensor_tensor(out=s_sb[:, s, :], in0=dist, scalar=slope[:, h:h + 1],
                                                in1=scb[:, 0:3 * P], op0=ALU.mult, op1=ALU.add))
                else:
                    dve.wait_ge(fox_cq, 2 * a + (k + 1))
                    v.scalar_tensor_tensor(out=s_sb[:, s, 0:T], in0=mask[:, 0:T], scalar=cq[:, 2 * h + 1:2 * h + 2],
                                           in1=scb[:, 0:T], op0=ALU.add, op1=ALU.add)
                    link(v.scalar_tensor_tensor(out=s_sb[:, s, T:T + P], in0=mask[:, T:T + P], scalar=cq[:, 2 * h:2 * h + 1],
                                                in1=scb[:, T:T + P], op0=ALU.add, op1=ALU.add))
                v.tensor_reduce(nmax[:, 2 * s:2 * s + 1], s_sb[:, s, T:T + P], AX.X, ALU.max, negate=True)
                v.tensor_reduce(nmax[:, 2 * s + 1:2 * s + 2], s_sb[:, s, 0:T], AX.X, ALU.max, negate=True).then_inc(sc_max, 1)

            def combine(a, h):
                dve.wait_ge(p_exp, score_no(0, a, 2 * h + 1) + 1)
                k = 4 * h
                link(v.reciprocal(rec[:, k:k + 4], lsum[:, k:k + 4]))
                link(v.tensor_scalar(rec[:, k + 2:k + 4], rec[:, k + 2:k + 4], nlam, None, ALU.mult))
                for t, o, w in ((0, T, P), (1, 0, T)):
                    p1, p2 = s_sb[:, 2 * h, o:o + w], s_sb[:, 2 * h + 1, o:o + w]
                    ins = v.tensor_scalar(p2, p2, rec[:, k + 2 + t:k + 3 + t], None, ALU.mult)
                link(ins)
                for t, o, w in ((0, T, P), (1, 0, T)):
                    p1, p2 = s_sb[:, 2 * h, o:o + w], s_sb[:, 2 * h + 1, o:o + w]
                    ins = v.scalar_tensor_tensor(out=p1, in0=p1, scalar=rec[:, k + t:k + t + 1], in1=p2,
                                                 op0=ALU.mult, op1=ALU.subtract)
                ins.then_inc(p_ready, 1)

            def head_out(layer, a, h):
                n = head_no(layer, a, h)
                if layer == 0:
                    dve.wait_ge(pv_rn, n + 1)
                    scale = rno[:, 2 * h:2 * h + 2]
                else:
                    dve.wait_ge(pv_ps, n + 1)
                    link(v.reciprocal(rec[:, 4 * h:4 * h + 2], lsum[:, 4 * h:4 * h + 2]))
                    scale = rec[:, 4 * h:4 * h + 2]
                for t in range(NT):
                    ins = v.scalar_tensor_tensor(out=y_o[:, h, t, :], in0=scb[:, t * P:(t + 1) * P],
                                                 scalar=scale[:, t:t + 1], in1=vz[:, t, T + h * HD:T + (h + 1) * HD],
                                                 op0=ALU.mult, op1=ALU.mult)
                ins.then_inc(y_ready, 1)

            def yt_low(layer, a, h):
                n = head_no(layer, a, h)
                dve.wait_ge(yt_hi, n + 1)
                kt = bass.ds(2 * a + h + (8 if layer == 0 else 0), 1)
                v.scalar_tensor_tensor(out=yl[:, kt, :], in0=trb[:, 0:T].rearrange("p (a t) -> p a t", a=1),
                                       scalar=g_dao if layer == 0 else 1.0, in1=yh[:, kt, :].bitcast(F32),
                                       op0=ALU.mult, op1=ALU.subtract).then_inc(yt_lo, 1)

            def fox_keys(a, h):
                if h == 0:
                    dve.wait_ge(sc_ps, score_no(1, a, 0))
                    dve.wait_ge(c_split, 1)
                v.tensor_scalar(nck[:, h, :], nks, sel[:, bass.ds(2 * a + h, 1)], None, ALU.mult).then_inc(fox_b, 1)

            def attention(layer, a, s):
                for h in range(2):
                    if QKT_SLOT[h] == s and layer:
                        fox_keys(a, h)
                for k, at in enumerate(SC_SLOT[layer]):
                    if at == s:
                        score_in(layer, a, k)
                if layer == 0 and s in (6, 7):
                    combine(a, s - 6)
                for h in range(2):
                    if PV_SLOT[h] + (2 if layer == 0 else 0) == s:
                        head_out(layer, a, h)
                    if YT_SLOT[h] == s:
                        yt_low(layer, a, h)
                if layer == 0 and s == 7:
                    link(v.tensor_scalar(slope, slope, 0.25, None, ALU.mult))

            def step(layer, i, ch, first, side=None):
                for c in range(2):
                    for j in range(UNITS):
                        s = c * UNITS + j
                        split_lo(dve, 2 * i + (ch + c), j + LEAD)
                        if layer == 0 and s == 2 * UNITS - 1:
                            stage(i + 1)
                        if not first and s == 13:
                            attention(layer, i - 1, s)
                        for g in range(GPI):
                            if layer == 0 and X_SLOT[g] + 1 == s:
                                scan(i, g)
                                angles(i * GPI + (g + 2), g)
                        if not first and s != 13:
                            attention(layer, i - 1, s)
                        if layer == 0:
                            for g in range(GPI):
                                if X_SLOT[g] == s:
                                    rotate_in(i, g)
                            if s == 3 and not first:
                                s5_out(i - 1)
                            if s == 6 and not first:
                                s5_low(i - 1)
                        if side:
                            side(s)
                        if s in (9, 11):
                            qk_squares(layer, i, (s - 9) // 2)

            stage(0)
            step(0, 0, CH_DA, True)
            with dve.Fori(1, DA_PAIRS) as i:
                dve_link.enter(i - 1, DA_LINKS)
                step(0, i, CH_DA, False)
            dve_link.leave(DA_PAIRS - 1)

            for j in range(UNITS):
                split_lo(dve, CH_GLU, j + LEAD)
                if j == 2:
                    s5_out(DA_PAIRS - 1)
                if j == 4:
                    s5_low(DA_PAIRS - 1)
                for s in WITH_GLU[j]:
                    attention(0, DA_PAIRS - 1, s)

            def glu_mul(n):
                if n == 0:
                    dve.wait_ge(silu_done, 1)
                dve.wait_ge(glu_sig, n + 1)
                v.tensor_tensor(glu_s[:, n, :], glu_s[:, n, :], uz[:, CT + n, :], ALU.mult).then_inc(glu_y0, 1)
                dve.wait_ge(glu_y0, n + 1)
                v.tensor_tensor(uz[:, n, :], uz[:, n, :], glu_s[:, n, :], ALU.mult).then_inc(glu_y, 1)

            def glu_low(n):
                dve.wait_ge(glu_hi, n + 1)
                v.tensor_tensor(yl[:, n, :], uz[:, n, :], yh[:, n, :].bitcast(F32), ALU.subtract).then_inc(glu_lo, 1)

            def x1_low(n):
                for e in range(4):
                    kt = 4 * n + e
                    dve.wait_ge(x1_hi, 2 * (kt // 2) + 2)
                    v.scalar_tensor_tensor(out=xl[:, kt, :],
                                           in0=bank[4 + 2 * (n % 2) + e // 2][:, e % 2 * T:(e % 2 + 1) * T],
                                           scalar=o_col[:, kt:kt + 1], in1=xh[:, kt, :].bitcast(F32),
                                           op0=ALU.mult, op1=ALU.subtract).then_inc(x1_lo, 1)

            for n in range(4):
                for j in range(UNITS):
                    split_lo(dve, CH_OUT0 + n, j + LEAD)
                    if n == 0:
                        if j < 4:
                            glu_mul(2 * j)
                            glu_mul(2 * j + 1)
                        for s in AFTER_GLU.get(j, ()):
                            attention(0, DA_PAIRS - 1, s)
                        if j < 4:
                            glu_low(2 * j)
                            glu_low(2 * j + 1)
                    if n and j == 2:
                        x1_low(n - 1)
                dve.wait_ge(unit_used, UNITS * (CH_OUT0 + n + 1) + 1)
                if n == 0:
                    dve.wait_ge(res_in, 16)
                if n >= 2:
                    dve.wait_ge(x1_ps, 2 * (n - 1))
                    dve.wait_ge(x1_kept, n - 1)
                    dve.wait_ge(x1_ssq, 2 * (n - 1))
                for t in range(NT):
                    v.tensor_tensor(x1_st[n % 2][:, t, :], res[:, t, n * CW:(n + 1) * CW], acc[n % 2][t][:, :], ALU.add)\
                        .then_inc(x1_done, 1)
            dve.wait_ge(x1_ssq, 8)
            v.tensor_reduce(ssr, ss1, AX.X, ALU.add).then_inc(r2_sum, 1)

            def side(s):
                if s == 0:
                    x1_low(3)
                if s == 2:
                    dve.wait_ge(wf_hi, 1)
                    v.tensor_tensor(wf2[:, :, 16:32], wf, wf2[:, :, 0:16].bitcast(F32), ALU.subtract).then_inc(wf_lo, 1)
                if s == 9:
                    dve.wait_ge(f_tps, 1)
                    dve.wait_ge(r2_done, 1)
                    for part in range(2):
                        for t in range(NT):
                            at = 400 + 32 * t + 16 * part
                            ins = v.scalar_tensor_tensor(out=ls[:, t, :], in0=yb[:, at:at + 16], scalar=r2_tok[:, t:t + 1],
                                                         in1=ls[:, t, :] if part else bf, op0=ALU.mult, op1=ALU.add)
                        if part == 0:
                            link(ins)
                    ins.then_inc(f_z, 1)
                if s == 10:
                    dve.wait_ge(f_abs, 2)
                    v.tensor_scalar(lsa, lsa, 1.0, None, ALU.add).then_inc(f_exp1, 1)
                if s == 14:
                    link(v.memset(nks, 0.0))
                    v.tensor_copy(ones_r[:, :], ones[0:48, :])
                    v.tensor_tensor(sel, ident[0:48, 0:16], ident[0:48, 32:48], ALU.add)
                    dve.wait_ge(c_done, 2)
                    link(v.tensor_copy(nck[0:16, 0, :], nct))
                    v.tensor_copy(nks[0:16, :], nck[0:16, 0, :].bitcast(F32))
                    v.tensor_tensor(nks[32:48, :], nct, nck[0:16, 0, :].bitcast(F32), ALU.subtract).then_inc(c_split, 1)
                if s == 12:
                    dve.wait_ge(f_ln, 1)
                    link(v.tensor_scalar(ls, ls, 0.0, None, ALU.min))
                    v.tensor_tensor(ls, ls, lsa, ALU.subtract).then_inc(f_ls, 1)

            step(1, 0, CH_FOX, True, side)
            with dve.Fori(1, FOX_PAIRS) as i:
                dve_link.enter(i - 1, FOX_LINKS)
                step(1, i, CH_FOX, False)
            dve_link.leave(FOX_PAIRS - 1)

            for n in range(4):
                for j in range(UNITS):
                    if UNITS * (CH_OUT1 + n) + j + LEAD < UNITS * CH_END:
                        split_lo(dve, CH_OUT1 + n, j + LEAD)
                    if n == 0:
                        for s in WITH_OUT1.get(j, ()):
                            attention(1, FOX_PAIRS - 1, s)
                dve.wait_ge(unit_used, UNITS * (CH_OUT1 + n + 1) + 1)
                if n == 0:
                    dve.wait_ge(x1_kept, 4)
                for t in range(NT):
                    at = res[:, t, n * CW:(n + 1) * CW]
                    v.tensor_tensor(at, at, acc[n % 2][t][:, :], ALU.add).then_inc(x1_done, 1)

        @block.gpsimd
        def _(pool):
            g = nc.gpsimd

            def link(ins):
                pool_link.inc(ins)
                pool.wait_ge(pool_link.sem, pool_link.value())

            link(g.memset(ident, 0.0))
            link(g.affine_select(out=ident, in_=ident, compare_op=ALU.not_equal, fill=1.0, base=0,
                                 pattern=[[-1, P]], channel_multiplier=1))
            g.memset(ones, 1.0).then_inc(pool_const, 1)
            link(g.iota(pint.bitcast(I32), pattern=[[0, 1]], base=0, channel_multiplier=1))
            link(g.iota(iot[:, 0:T].bitcast(I32), pattern=[[1, T]], base=0, channel_multiplier=0))
            link(g.tensor_copy(steps, iot[:, 0:T].bitcast(I32)))
            link(g.iota(iot[:, T:2 * T].bitcast(I32), pattern=[[-1, T]], base=P, channel_multiplier=1))
            link(g.iota(iot[:, 2 * T:2 * T + P].bitcast(I32), pattern=[[-1, P]], base=0, channel_multiplier=1))
            link(g.tensor_copy(dist, iot[:, T:2 * T + P].bitcast(I32)))
            link(g.memset(mask, 0.0))
            link(g.memset(upto, 1.0))
            for o, w, base in ((0, T, P), (T, P, 0)):
                for m, fill in ((dist, FAR), (mask, -FAR)):
                    link(g.affine_select(out=m[:, o:o + w], in_=m[:, o:o + w], compare_op=ALU.is_ge, fill=fill,
                                         base=base, pattern=[[-1, w]], channel_multiplier=1))
            g.affine_select(out=upto, in_=upto, compare_op=ALU.is_ge, fill=0.0,
                            base=0, pattern=[[1, P]], channel_multiplier=-1).then_inc(pool_const, 1)
            pool.wait_ge(ssq_done, 2)
            pool.wait_ge(slopes, 1)
            link(g.tensor_scalar(ssq, ssq, 1.0 / D, EPS, ALU.mult, ALU.add))
            g.tensor_tensor(r_tok, ssq, expo[:, 0:2], ALU.pow).then_inc(r_done, 1)

            def rotate_in(i, j):
                pool.wait_ge(x_read, i * GPI + (j + 1))
                m1, (m2, gg) = hs[j % 4], rot[j % 2]
                g.tensor_tensor(gg[:, 0, :], m1[:, 0, :], m2[:, 1, :], ALU.add)
                g.tensor_tensor(gg[:, 1, :], m1[:, 1, :], m2[:, 0, :], ALU.subtract).then_inc(g_done, 1)

            def rotate_out(i, j):
                pool.wait_ge(scan_done, i * GPI + (j + 1))
                m1, (m2, gg) = hs[j % 4], rot[j % 2]
                c, s = (tab[j % 2][:, k:k + 1, :].to_broadcast([P, 2, T]) for k in range(2))
                link(g.tensor_tensor(m2, m1, s, ALU.mult))
                link(g.tensor_tensor(gg, m1, c, ALU.mult))
                g.tensor_tensor(m1[:, 0, :], gg[:, 0, :], m2[:, 1, :], ALU.subtract)
                g.tensor_tensor(m1[:, 1, :], gg[:, 1, :], m2[:, 0, :], ALU.add).then_inc(h_done, 1)

            def qk_norm(layer, i, t):
                na = DA_PAIRS if layer else 0
                seg = 64 if layer == 0 else HD
                n = CW // seg
                pool.wait_ge(qk_ss, i * NT + (NT * na + t + 1))
                at = slice(t * n, (t + 1) * n)
                link(g.tensor_tensor(rnn[:, at], ssn[:, at], expo[:, at], ALU.pow))
                x = qk[:, t, :].rearrange("p (s e) -> p s e", e=seg)
                rn = rnn[:, t * n:(t + 1) * n].rearrange("p (s e) -> p s e", e=1)
                g.tensor_tensor(x, x, rn.to_broadcast([P, n, seg]), ALU.mult).then_inc(qk_ready, 1)

            def out_norm(a, h):
                pool.wait_ge(pv_ssq, head_no(0, a, h) + 1)
                link(g.tensor_tensor(sso[:, 2 * h:2 * h + 2], sso[:, 2 * h:2 * h + 2], eps, ALU.add))
                g.tensor_tensor(rno[:, 2 * h:2 * h + 2], sso[:, 2 * h:2 * h + 2], expo[:, 0:2], ALU.pow).then_inc(pv_rn, 1)

            def step(layer, i, first):
                for s in range(2 * UNITS):
                    if layer == 0:
                        for k in range(GPI):
                            if X_SLOT[k] == s:
                                rotate_in(i, k)
                            if X_SLOT[k] + 1 == s:
                                rotate_out(i, k)
                    if layer == 0 and not first:
                        for h in range(2):
                            if PV_SLOT[h] == s:
                                out_norm(i - 1, h)
                    if s in (12, 14):
                        qk_norm(layer, i, (s - 12) // 2)

            step(0, 0, True)
            with pool.Fori(1, DA_PAIRS) as i:
                pool_link.enter(i - 1, DA_POOL_LINKS)
                step(0, i, False)
            pool_link.leave(DA_PAIRS - 1)
            for h in range(2):
                out_norm(DA_PAIRS - 1, h)
            for n in range(4):
                pool.wait_ge(x1_done, 2 * (n + 1))
                for t in range(NT):
                    ins = g.tensor_copy(res[:, t, n * CW:(n + 1) * CW], x1_st[n % 2][:, t, :])
                ins.then_inc(x1_kept, 1)
            pool.wait_ge(r2_sum, 1)
            link(g.tensor_scalar(ssr, ssr, 1.0 / D, EPS, ALU.mult, ALU.add))
            g.tensor_tensor(r2_tok, ssr, expo[:, 0:2], ALU.pow).then_inc(r2_done, 1)
            step(1, 0, True)
            with pool.Fori(1, FOX_PAIRS) as i:
                pool_link.enter(i - 1, FOX_POOL_LINKS)
                step(1, i, False)
            pool_link.leave(FOX_PAIRS - 1)


_INS = ["x", "e_norm", "e_w_in", "e_w_out", "s5_lambda_re", "s5_lambda_im", "s5_log_dt", "s5_b_re", "s5_b_im",
        "s5_c_re", "s5_c_im", "s5_d", "s5_w_glu", "s5_b_glu", "da_q_norm", "da_k_norm", "da_lambda_q1",
        "da_lambda_k1", "da_lambda_q2", "da_lambda_k2", "da_out_norm", "o_norm", "o_w_in", "o_b_f", "o_w_out",
        "fox_q_norm", "fox_k_norm"]


def kernel(**inputs):
    import numpy as _np
    import concourse.bacc as _bacc
    from concourse import mybir as _mybir
    from concourse.bass_utils import run_bass_kernel_spmd as _run

    nc = _bacc.Bacc("TRN2", target_bir_lowering=False, num_devices=1)
    arrays, args = {}, {}
    for name in _INS:
        a = _np.ascontiguousarray(inputs[name])
        arrays[f"in_{name}"] = a
        args[name] = nc.dram_tensor(f"in_{name}", a.shape, _mybir.dt.from_np(a.dtype), kind="ExternalInput").ap()
    out = nc.dram_tensor("out_dram", (1, T, D), F32, kind="ExternalOutput").ap()
    build(nc, args, out)
    r = _run(nc, [arrays], core_ids=[0])
    return r.results[0]["out_dram"]
```
